# Optimizing a Trainium2 kernel written in Bass

```python
import jax, jax.numpy as jnp
from jax import lax
import numpy as np
import math

D_MODEL = 2048
BATCH = 1
SEQ = 256
DEPTH = 1

N_DN_HEADS = 8
DN_HEAD_DIM = 128
DN_WIDTH = N_DN_HEADS * DN_HEAD_DIM
N_FOURIER_GROUPS = 8
FOURIER_GROUP_DIM = 128
FOURIER_WIDTH = N_FOURIER_GROUPS * FOURIER_GROUP_DIM
CONV_WIDTH = 5
CHUNK = 64
D_FF = 4 * D_MODEL
N_BRANCHES = 2
EPS = 1e-6

SPLIT_SIZES = (DN_WIDTH, DN_WIDTH, DN_WIDTH, DN_WIDTH, FOURIER_WIDTH, 4 * N_DN_HEADS, N_BRANCHES * D_MODEL)
IN_WIDTH = int(sum(SPLIT_SIZES))
SPLIT_POINTS = tuple(int(s) for s in np.cumsum(SPLIT_SIZES)[:-1])


def rms_norm(x, g):
    xf = x.astype(jnp.float32)
    y = xf * lax.rsqrt(jnp.mean(xf * xf, axis=-1, keepdims=True) + EPS)
    return (y * g.astype(jnp.float32)).astype(x.dtype)

def l2_norm(x):
    return x * lax.rsqrt(jnp.sum(x * x, axis=-1, keepdims=True) + EPS)

def centred_short_conv(u, w):
    c = u.shape[-1]
    pad = (CONV_WIDTH - 1) // 2
    return lax.conv_general_dilated(u, w[:, None, :].astype(u.dtype), window_strides=(1,),
                                    padding=[(pad, pad)], dimension_numbers=("NWC", "WIO", "NWC"),
                                    feature_group_count=c)

def gated_delta_rule_chunked(q, k, v, g, beta):
    b, h, t, dk = q.shape
    dv = v.shape[-1]
    n = t // CHUNK
    q = q.reshape(b, h, n, CHUNK, dk)
    k = k.reshape(b, h, n, CHUNK, dk)
    v = v.reshape(b, h, n, CHUNK, dv)
    gc = jnp.cumsum(g.reshape(b, h, n, CHUNK), axis=-1)
    beta = beta.reshape(b, h, n, CHUNK, 1)
    idx = jnp.arange(CHUNK)
    incl = idx[:, None] >= idx[None, :]
    strict = idx[:, None] > idx[None, :]
    diff = gc[..., :, None] - gc[..., None, :]
    decay = jnp.where(incl, jnp.exp(jnp.where(incl, diff, 0.0)), 0.0)
    kb = k * beta
    m = jnp.where(strict, jnp.einsum("bhnid,bhnjd->bhnij", kb, k) * decay, 0.0)
    a_mat = m + jnp.eye(CHUNK, dtype=m.dtype)
    rhs = jnp.concatenate([v * beta, kb * jnp.exp(gc)[..., None]], axis=-1)
    sol = lax.linalg.triangular_solve(a_mat, rhs, left_side=True, lower=True, unit_diagonal=True)
    u, w = sol[..., :dv], sol[..., dv:]
    qk = jnp.where(incl, jnp.einsum("bhnid,bhnjd->bhnij", q, k) * decay, 0.0)
    q_dec = q * jnp.exp(gc)[..., None]
    k_dec = k * jnp.exp(gc[..., -1:] - gc)[..., None]
    g_last = jnp.exp(gc[..., -1])
    xs = tuple(jnp.moveaxis(a, 2, 0) for a in (q_dec, k_dec, u, w, qk, g_last))

    def step(s, inp):
        qd, kd, uc, wc, qkc, gl = inp
        v_new = uc - jnp.einsum("bhck,bhkv->bhcv", wc, s)
        o = jnp.einsum("bhck,bhkv->bhcv", qd, s) + jnp.einsum("bhij,bhjv->bhiv", qkc, v_new)
        s = s * gl[..., None, None] + jnp.einsum("bhck,bhcv->bhkv", kd, v_new)
        return s, o

    s0 = jnp.zeros((b, h, dk, dv), jnp.float32)
    _, o = lax.scan(step, s0, xs)
    return jnp.moveaxis(o, 0, 2).reshape(b, h, t, dv)

def gated_deltanet_branch(q, k, v, z, scal, conv_w, a_log_f, a_log_b, dt_b_f, dt_b_b, g_head, w_up):
    b, t, _ = q.shape
    dtype = q.dtype
    qkv = jax.nn.silu(centred_short_conv(jnp.concatenate([q, k, v], axis=-1), conv_w)).astype(jnp.float32)
    q, k, v = jnp.split(qkv, 3, axis=-1)
    heads = lambda a: a.reshape(b, t, N_DN_HEADS, DN_HEAD_DIM).transpose(0, 2, 1, 3)
    q = l2_norm(heads(q)) * (DN_HEAD_DIM ** -0.5)
    k = l2_norm(heads(k))
    v = heads(v)
    scal = scal.astype(jnp.float32).transpose(0, 2, 1)
    beta_f, beta_b, a_f, a_b = jnp.split(scal, 4, axis=1)
    beta_f, beta_b = jax.nn.sigmoid(beta_f), jax.nn.sigmoid(beta_b)
    g_f = -jnp.exp(a_log_f.astype(jnp.float32))[:, None] * jax.nn.softplus(a_f + dt_b_f.astype(jnp.float32)[:, None])
    g_b = -jnp.exp(a_log_b.astype(jnp.float32))[:, None] * jax.nn.softplus(a_b + dt_b_b.astype(jnp.float32)[:, None])
    o_f = gated_delta_rule_chunked(q, k, v, g_f, beta_f)
    flip = lambda a: jnp.flip(a, axis=2)
    o_b = flip(gated_delta_rule_chunked(flip(q), flip(k), flip(v), flip(g_b), flip(beta_b)))
    o = (o_f + o_b).transpose(0, 2, 1, 3)
    o = o * lax.rsqrt(jnp.mean(o * o, axis=-1, keepdims=True) + EPS) * g_head.astype(jnp.float32)
    o = o * jax.nn.silu(z.astype(jnp.float32).reshape(b, t, N_DN_HEADS, DN_HEAD_DIM))
    return o.reshape(b, t, DN_WIDTH).astype(dtype) @ w_up

def fourier_branch(f, w_lin):
    b, t, _ = f.shape
    fg = f.astype(jnp.float32).reshape(b, t, N_FOURIER_GROUPS, FOURIER_GROUP_DIM)
    fr = jnp.real(jnp.fft.fft2(fg, axes=(1, 3), norm="ortho"))
    return fr.reshape(b, t, FOURIER_WIDTH).astype(f.dtype) @ w_lin

def first_inputs(seed: int = 0) -> dict:
    key = jax.random.key(seed)
    ks = jax.random.split(key, 20)
    nrm = lambda k, shape, fan_in: jax.random.normal(k, shape, jnp.float32) * (fan_in ** -0.5)
    gain = lambda k, shape: 1.0 + 0.02 * jax.random.normal(k, shape, jnp.float32)
    a_log = lambda k: jnp.log(jax.random.uniform(k, (DEPTH, N_DN_HEADS), jnp.float32, 1.0, 16.0))

    def dt_bias(k):
        dt = jnp.exp(jax.random.uniform(k, (DEPTH, N_DN_HEADS), jnp.float32, np.log(1e-3), np.log(1e-1)))
        return dt + jnp.log(-jnp.expm1(-dt))

    return {
        "x": jax.random.normal(ks[0], (BATCH, SEQ, D_MODEL), jnp.float32),
        "g_mix": gain(ks[1], (DEPTH, D_MODEL)),
        "w_in": nrm(ks[2], (DEPTH, D_MODEL, IN_WIDTH), D_MODEL),
        "conv_w": nrm(ks[3], (DEPTH, CONV_WIDTH, 3 * DN_WIDTH), CONV_WIDTH),
        "a_log_fwd": a_log(ks[4]),
        "a_log_bwd": a_log(ks[5]),
        "dt_bias_fwd": dt_bias(ks[6]),
        "dt_bias_bwd": dt_bias(ks[7]),
        "g_dn_head": gain(ks[8], (DEPTH, DN_HEAD_DIM)),
        "w_dn_up": nrm(ks[9], (DEPTH, DN_WIDTH, D_MODEL), DN_WIDTH),
        "w_fourier": nrm(ks[10], (DEPTH, FOURIER_WIDTH, D_MODEL), FOURIER_WIDTH),
        "w_o": nrm(ks[11], (DEPTH, D_MODEL, D_MODEL), D_MODEL),
        "g_mlp": gain(ks[12], (DEPTH, D_MODEL)),
        "w_mlp_up": nrm(ks[13], (DEPTH, D_MODEL, D_FF), D_MODEL),
        "w_mlp_down": nrm(ks[14], (DEPTH, D_FF, D_MODEL), D_FF),
        "g_final": gain(ks[15], (D_MODEL,)),
    }

def first_block(x, g_mix, w_in, conv_w, a_log_fwd, a_log_bwd, dt_bias_fwd, dt_bias_bwd, g_dn_head,
              w_dn_up, w_fourier, w_o, g_mlp, w_mlp_up, w_mlp_down, g_final):
    for l in range(DEPTH):
        h = rms_norm(x, g_mix[l])
        proj = h @ w_in[l]
        q, k, v, z, f, scal, gates = jnp.split(proj, SPLIT_POINTS, axis=-1)
        y_a = gated_deltanet_branch(q, k, v, z, scal, conv_w[l], a_log_fwd[l], a_log_bwd[l],
                                    dt_bias_fwd[l], dt_bias_bwd[l], g_dn_head[l], w_dn_up[l])
        y_f = fourier_branch(f, w_fourier[l])
        gate_a, gate_f = jnp.split(jax.nn.sigmoid(gates), N_BRANCHES, axis=-1)
        x = x + (gate_a * y_a + gate_f * y_f) @ w_o[l]
        h = rms_norm(x, g_mlp[l])
        x = x + jnp.square(jax.nn.relu(h @ w_mlp_up[l])) @ w_mlp_down[l]
    return rms_norm(x, g_final)


N_MEM = 256
BRANCH_W = 1024
N_BRANCH = 3
CHUNK_2 = 128
SG_GROUPS = 8
SG_GROUP_W = BRANCH_W // SG_GROUPS
SSM_GROUP_W = 16
SSM_GROUPS = BRANCH_W // SSM_GROUP_W
SSM_STATE = 64
XA_HEADS = 4
XA_HEAD_DIM = BRANCH_W // XA_HEADS
N_IN = 7 * BRANCH_W + N_BRANCH * D_MODEL
DT_MIN = 1e-3
DT_MAX = 1e-1
EIG_CLIP = 1e-4


def rms_norm_2(x, g):
    xf = x.astype(jnp.float32)
    y = xf * lax.rsqrt(jnp.mean(xf * xf, axis=-1, keepdims=True) + EPS)
    return (y * g.astype(jnp.float32)).astype(x.dtype)

def layer_norm(x, g, b):
    xf = x.astype(jnp.float32)
    mu = jnp.mean(xf, axis=-1, keepdims=True)
    xc = xf - mu
    y = xc * lax.rsqrt(jnp.mean(xc * xc, axis=-1, keepdims=True) + EPS)
    return (y * g.astype(jnp.float32) + b.astype(jnp.float32)).astype(x.dtype)

def spatial_gating(u, v, ln_g, ln_b, w_s, b_s):
    bsz, seq, _ = v.shape
    n_chunks = seq // CHUNK_2
    vn = layer_norm(v, ln_g, ln_b).reshape(bsz, n_chunks, CHUNK_2, SG_GROUPS, SG_GROUP_W)
    causal = jnp.tril(jnp.ones((CHUNK_2, CHUNK_2), dtype=bool))
    w = jnp.where(causal[None], w_s, 0).astype(vn.dtype)
    z = jnp.einsum('gts,bcsgd->bctgd', w, vn) + b_s.T[None, None, :, :, None].astype(vn.dtype)
    return u * z.reshape(bsz, seq, BRANCH_W)

def s5_branch(u, a_re, a_im, log_dt, b_re, b_im, c_re, c_im, d, glu_w, glu_b):
    bsz, seq, _ = u.shape
    f32 = jnp.float32
    uf = u.astype(f32).reshape(bsz, seq, SSM_GROUPS, SSM_GROUP_W)
    lam = lax.complex(jnp.minimum(a_re.astype(f32), -EIG_CLIP), a_im.astype(f32))
    dt = jnp.exp(log_dt.astype(f32))[:, None]
    lam_bar = jnp.exp(lam * dt)
    b_mat = lax.complex(b_re.astype(f32), b_im.astype(f32))
    b_bar = ((lam_bar - 1) / lam)[:, :, None] * b_mat
    c_mat = lax.complex(c_re.astype(f32), c_im.astype(f32))
    bu = jnp.einsum('bsgh,gph->bsgp', uf.astype(jnp.complex64), b_bar)
    a_el = jnp.broadcast_to(lam_bar, bu.shape)

    def combine(left, right):
        a_l, s_l = left
        a_r, s_r = right
        return a_r * a_l, a_r * s_l + s_r

    _, states = lax.associative_scan(combine, (a_el, bu), axis=1)
    y = jnp.einsum('bsgp,ghp->bsgh', states, c_mat).real + d.astype(f32) * uf
    y = jax.nn.gelu(y.reshape(bsz, seq, BRANCH_W)).astype(u.dtype)
    return y * jax.nn.sigmoid(y @ glu_w + glu_b)

def memory_cross_attention(q, mem_n, w_k, w_v):
    bsz, seq, _ = q.shape
    n_mem = mem_n.shape[1]
    qh = q.reshape(bsz, seq, XA_HEADS, XA_HEAD_DIM)
    k = (mem_n @ w_k).reshape(bsz, n_mem, XA_HEADS, XA_HEAD_DIM)
    v = (mem_n @ w_v).reshape(bsz, n_mem, XA_HEADS, XA_HEAD_DIM)
    scores = jnp.einsum('bshd,bmhd->bhsm', qh, k).astype(jnp.float32) * (XA_HEAD_DIM ** -0.5)
    p = jax.nn.softmax(scores, axis=-1).astype(v.dtype)
    o = jnp.einsum('bhsm,bmhd->bshd', p, v)
    return o.reshape(bsz, seq, BRANCH_W)

def hybrid_layer(x, mem, pre_g, post_g, mem_g, w_in, sg_ln_g, sg_ln_b, sg_w, sg_b,
                 a_re, a_im, log_dt, b_re, b_im, c_re, c_im, d, glu_w, glu_b,
                 xa_wk, xa_wv, w_branch, w_out):
    bsz, seq, _ = x.shape
    h = rms_norm_2(x, pre_g)
    proj = h @ w_in
    splits = [BRANCH_W * i for i in range(1, 8)]
    a_u, a_v, a_g, b_x, b_g, x_q, x_g, gate_logits = jnp.split(proj, splits, axis=-1)
    y_a = spatial_gating(a_u, a_v, sg_ln_g, sg_ln_b, sg_w, sg_b) * jax.nn.silu(a_g)
    y_b = s5_branch(b_x, a_re, a_im, log_dt, b_re, b_im, c_re, c_im, d, glu_w, glu_b) * jax.nn.silu(b_g)
    y_x = memory_cross_attention(x_q, rms_norm_2(mem, mem_g), xa_wk, xa_wv) * jax.nn.silu(x_g)
    ys = jnp.stack([y_a, y_b, y_x], axis=2)
    branch = jnp.einsum('bsnc,ncd->bsnd', ys, w_branch)
    gates = jax.nn.sigmoid(gate_logits.reshape(bsz, seq, N_BRANCH, D_MODEL))
    merged = jnp.sum(gates * branch, axis=2)
    out = merged @ w_out
    return x + rms_norm_2(out, post_g)

def second_inputs(seed: int = 0) -> dict:
    key = jax.random.key(seed)
    ks = jax.random.split(key, 26)
    f32 = jnp.float32

    def nrm(k, shape, scale):
        return jax.random.normal(k, shape, f32) * scale

    L, D, W = DEPTH, D_MODEL, BRANCH_W
    G, H, P = SSM_GROUPS, SSM_GROUP_W, SSM_STATE
    x = nrm(ks[0], (BATCH, SEQ, D), 1.0)
    mem = nrm(ks[1], (BATCH, N_MEM, D), 1.0)
    pre_norm_g = 1.0 + nrm(ks[2], (L, D), 0.05)
    post_norm_g = 1.0 + nrm(ks[3], (L, D), 0.05)
    mem_norm_g = 1.0 + nrm(ks[4], (L, D), 0.05)
    w_in = nrm(ks[5], (L, D, N_IN), D ** -0.5)
    sg_ln_g = 1.0 + nrm(ks[6], (L, W), 0.05)
    sg_ln_b = nrm(ks[7], (L, W), 0.01)
    sg_w = nrm(ks[8], (L, SG_GROUPS, CHUNK_2, CHUNK_2), 0.5 * CHUNK_2 ** -0.5)
    sg_b = 1.0 + nrm(ks[9], (L, SG_GROUPS, CHUNK_2), 0.1)
    ssm_a_re = -0.5 + nrm(ks[10], (L, G, P), 0.01)
    ssm_a_im = jnp.broadcast_to(math.pi * jnp.arange(P, dtype=f32), (L, G, P))
    ssm_log_dt = jax.random.uniform(ks[11], (L, G), f32, math.log(DT_MIN), math.log(DT_MAX))
    ssm_b_re = nrm(ks[12], (L, G, P, H), (2 * H) ** -0.5)
    ssm_b_im = nrm(ks[13], (L, G, P, H), (2 * H) ** -0.5)
    ssm_c_re = nrm(ks[14], (L, G, H, P), P ** -0.5)
    ssm_c_im = nrm(ks[15], (L, G, H, P), P ** -0.5)
    ssm_d = nrm(ks[16], (L, G, H), 0.5)
    glu_w = nrm(ks[17], (L, W, W), W ** -0.5)
    glu_b = nrm(ks[18], (L, W), 0.01)
    xa_wk = nrm(ks[19], (L, D, W), D ** -0.5)
    xa_wv = nrm(ks[20], (L, D, W), D ** -0.5)
    w_branch = nrm(ks[21], (L, N_BRANCH, W, D), W ** -0.5)
    w_out = nrm(ks[22], (L, D, D), D ** -0.5)
    return {'x': x, 'mem': mem, 'pre_norm_g': pre_norm_g, 'post_norm_g': post_norm_g,
            'mem_norm_g': mem_norm_g, 'w_in': w_in, 'sg_ln_g': sg_ln_g, 'sg_ln_b': sg_ln_b,
            'sg_w': sg_w, 'sg_b': sg_b, 'ssm_a_re': ssm_a_re, 'ssm_a_im': ssm_a_im,
            'ssm_log_dt': ssm_log_dt, 'ssm_b_re': ssm_b_re, 'ssm_b_im': ssm_b_im,
            'ssm_c_re': ssm_c_re, 'ssm_c_im': ssm_c_im, 'ssm_d': ssm_d, 'glu_w': glu_w,
            'glu_b': glu_b, 'xa_wk': xa_wk, 'xa_wv': xa_wv, 'w_branch': w_branch, 'w_out': w_out}

def second_block(x, mem, pre_norm_g, post_norm_g, mem_norm_g, w_in, sg_ln_g, sg_ln_b, sg_w, sg_b,
              ssm_a_re, ssm_a_im, ssm_log_dt, ssm_b_re, ssm_b_im, ssm_c_re, ssm_c_im, ssm_d,
              glu_w, glu_b, xa_wk, xa_wv, w_branch, w_out):
    for l in range(DEPTH):
        x = hybrid_layer(x, mem, pre_norm_g[l], post_norm_g[l], mem_norm_g[l], w_in[l],
                         sg_ln_g[l], sg_ln_b[l], sg_w[l], sg_b[l],
                         ssm_a_re[l], ssm_a_im[l], ssm_log_dt[l], ssm_b_re[l], ssm_b_im[l],
                         ssm_c_re[l], ssm_c_im[l], ssm_d[l], glu_w[l], glu_b[l],
                         xa_wk[l], xa_wv[l], w_branch[l], w_out[l])
    return x


def setup_inputs(seed=0):
    out = dict(first_inputs(seed))
    for name, value in second_inputs(seed + 1).items():
        if name != "x":
            out[name + "_2"] = value
    return out


def reference(
    x, g_mix, w_in, conv_w, a_log_fwd, a_log_bwd, dt_bias_fwd, dt_bias_bwd, g_dn_head, w_dn_up,
    w_fourier, w_o, g_mlp, w_mlp_up, w_mlp_down, g_final, mem_2, pre_norm_g_2, post_norm_g_2,
    mem_norm_g_2, w_in_2, sg_ln_g_2, sg_ln_b_2, sg_w_2, sg_b_2, ssm_a_re_2, ssm_a_im_2,
    ssm_log_dt_2, ssm_b_re_2, ssm_b_im_2, ssm_c_re_2, ssm_c_im_2, ssm_d_2, glu_w_2, glu_b_2,
    xa_wk_2, xa_wv_2, w_branch_2, w_out_2,
):
    x = first_block(
        x, g_mix, w_in, conv_w, a_log_fwd, a_log_bwd, dt_bias_fwd, dt_bias_bwd, g_dn_head,
        w_dn_up, w_fourier, w_o, g_mlp, w_mlp_up, w_mlp_down, g_final,
    )
    return second_block(
        x, mem_2, pre_norm_g_2, post_norm_g_2, mem_norm_g_2, w_in_2, sg_ln_g_2, sg_ln_b_2,
        sg_w_2, sg_b_2, ssm_a_re_2, ssm_a_im_2, ssm_log_dt_2, ssm_b_re_2, ssm_b_im_2,
        ssm_c_re_2, ssm_c_im_2, ssm_d_2, glu_w_2, glu_b_2, xa_wk_2, xa_wv_2, w_branch_2,
        w_out_2,
    )


_drawn_inputs = setup_inputs


def setup_inputs(seed=0):
    import zlib

    import numpy as np

    out = dict(_drawn_inputs(seed))
    spreads = {}
    factors = {'g_mix': 3.306,
     'g_dn_head': 6.559,
     'mem_norm_g_2': 8.0,
     'sg_ln_g_2': 30.955,
     'sg_ln_b_2': 200.0,
     'ssm_a_re_2': 64.0,
     'ssm_a_im_2': 24.024,
     'ssm_log_dt_2': 27.656,
     'ssm_b_re_2': 33.912,
     'ssm_b_im_2': 34.272,
     'ssm_c_re_2': 32.52,
     'ssm_c_im_2': 34.688,
     'glu_w_2': 25.193,
     'glu_b_2': 200.0,
     'g_mlp': 8.0,
     'sg_b_2': 5.139,
     'ssm_d_2': 3.3}
    for name, (base, spread) in spreads.items():
        noise = np.random.default_rng([zlib.crc32(name.encode()), seed]).standard_normal(out[name].shape)
        drawn = base * np.exp(spread * noise) if base else spread * noise
        out[name] = __import__('jax').numpy.asarray(drawn.astype(out[name].dtype))
    for name, factor in factors.items():
        out[name] = (out[name] * factor).astype(out[name].dtype)
    return out
```

```python
from contextlib import ExitStack

import numpy as np

import concourse.bass as bass
from concourse import mybir

F32 = mybir.dt.float32
F32R = mybir.dt.float32r
ALU = mybir.AluOpType
ACT = mybir.ActivationFunctionType
AX = mybir.AxisListType

P = 128
T = 256
NT = T // P
D = 2048
KD = D // P
W = 1024
KW = W // P
HD = 128
NW = 512
KU = 4
UE = KU * NW
RAW = 4
SPLIT = 2
EPS = 1e-6
NPIECE = 8
LEVELS = (1, 2, 4, 8, 16, 32)
MAGIC = 12582912.0
TWO_PI = (6.28125, 0.0019340515136718750, 1.2556659146e-06)


def weight_chunks():
    c = []
    add = lambda name, n0, n1, units, by: c.extend((name, n, units, by) for n in range(n0, n1))
    add("w_f", 0, 2, 4, "act")
    for half in (0, 1):
        for name in ("w_q", "w_k", "w_v"):
            add(name, half, half + 1, 4, "act")
        if half == 0:
            add("w_z", 0, 2, 4, "act")
            add("w_gate_f", 0, 4, 4, "act")
    add("w_gate_a", 0, 4, 4, "act")
    add("w_fourier", 0, 4, 2, "dve")
    add("w_dn_up", 0, 4, 2, "dve")
    add("w_o", 0, 4, 4, "dve")
    add("w_mlp_up", 0, 2, 4, "act")
    for p in range(NPIECE):
        if p + 1 < NPIECE:
            add("w_mlp_up", 2 * p + 2, 2 * p + 4, 4, "act")
        c.extend((f"w_mlp_down{p}", n, 2, "dve") for n in range(4))
    add("xa_wv", 0, 2, 4, "act")
    add("xa_wk", 0, 2, 4, "act")
    for name in ("w2_bx", "w2_bg", "w2_av", "w2_au", "w2_ag", "w2_xq", "w2_xg"):
        add(name, 0, 2, 4, "act")
    for n in range(3):
        add(f"w2_gate{n}", 0, 4, 4, "act")
    add("glu_w", 0, 2, 2, "dve")
    for n in (0, 2, 1):
        add(f"w_branch{n}", 0, 4, 2, "dve")
    add("w_out", 0, 4, 4, "dve")
    return c


CHUNKS = weight_chunks()
INDEX = {(c[0], c[1]): i for i, c in enumerate(CHUNKS)}
FIRST = list(np.cumsum([0] + [c[2] for c in CHUNKS]))
FIRST = [int(f) for f in FIRST]
UNITS = FIRST[-1]
EMPTIED = [sum(1 for c in CHUNKS[:i + 1] if c[3] == by) * NT for i in range(len(CHUNKS))
           for by in ("act", "dve")]


def emptied(i, by):
    return EMPTIED[2 * i + (by == "dve")]


def end(name, n):
    return FIRST[INDEX[(name, n)] + 1]


SPILLED = {"w_z": ACT.Silu, "w_gate_f": ACT.Sigmoid, "w_gate_a": ACT.Sigmoid,
           "xa_wv": ACT.Copy, "xa_wk": ACT.Copy, "w2_bg": ACT.Silu, "w2_av": ACT.Copy,
           "w2_au": ACT.Copy, "w2_ag": ACT.Silu, "w2_xq": ACT.Copy, "w2_xg": ACT.Silu,
           "w2_bx": ACT.Copy,
           "w2_gate0": ACT.Sigmoid, "w2_gate1": ACT.Sigmoid, "w2_gate2": ACT.Sigmoid}
SPILLS = [i for i, c in enumerate(CHUNKS) if c[0] in SPILLED]
SPILL_OF = {i: k for k, i in enumerate(SPILLS)}

SMALL = [("ident", 128), ("ones", 128), ("LE", 128), ("GE", 128), ("GT", 128), ("LT", 128), ("causal", 128),
         ("chunk", 256), ("level_f", 768), ("level_b", 768),
         ("g_mix", 16), ("g_mlp", 16), ("pre_g", 16), ("mem_g", 16), ("g_head", 1),
         ("conv_w", 120), ("a_log", 16), ("dt_bias", 16),
         ("a_re", 32), ("a_im", 32), ("log_dt", 32), ("d", 8), ("sg_b", 8)]
AT, _n = {}, 0
for _name, _w in SMALL:
    AT[_name] = (_n, _n + _w)
    _n += _w
NSMALL = _n


def mask_constants():
    r, c = np.meshgrid(np.arange(P), np.arange(P), indexing="ij")
    same = r // 64 == c // 64
    out = {"ident": r == c, "ones": r >= 0, "LE": same & (r <= c), "GE": same & (r >= c),
           "GT": same & (r > c), "LT": same & (r < c), "causal": r <= c,
           "chunk": np.concatenate([r // 64 == 0, r // 64 == 1], 1)}
    lower = [(r // (2 * s) == c // (2 * s)) & (r // s % 2 == 1) & (c // s % 2 == 0) for s in LEVELS]
    out["level_f"] = np.concatenate([m.T for m in lower], 1)
    out["level_b"] = np.concatenate(lower, 1)
    out = {k: v.astype(np.float32) for k, v in out.items()}
    t = np.arange(T)
    a = 2 * np.pi * np.outer(t, t) / T
    cs = np.concatenate([np.cos(a), np.sin(a)], 1) / np.sqrt(T)
    d = np.arange(P)
    b = 2 * np.pi * np.outer(d, d) / P
    dft = np.concatenate([cs.reshape(NT, P, 2 * T)[0], cs.reshape(NT, P, 2 * T)[1],
                          np.cos(b) / np.sqrt(P), -np.sin(b) / np.sqrt(P)], 1)
    return out, dft.astype(np.float32)


def delta_steps(half):
    s = [("conv_in", half, 2), ("conv_back", half, 2), ("key_rows", half)]
    for t in range(NT):
        s += [("gram", half, t), ("decay", half, t), ("turn", half, t)]
        for n in range(1, len(LEVELS)):
            s += [("solve_y", half, t, n), ("solve_x", half, t, n)]
    for st in range(4):
        s += [("scan_in", half, st), ("scan_new", half, st), ("scan_out", half, st)]
    return s


def schedule():
    s = {}
    put = lambda slot, *step: s.setdefault(slot, []).append(step)
    f = end("w_f", 1)
    put(f, "scalars")
    put(f + 2, "decays")
    for g in range(9):
        put(f + g, "fourier", g)
    for half in (0, 1):
        put(end("w_q", half), "conv_in", half, 0)
        put(end("w_q", half) + 1, "conv_norm", half, 0)
        put(end("w_k", half), "conv_in", half, 1)
        put(end("w_k", half) + 1, "conv_norm", half, 1)
        at = end("w_v", half)
        steps, rate = delta_steps(half), 2 + half
        for i, step in enumerate(steps):
            put(at + i // rate, *step)
        last = at + len(steps) // rate
        assert last < (end("w_q", 1) - 1 if half == 0 else end("w_gate_a", 3)), last
    put(end("w_gate_a", 3) - 1, "load_z")
    for k in range(8):
        put(end("w_gate_a", 3) - 1 if k < 2 else end("w_fourier" if k < 6 else "w_dn_up", (k - 2) % 4) - 1,
            "load_gate", k)
    put(end("w_gate_a", 3) - 1, "heads_norm")
    put(end("w_dn_up", 0), "load_x")
    put(end("w_fourier", 0), "heads_turn")
    put(end("w_dn_up", 3) - 1, "y_turn")
    put(end("w_o", 3) - 1, "mlp_norm")
    put(end("w_mlp_up", 0), "hidden", 0, 0)
    put(end("w_mlp_up", 0) + 1, "mem_turn", 0)
    put(end("w_mlp_up", 0) + 2, "mem_turn", 1)
    put(end("w_mlp_up", 1) - 1, "hidden", 0, 1)
    for t in range(NT):
        put(end("w_mlp_up", 0) + t, "load_mem", t)
    p = NPIECE - 1
    put(end(f"w_mlp_down{p}", 2) - 2, "load_g_final")
    put(end("w_mlp_up", 2 * p), "hidden", p, 0)
    put(end("w_mlp_up", 2 * p + 1), "hidden", p, 1)
    put(end(f"w_mlp_down{p}", 3) - 1, "final_norm")
    put(end("xa_wk", 1) - 1, "ssm_small")
    put(end("xa_wk", 1) - 1, "load_c")
    a = end("w2_bx", 1) + 1
    put(a - 1, "load_u")
    for ct in range(KW):
        put(a + 4 * ct, "load_b_pad", ct)
    put(a, "ssm_u")
    for i in range(17):
        put(a + 3 + 2 * i, "ssm", i)
    a += 3 + 2 * 17
    put(a - 1, "load_gating")
    put(a, "sg_norm")
    put(a + 2, "sg_mix")
    put(a + 4, "sg_turn")
    put(a + 6, "gelu_turn")
    a = max(a + 8, end("w2_xg", 1) + 1)
    put(a - 1, "load_memory")
    put(a, "xa_k")
    put(a + 1, "load_xq")
    put(a + 2, "xa_q")
    for h in range(4):
        put(a + 4 + 3 * h, "xa_score", h)
        put(a + 5 + 3 * h, "xa_prob", h)
        put(a + 6 + 3 * h, "xa_out", h)
    assert a + 16 < end("w2_gate2", 3)
    put(a + 16, "load_xg")
    for k in range(12):
        j, n = (0, 2, 1)[(k - 2) // 4], (k - 2) % 4
        put(end("w2_gate2", 3) if k < 2 else end(f"w_branch{j}", n) - 1, "load_gate2", k)
    put(end("glu_w", 1), "load_bg")
    put(end("w_branch1", 0), "load_post_g")
    put(end("w2_gate2", 3) - 1, "xa_turn")
    put(end("glu_w", 1) - 1, "glu_rest")
    put(end("w_branch0", 0) - 1, "glu_turn")
    put(end("w_branch1", 3) - 1, "merge_turn")
    return s


SCHED = schedule()
LOOP0 = FIRST[INDEX[("w_mlp_up", 2)]]
LOOP_UNITS = 32
LOOPS = 3


class Side:

    def __init__(self, key, eng, sems, old, new):
        self.key, self.eng, self.sems, self.old, self.new = key, eng, sems, old, new
        self.count, self.it, self.per = 0, None, None

    def done(self, *names):
        self.count += 1
        for n in names:
            self.new[n] = (self.key, self.count)
        return 1

    def _in_loop(self, key, value):
        return value if self.it is None else value + self.it * self.per[key]

    def engine_of(self, name):
        return self.old[name][0] if self.old else "act"

    def at(self, *names):
        marks = [self.old[n] if self.old else ("act", 1) for n in names]
        assert len({key for key, _ in marks}) == 1, names
        return self._in_loop(marks[0][0], max(value for _, value in marks))

    def here(self):
        assert self.count > 0
        return self._in_loop(self.key, self.count)


KB = 1024


def build(nc, t_in, out, old, new):
    with ExitStack() as ctx:
        sem = lambda n: ctx.enter_context(nc.semaphore(n))
        base = -(-nc.sbuf_base // 64) * 64
        ctx.enter_context(nc.sbuf_tensor("arena", [P, 52984], F32))
        top = [0]

        def at(name, off, shape, dt=F32):
            return nc.alloc_sbuf_tensor_at(name, shape, dt, offset=base + off)

        def take(name, shape, dt=F32):
            n = int(np.prod(shape[1:])) * (2 if dt == mybir.dt.bfloat16 else 4)
            off = top[0]
            top[0] += -(-n // 64) * 64
            return at(name, off, shape, dt)

        raw = take("raw", [P, RAW, UE])
        w_hi = take("w_hi", [P, SPLIT, UE], F32R)
        w_lo = take("w_lo", [P, SPLIT, UE], F32R)
        a_hi = take("a_hi", [P, KD, T], F32R)
        a_lo = take("a_lo", [P, KD, T], F32R)
        bb = top[0]
        b_hi, b_lo = [], []
        for i in range(2):
            b_hi.append(take(f"b{i}_hi", [P, KW, T], F32R))
            b_lo.append(take(f"b{i}_lo", [P, KW, T], F32R))
        small = take("small", [P, NSMALL - 1536])
        levels = take("levels", [P, 2 * 6 * P], mybir.dt.bfloat16)
        ts = take("ts", [P, 2, NW])
        sc = take("sc", [P, 320])
        st_ = take("stats", [P, 96])
        dr = top[0]
        cols = {}
        off = 0
        for name, w in SMALL:
            if name in ("level_f", "level_b"):
                continue
            cols[name] = small[:, off:off + w]
            off += w
        ident, ones = cols["ident"], cols["ones"]
        level = [levels[:, 0:768].rearrange("p (n c) -> p n c", n=6),
                 levels[:, 768:1536].rearrange("p (n c) -> p n c", n=6)]

        def region(name, kb, shape, dt=F32):
            assert dr + kb * KB + int(np.prod(shape[1:])) * 4 <= 52984 * 4, name
            return at(name, dr + kb * KB, shape, dt)

        qT = region("qT", 0, [P, 4, T])
        kT = region("kT", 4, [P, 4, T])
        v_rows = region("v_rows", 8, [P, NT, 4, HD])
        k_dec = region("k_dec", 12, [P, 2, NT, 4, HD])
        solT = region("solT", 20, [P, NT, 2, 4, P])
        qkT = region("qkT", 28, [P, NT, 2, 4, P])
        qkv = region("qkv", 20, [P, 3, NT, NW])
        state = region("state", 36, [P, 2, 4, HD])
        o_rows = region("o_rows", 40, [P, NT, 8, HD])
        f_rows = region("f_rows", 48, [P, NT, W])
        work_c = region("work_c", 48, [P, 4, NW])
        stage = region("stage", 56, [P, 4, NW])
        gate_in = region("gate_in", 56, [P, 2, NT, NW])
        work_b = at("work_b", bb + 16 * KB, [P, 8, NW])
        dft = region("dft", 40, [P, 1280])
        fp = region("fp", 36, [P, 2, NW])
        padT = at("padT", bb + 16 * KB, [P, 4, 260])
        convT = at("convT", bb + 16 * KB + 4160, [P, 4, T])
        squares = at("squares", bb + 16 * KB + 4160 + 4096, [P, 4, T])
        w_sc = region("w_sc", 0, [P, KD * 32])
        w_sc_hi = region("w_sc_hi", 2, [P, KD, 32], F32R)
        w_sc_lo = region("w_sc_lo", 4, [P, KD, 32], F32R)
        level_in = at("level_in", bb + 16 * KB, [P, 1536])
        z_rows = region("z_rows", 16, [P, NT, 8, HD])
        heads = region("heads", 24, [P, NT, 8, HD])
        y_rows = region("y_rows", 0, [P, NT, D])
        x_rows = region("x_rows", 16, [P, NT, D])
        hidden = region("hidden", 0, [P, NT, W])
        mem_rows = region("mem_rows", 8, [P, D])
        m_hi = region("m_hi", 32, [P, KD, T], F32R)
        m_lo = region("m_lo", 48, [P, KD, T], F32R)
        stage_b = at("stage_b", bb, [P, 4, NW])
        gain = at("gain", bb + 8 * KB, [P, D])
        post_gain = region("post_gain", 40, [P, D])
        b_pad = at("b_pad", bb, [P, 2, 4, 2, P])
        c_pad = at("c_pad", bb + 8 * KB, [P, 2, 2, 640])
        rot = at("rot", bb + 18 * KB, [P, 2, 2, 2, T])
        ssm_t = at("ssm_t", bb + 26 * KB, [P, 40, 32])
        s_out = region("s_out", 0, [P, 2, 2, 2, T])
        prod = region("prod", 8, [P, 4, 2, T])
        c_in = region("c_in", 8, [P, 2, 32, 16])
        c_tmp = region("c_tmp", 12, [P, 2, 32, 16])
        pow_a = region("pow_a", 32, [P, 2, 32, 16])
        pow_b = region("pow_b", 36, [P, 2, 32, 16])
        c_eff = region("c_eff", 40, [P, 2, 32, 16])
        rad = region("rad", 44, [P, 32])
        u_rows = region("u_rows", 0, [P, NT, W])
        uT = region("uT", 48, [P, KW, T])
        av = region("av", 0, [P, NT, W])
        au = region("au", 8, [P, NT, W])
        ag = at("ag", bb + 16 * KB, [P, NT, W])
        ln_gb = at("ln_gb", bb + 24 * KB, [P, 2, W])
        w_sg = region("w_sg", 32, [P, 8, P])
        km_rows = region("km_rows", 8, [P, NT, W])
        kmT = region("kmT", 0, [P, KW, T])
        vm = region("vm", 40, [P, NT, W])
        xq_rows = region("xq_rows", 8, [P, NT, W])
        xqT = region("xqT", 32, [P, KW, T])
        prob = region("prob", 8, [P, NT, T])
        probT = region("probT", 10, [P, NT, T])
        xg_rows = region("xg_rows", 8, [P, NT, W])
        glu_b = region("glu_b", 0, [P, W])
        glu = region("glu", 40, [P, NT, W])
        bg_rows = region("bg_rows", 48, [P, NT, W])
        acc = ctx.enter_context(nc.psum_tensor("acc", [P, 2, NT, NW], F32))
        banks = ctx.enter_context(nc.psum_tensor("banks", [P, 4, NW], F32))
        spilled = nc.dram_tensor("spilled", [len(SPILLS), NT, P, NW], F32).ap()

        act_done, dve_done, pool_done, pe_done = (sem(f"{e}_done") for e in ("act", "dve", "pool", "pe"))
        done = {"act": act_done, "dve": dve_done, "pool": pool_done, "pe": pe_done}
        landed = [sem(f"landed{i}") for i in range(RAW)]
        hi_split, lo_split = sem("hi_split"), sem("lo_split")
        pe_used = sem("pe_used")
        act_emptied, dve_emptied = sem("act_emptied"), sem("dve_emptied")
        spill_stored = [sem(f"spill_stored{i}") for i in range(RAW)]
        out_stored = sem("out_stored")
        loaded = {n: sem(f"loaded_{n}") for n in (
            "x", "small", "w_sc", "level", "dft", "z", "gate0", "gate1", "x2", "mem", "g_final", "c",
            "u", "b_pad0", "b_pad1", "av", "au", "ag", "ln_gb", "w_sg", "km", "vm", "xq", "xg",
            "glu_b", "bg", "post_g")}

        beta, g_log, e_sc = sc[:, 0:32], sc[:, 32:64], sc[:, 64:192]
        xa, tmp_a, tmp_b, e_alog = sc[:, 192:224], sc[:, 224:256], sc[:, 256:288], sc[:, 288:304]
        e_gc = lambda t, d, half: slice(64 + t * 16 + d * 8 + 4 * half, 68 + t * 16 + d * 8 + 4 * half)
        e_kd = lambda t, d, half: slice(96 + t * 16 + d * 8 + 4 * half, 100 + t * 16 + d * 8 + 4 * half)
        e_gl = lambda c, d, half: slice(128 + c * 16 + d * 8 + 4 * half, 132 + c * 16 + d * 8 + 4 * half)
        bt = lambda t, d, half: slice(t * 16 + d * 8 + 4 * half, t * 16 + d * 8 + 4 * half + 4)

        def wide(ap, m):
            return ap.unsqueeze(2).broadcast_to([ap.shape[0], ap.shape[1], m])

        def many(ap, n):
            return ap.unsqueeze(1).broadcast_to([ap.shape[0], n, ap.shape[1]])

        def four(ap):
            return ap.rearrange("p (h c) -> p h c", h=4)

        def flat(ap):
            return ap.rearrange("p a b -> p (a b)")

        BANK_OF = old["bank"] if old else {}
        bank_of = lambda tag, j: banks[:, BANK_OF.get((tag, j), 0), :]
        prod_y = lambda ct: ts[:, ct % 2, 0:T]
        ptmp = region("ptmp", 45, [P, 2 * T])
        scr = region("scr", 47, [P, 256])

        wb = [work_b[:, i, :] for i in range(8)] + [work_c[:, i, :] for i in range(4)]
        RG, EM, EB, MM = (lambda d: wb[d]), (lambda d: wb[2 + d]), (lambda d: wb[4 + d]), (lambda d: wb[6 + d])
        QK, MT = (lambda d: wb[8 + d]), (lambda d: wb[10 + d])
        bank = lambda i: banks[:, i, :]

        def b_dst(kt, t, parts=(b_hi, b_lo)):
            return [x[kt // KW][:, kt % KW:kt % KW + 4, t * P:(t + 1) * P] for x in parts]

        def a_dst(kt, t):
            return [x[:, kt:kt + 4, t * P:(t + 1) * P] for x in (a_hi, a_lo)]

        def rows_src(rows, t, kt):
            return lambda q: rows[:, t, (kt + q) * P:(kt + q + 1) * P]

        def wide_jobs(rows, dst, mode, gains=None, ts_=range(NT), kts=KD):
            return [(rows_src(rows, t, kt), dst(kt, t), mode, gains and wide(gains[:, kt:kt + 4], P))
                    for t in ts_ for kt in range(0, kts, 4)]

        JOBS = {
            "x": wide_jobs(x_rows, a_dst, "gain", cols["g_mix"]),
            "heads": [((lambda t, kt: lambda q: heads[:, t, kt + q, :])(t, kt), b_dst(KW + kt, t), "gain",
                       cols["g_head"].unsqueeze(2).broadcast_to([P, 4, P]))
                      for t in range(NT) for kt in (0, 4)],
            "y": wide_jobs(y_rows, b_dst, "plain"),
            "mlp": wide_jobs(y_rows, a_dst, "gain", cols["g_mlp"]),
            "pre": wide_jobs(y_rows, a_dst, "gain", cols["pre_g"]),
            "sg": wide_jobs(av, b_dst, "plain", kts=KW),
            "glu": wide_jobs(glu, lambda kt, t: a_dst(KW + kt, t), "plain", kts=KW),
            "xo": [((lambda t, kt: lambda q: xqT[:, 2 * ((kt + q) // 2) + t, (q % 2) * P:(q % 2 + 1) * P])(t, kt),
                    a_dst(kt, t), "plain", None) for t in range(NT) for kt in (0, 4)],
            "merge": wide_jobs(y_rows, b_dst, "plain"),
        }
        for t in range(NT):
            JOBS[f"mem{t}"] = [
                ((lambda kt: lambda q: mem_rows[:, (kt + q) * P:(kt + q + 1) * P])(kt),
                 [x[:, kt:kt + 4, t * P:(t + 1) * P] for x in (m_hi, m_lo)], "gain",
                 wide(cols["mem_g"][:, kt:kt + 4], P)) for kt in range(0, KD, 4)]
        for p in range(NPIECE):
            for j in range(2):
                JOBS[f"hidden{p}.{j}"] = [
                    (rows_src(hidden, t, 4 * j), b_dst(KW * (p % 2) + 4 * j, t), "square", None)
                    for t in range(NT)]

        def operand(name):
            if name in ("w_o", "w_out"):
                return lambda k: (b_hi[k // KW][:, k % KW, :], b_lo[k // KW][:, k % KW, :])
            if name in ("w_fourier", "w_branch0"):
                return lambda k: (b_hi[0][:, k, :], b_lo[0][:, k, :])
            if name in ("w_dn_up", "glu_w"):
                return lambda k: (b_hi[1][:, k, :], b_lo[1][:, k, :])
            if name.startswith("w_mlp_down"):
                i = int(name[10:]) % 2
                return lambda k: (b_hi[i][:, k, :], b_lo[i][:, k, :])
            if name.startswith("xa_w"):
                return lambda k: (m_hi[:, k, :], m_lo[:, k, :])
            first = KW if name == "w_branch1" else 0
            return lambda k: (a_hi[:, first + k, :], a_lo[:, first + k, :])

        spill = lambda name, n: spilled[SPILL_OF[INDEX[(name, n)]]].rearrange("t p n -> p t n")
        spills_until = lambda name, n, t: 16 * ((NT * SPILL_OF[INDEX[(name, n)]] + t) // RAW + 1)

        block = ctx.enter_context(nc.Block())

        def value(me, static, per):
            return static if me.it is None else static + me.it * per

        def drive(me, slot_work, after_loop):
            n = 0
            while n < UNITS:
                if n == LOOP0:
                    start = me.count
                    me.per = {k: v for k, v in (old or {}).get("per", {}).items()} if old else \
                        {"act": 0, "dve": 0, "pe": 0, "pool": 0}
                    with me.eng.Fori(0, LOOPS) as it:
                        me.it = it
                        for m in range(LOOP_UNITS):
                            slot_work(n + m)
                    me.it = None
                    per = me.count - start
                    new.setdefault("per", {})[me.key] = per
                    me.count += per * (LOOPS - 1)
                    for j in range(2):
                        for key, x in (("act", "hi"), ("dve", "lo")):
                            if me.key == key:
                                new[f"hidden{NPIECE - 2}.{j}.{x}"] = (key, me.count)
                                for k in range(NT):
                                    new[f"hidden{NPIECE - 2}.{j}.{k}.{x}"] = (key, me.count)
                    after_loop()
                    n += LOOPS * LOOP_UNITS
                    continue
                slot_work(n)
                n += 1

        def run_steps(me, steps, slot):
            if LOOP0 <= slot < LOOP0 + LOOP_UNITS:
                local = slot - LOOP0
                for s, piece, j in ((4, 1, 0), (8, 1, 1), (20, 2, 0), (24, 2, 1)):
                    if local == s:
                        steps["hidden"](piece, j)
                return
            for step in SCHED.get(slot, []):
                if step[0] in steps:
                    steps[step[0]](*step[1:])

        CHUNK_END = {FIRST[i + 1] - 1: i for i in range(len(CHUNKS))}
        CHUNK_AT = {}
        for i in range(len(CHUNKS)):
            for u in range(CHUNKS[i][2]):
                CHUNK_AT[FIRST[i] + u] = i

        @block.sync
        def _(sp):
            me = Side("sp", sp, done, old, new)

            def weight(n, it=None):
                if n >= RAW:
                    value = n - RAW + 1
                    sp.wait_ge(lo_split, value if it is None else value + it * LOOP_UNITS)
                if it is None:
                    src = t_in["w"][n]
                else:
                    src = t_in["w"][bass.ds(n + it * LOOP_UNITS, 1)].rearrange("a p n -> (a p) n")
                sp.dma_start(raw[:, n % RAW, :], src).then_inc(landed[n % RAW], 16)

            def load(dst, src, landing):
                sp.dma_start(dst, src).then_inc(landing, 16)

            def load_spilled(dst, matrix, n, landing):
                for t in range(NT):
                    k = (NT * SPILL_OF[INDEX[(matrix, n)]] + t) % RAW
                    sp.wait_ge(spill_stored[k], spills_until(matrix, n, t))
                sp.dma_start(dst, spill(matrix, n)).then_inc(landing, 16)

            def load_rows(dst, matrix, landing):
                for n in range(2):
                    load_spilled(dst[:, :, n * NW:(n + 1) * NW], matrix, n, landing)

            def load_z():
                sp.wait_ge(pe_done, me.at("scan1.3.out.PE"))
                sp.wait_ge(dve_done, me.at("scan1.3.out.DVE"))
                load_rows(z_rows[:, :, :, :].rearrange("p t h c -> p t (h c)"), "w_z", loaded["z"])

            def load_gate(k):
                m = "w_gate_f" if k < 4 else "w_gate_a"
                if k < 2:
                    for n in (2, 3):
                        for t in range(NT):
                            sp.wait_ge(spill_stored[(2 * n + t) % RAW], spills_until("w_gate_a", n, t))
                elif k < 6:
                    sp.wait_ge(dve_emptied, emptied(INDEX[("w_fourier", k - 2)], "dve"))
                else:
                    sp.wait_ge(dve_done, me.at(f"w_dn_up{k - 6}.y"))
                load_spilled(gate_in[:, k % 2], m, k % 4, loaded[f"gate{k % 2}"])

            def load_x():
                sp.wait_ge(act_done, me.at("heads.hi"))
                sp.wait_ge(dve_done, me.at("heads.lo"))
                load(x_rows[:, :, :], t_in["x"].rearrange("t p n -> p t n"), loaded["x2"])

            def load_mem(t):
                if t == 0:
                    sp.wait_ge(pe_done, me.at("mlp.T"))
                else:
                    sp.wait_ge(pe_done, me.at("mem0.T"))
                load(mem_rows[:, :], t_in["mem"][t], loaded["mem"])

            def load_g_final():
                sp.wait_ge(pe_used, end(f"w_mlp_down{NPIECE - 2}", 3))
                load(gain[:, :], t_in["g_final"], loaded["g_final"])

            def load_c():
                sp.wait_ge(pe_done, me.at("pre.T"))
                load(c_in[:, 0], t_in["c_re"], loaded["c"])
                load(c_in[:, 1], t_in["c_im"], loaded["c"])

            def load_u():
                sp.wait_ge(pe_done, me.at("pre.T"))
                load_rows(u_rows, "w2_bx", loaded["u"])

            def load_b_pad(ct):
                if ct >= 2:
                    sp.wait_ge(pe_done, me.at(f"ssm{2 * ct - 3}.bu"))
                else:
                    for t in range(NT):
                        sp.wait_ge(spill_stored[2 + t], spills_until("xa_wk", 1, t))
                load(b_pad[:, ct % 2], t_in["b_pad"][ct], loaded[f"b_pad{ct % 2}"])

            def load_gating():
                sp.wait_ge(pe_done, me.at("ssm16.y"))
                sp.wait_ge(dve_done, me.at("ssm15.DVE"))
                sp.wait_ge(pool_done, me.at("ssm15.POOL"))
                load_rows(av, "w2_av", loaded["av"])
                load_rows(au, "w2_au", loaded["au"])
                load_rows(ag, "w2_ag", loaded["ag"])
                load(ln_gb[:, :, :], t_in["ln_gb"], loaded["ln_gb"])
                load(w_sg[:, :, :], t_in["w_sg"], loaded["w_sg"])

            def load_memory():
                sp.wait_ge(act_done, me.at("sg.hi"))
                sp.wait_ge(dve_done, me.at("sg.lo"))
                load_rows(km_rows, "xa_wk", loaded["km"])
                load_rows(vm, "xa_wv", loaded["vm"])

            def load_xq():
                sp.wait_ge(pe_done, me.at("km.T"))
                load_rows(xq_rows, "w2_xq", loaded["xq"])

            def load_xg():
                sp.wait_ge(act_done, me.at("xa3.out"))
                sp.wait_ge(pe_done, me.at("xa3.score"))
                load_rows(xg_rows, "w2_xg", loaded["xg"])
                load(glu_b[:, :], t_in["glu_b"], loaded["glu_b"])

            def load_gate2(k):
                j, n = (0, 2, 1)[k // 4], k % 4
                if k < 2:
                    for c in (2, 3):
                        for t in range(NT):
                            sp.wait_ge(spill_stored[(2 * c + t) % RAW], spills_until("w2_gate2", c, t))
                elif k < 6:
                    sp.wait_ge(dve_emptied, emptied(INDEX[("w_branch0", k - 2)], "dve"))
                else:
                    sp.wait_ge(dve_done, me.at(f"w_branch{(0, 2, 1)[(k - 2) // 4]}{(k - 2) % 4}.y"))
                load_spilled(gate_in[:, k % 2], f"w2_gate{j}", n, loaded[f"gate{k % 2}"])

            def load_bg():
                sp.wait_ge(pe_done, me.at("gelu_rows.T"))
                load_rows(bg_rows, "w2_bg", loaded["bg"])

            def load_post_g():
                sp.wait_ge(pe_done, me.at("glu.T"))
                load(post_gain[:, :], t_in["post_g"], loaded["post_g"])

            def store(i):
                k = SPILL_OF[i]
                for t in range(NT):
                    sp.wait_ge(act_emptied, emptied(i, "act") - NT + t + 1)
                    b = (NT * k + t) % RAW
                    src = stage_b if CHUNKS[i][0].startswith("xa_w") else stage
                    sp.dma_start(spilled[k, t], src[:, b, :]).then_inc(spill_stored[b], 16)

            steps = {"load_z": load_z, "load_gate": load_gate, "load_x": load_x, "load_mem": load_mem,
                     "load_g_final": load_g_final, "load_c": load_c, "load_u": load_u,
                     "load_b_pad": load_b_pad, "load_gating": load_gating, "load_memory": load_memory,
                     "load_xq": load_xq, "load_xg": load_xg, "load_gate2": load_gate2,
                     "load_bg": load_bg, "load_post_g": load_post_g}
            load(x_rows[:, 0, :], t_in["x"][0], loaded["x"])
            load(small[:, :], t_in["small"], loaded["small"])
            load(x_rows[:, 1, :], t_in["x"][1], loaded["x"])
            load(w_sc[:, :], t_in["w_sc"], loaded["w_sc"])
            load(level_in[:, :], t_in["level"], loaded["level"])
            load(dft[:, :], t_in["dft"], loaded["dft"])
            for n in range(RAW):
                weight(n)
            ends = {FIRST[i + 1] - 1: i for i in SPILLS}
            n = 0
            while n < UNITS:
                if n == LOOP0:
                    with sp.Fori(0, LOOPS) as it:
                        for m in range(LOOP_UNITS):
                            weight(n + m + RAW, it)
                    n += LOOPS * LOOP_UNITS
                    continue
                if n + RAW < UNITS:
                    weight(n + RAW)
                if n in ends:
                    store(ends[n])
                run_steps(me, steps, n)
                n += 1
            for t in range(NT):
                sp.wait_ge(dve_done, me.at(f"out{t}"))
                sp.dma_start(out[0].rearrange("(t p) n -> t p n", p=P)[t], y_rows[:, t, :])\
                    .then_inc(out_stored, 16)
            sp.wait_ge(out_stored, 16 * NT)

        @block.scalar
        def _(act):
            me = Side("act", act, done, old, new)
            ts_user = [None, None]
            ts_turn = [0]

            def split(n):
                act.wait_ge(landed[n % RAW], value(me, 16 * (n // RAW + 1), 16 * LOOP_UNITS // RAW))
                if n >= SPLIT:
                    act.wait_ge(pe_used, value(me, n - SPLIT + 1, LOOP_UNITS))
                act.activation(w_hi[:, n % SPLIT, :], raw[:, n % RAW, :], ACT.Copy)\
                   .then_inc(hi_split, 1)

            def jobs(tag):
                for j, (src, dst, mode, g) in enumerate(JOBS[tag]):
                    if mode == "plain":
                        act.wait_ge(pe_done, me.at(f"{tag}.{j}.T"))
                        act.activation(dst[0], four(bank_of(tag, j)), ACT.Copy)\
                            .then_inc(act_done, me.done(f"{tag}.{j}.hi", f"{tag}.hi"))
                        continue
                    k = ts_turn[0] % 2
                    ts_turn[0] += 1
                    if mode == "square":
                        if ts_user[k] and me.it is None:
                            act.wait_ge(dve_done, me.at(f"{ts_user[k]}.lo"))
                        act.wait_ge(pe_done, me.at(f"{tag}.{j}.T"))
                        act.activation(ts[:, k, :], bank_of(tag, j), ACT.Square)\
                            .then_inc(act_done, me.done(f"{tag}.{j}.tmp"))
                        act.wait_ge(act_done, me.here())
                    else:
                        act.wait_ge(dve_done, me.at(f"{tag}.{j}.tmp"))
                    act.activation(dst[0], four(ts[:, k, :]), ACT.Copy)\
                        .then_inc(act_done, me.done(f"{tag}.{j}.hi", f"{tag}.hi"))
                    ts_user[k] = f"{tag}.{j}"

            def root(tag, n):
                act.wait_ge(dve_done, me.at(tag + ".inv"))
                act.activation(st_[:, 64:64 + n], st_[:, 64:64 + n], ACT.Sqrt)\
                    .then_inc(act_done, me.done(tag + ".rinv"))

            def empty(i):
                name, n, _, by = CHUNKS[i]
                if by != "act":
                    return
                act.wait_ge(pe_used, value(me, FIRST[i + 1], LOOP_UNITS))
                for t in range(NT):
                    src, func = acc[:, i % 2, t, :], ACT.Copy
                    if name == "w_f":
                        dst = f_rows[:, t, n * NW:(n + 1) * NW]
                    elif name in ("w_q", "w_k", "w_v"):
                        dst = qkv[:, ("w_q", "w_k", "w_v").index(name), t, :]
                        if n == 1 and name == "w_q" and t == 0:
                            act.wait_ge(pe_done, me.at("scan0.3.out.PE"))
                            act.wait_ge(dve_done, me.at("scan0.3.out.DVE"))
                    elif name == "w_mlp_up":
                        dst, func = hidden[:, t, (n % 2) * NW:(n % 2 + 1) * NW], ACT.Relu
                    else:
                        k, func = NT * SPILL_OF[i] + t, SPILLED[name]
                        dst = (stage_b if name.startswith("xa_w") else stage)[:, k % RAW, :]
                        if k >= RAW:
                            act.wait_ge(spill_stored[k % RAW], 16 * (k // RAW))
                    act.activation(dst, src, func).then_inc(act_emptied, 1)

            def scalars():
                act.wait_ge(pe_done, me.at("sc.proj"))
                b = bank_of("sc", 0)
                pr = b[:, 0:64].rearrange("p (t c) -> p t c", t=NT)
                act.activation(beta.rearrange("p (t c) -> p t c", t=NT), pr[:, :, 0:16], ACT.Sigmoid)\
                    .then_inc(act_done, me.done("beta"))
                act.wait_ge(dve_done, me.at("sc.xa"))
                act.activation(tmp_a, xa, ACT.Abs).then_inc(act_done, me.done())
                act.wait_ge(act_done, me.here())
                act.activation(tmp_a, tmp_a, ACT.Exp, scale=-1.0).then_inc(act_done, me.done("sc.exp"))
                act.activation(e_alog, cols["a_log"], ACT.Exp).then_inc(act_done, me.done("sc.ealog"))
                act.wait_ge(dve_done, me.at("sc.plus1"))
                act.activation(tmp_b, tmp_a, ACT.Ln).then_inc(act_done, me.done("sc.ln"))

            def decays():
                act.wait_ge(pe_done, me.at("sc.sums"))
                act.activation(e_sc, bank_of("dec", 0)[:, 0:128], ACT.Exp).then_inc(act_done, me.done("e_sc"))

            def fourier(g):
                if g >= 1:
                    act.wait_ge(pe_done, me.at(f"fourier{g}.out"))
                    act.activation(b_hi[0][:, g - 1, :], bank_of("f_out", g)[:, 0:T], ACT.Copy)\
                        .then_inc(act_done, me.done(f"fourier{g}.hi"))
                if g < 8:
                    act.wait_ge(pe_done, me.at(f"fourier{g}.time"))
                    act.activation(fp[:, g % 2, :], bank_of("f_time", g), ACT.Copy)\
                        .then_inc(act_done, me.done(f"fourier{g}.P"))

            def conv_in(half, x):
                for b in range(2):
                    act.wait_ge(pe_done, me.at(f"conv{half}{x}.T{b}"))
                    act.wait_ge(pool_done, me.at(f"pad{half}"))
                    if (half, x) != (0, 0):
                        act.wait_ge(dve_done, me.at(f"conv{half}{x - 1}.sum" if x else f"conv{half - 1}2.sum"))
                    act.activation(padT[:, 2 * b:2 * b + 2, 2:2 + T], bank_of(f"conv{half}{x}",
                        b).rearrange("p (h c) -> p h c", h=2), ACT.Copy)\
                        .then_inc(act_done, me.done(f"conv{half}{x}.pad{b}"))
                act.wait_ge(dve_done, me.at(f"conv{half}{x}.sum"))
                act.activation(flat(convT[:, :, :]), flat(convT[:, :, :]), ACT.Silu)\
                    .then_inc(act_done, me.done(f"conv{half}{x}.silu"))
                if x < 2:
                    act.wait_ge(act_done, me.here())
                    act.activation(flat(squares[:, :, :]), flat(convT[:, :, :]), ACT.Square)\
                        .then_inc(act_done, me.done(f"conv{half}{x}.sq"))

            def conv_norm(half, x):
                act.wait_ge(dve_done, me.at(f"conv{half}{x}.inv"))
                act.activation(flat(squares[:, :, :]), flat(squares[:, :, :]), ACT.Sqrt,
                    scale=1.0 / HD if x == 0 else 1.0)\
                    .then_inc(act_done, me.done(f"conv{half}{x}.rinv"))

            def conv_back(half, x):
                for t in range(NT):
                    act.wait_ge(pe_done, me.at(f"v{half}.T{t}"))
                    act.activation(v_rows[:, t].rearrange("p h c -> p (h c)"), bank_of(f"v{half}", t), ACT.Copy)\
                        .then_inc(act_done, me.done(f"v{half}.rows{t}"))

            def decay(half, t):
                for d in range(2):
                    act.wait_ge(pe_done, me.at(f"decay{half}{t}.D{d}"))
                    if (half, t) != (0, 0):
                        act.wait_ge(pool_done, me.at(f"solT{prev(half, t)}.{d}"))
                    if (half, t) == (1, 0):
                        act.wait_ge(dve_done, me.at("scan0.3.out.DVE"))
                    act.activation(EM(d), bank_of(f"decay{half}{t}", d), ACT.Exp)\
                        .then_inc(act_done, me.done(f"decay{half}{t}.E{d}"))

            def turn(half, t):
                for d in range(2):
                    act.wait_ge(pe_done, me.at(f"turn{half}{t}.M{d}"))
                    act.activation(MT(d), bank_of(f"turnM{half}{t}", d), ACT.Copy)\
                        .then_inc(act_done, me.done(f"turn{half}{t}.MT{d}"))
                for d in range(2):
                    act.wait_ge(pe_done, me.at(f"turn{half}{t}.Q{d}"))
                    act.activation(qkT[:, t, d].rearrange("p h c -> p (h c)"), bank_of(f"turnQ{half}{t}", d),
                        ACT.Copy)\
                        .then_inc(act_done, me.done(f"turn{half}{t}.QT{d}"))

            def solve_y(half, t, n):
                for d in range(2):
                    act.wait_ge(pe_done, me.at(f"solve{half}{t}{n}.Y{d}"))
                    if n == 1:
                        act.wait_ge(dve_done, me.at(f"turn{half}{t}.X{d}"))
                    act.activation(MM(d), bank_of(f"solveY{half}{t}{n}", d), ACT.Copy)\
                        .then_inc(act_done, me.done(f"solve{half}{t}{n}.Yc{d}"))

            def scan_new(half, st):
                for d in range(2):
                    c, t, rs = chunk_of(st, d)
                    act.wait_ge(pe_done, me.at(f"scan{half}.{st}.new{d}"))
                    act.activation(EB(d)[rs, :], bank_of(f"scanN{half}{st}", d)[rs, :], ACT.Copy)\
                        .then_inc(act_done, me.done(f"scan{half}.{st}.vnew{d}"))

            def ssm_small():
                T_ = lambda i: ssm_t[:, i, :]
                act.wait_ge(loaded["small"], 16)
                act.wait_ge(act_done, me.at("pre.7.hi"))
                act.activation(T_(0), cols["log_dt"], ACT.Exp).then_inc(act_done, me.done("ssm.dt"))
                act.wait_ge(dve_done, me.at("ssm.ab"))
                act.activation(T_(4), T_(1), ACT.Exp).then_inc(act_done, me.done())
                act.activation(T_(5), T_(1), ACT.Tanh, scale=0.5).then_inc(act_done, me.done())
                act.activation(T_(6), T_(3), ACT.Sin).then_inc(act_done, me.done())
                act.activation(T_(7), T_(3), ACT.Sin, scale=0.5).then_inc(act_done, me.done("ssm.sin"))

            def ssm_u():
                for j in range(4):
                    t, q = j // 2, j % 2
                    act.wait_ge(pe_done, me.at(f"uT.{j}.T"))
                    act.activation(uT[:, 4 * q:4 * q + 4, t * P:(t + 1) * P], four(bank_of("uT", j)), ACT.Copy)\
                        .then_inc(act_done, me.done(f"uT.{j}"))

            def ssm(i):
                if i >= 2 and i % 2 == 0:
                    ct = (i - 2) // 2
                    act.wait_ge(dve_done, me.at(f"ssm{i}.ysum"))
                    act.activation(uT[:, ct, :], prod_y(ct), ACT.Gelu_apprx_tanh)\
                        .then_inc(act_done, me.done(f"gelu{ct}"))

            def gelu_turn():
                act.wait_ge(act_done, me.here())
                act.wait_ge(pe_done, me.at("sg_mix.PE"))
                act.wait_ge(dve_done, me.at("sg.gated"))
                act.activation(b_hi[1][:, :, :], uT[:, :, :], ACT.Copy).then_inc(act_done, me.done("gelu.hi"))

            def turned(tag, dst, scale):
                for j in range(4):
                    t, q = j // 2, j % 2
                    act.wait_ge(pe_done, me.at(f"{tag}.{j}.T"))
                    act.activation(dst[:, 4 * q:4 * q + 4, t * P:(t + 1) * P], four(bank_of(tag, j)), ACT.Copy,
                        scale=scale)\
                        .then_inc(act_done, me.done(f"{tag}.{j}.t"))

            def xa_score(h):
                act.wait_ge(dve_done, me.at(f"xa{h}.max"))
                if h:
                    act.wait_ge(pe_done, me.at(f"xa{h - 1}.PT"))
                for t in range(NT):
                    act.activation(prob[:, t, :], bank_of("xs", h)[:, t * T:(t + 1) * T], ACT.Exp, bias=st_[:,
                        4 + t:5 + t], accum_out=st_[:, 8 + t:9 + t])\
                        .then_inc(act_done, me.done(f"xa{h}.exp"))

            def xa_prob(h):
                act.wait_ge(pe_done, me.at(f"xa{h}.PT"))
                act.activation(flat(probT[:, :, :]), bank_of("xp", h), ACT.Copy)\
                    .then_inc(act_done, me.done(f"xa{h}.pT"))

            def xa_out(h):
                act.wait_ge(pe_done, me.at(f"xa{h}.O"))
                act.activation(flat(xqT[:, 2 * h:2 * h + 2, :]), bank_of("xo_", h), ACT.Copy)\
                    .then_inc(act_done, me.done(f"xa{h}.out"))

            def glu_rest():
                act.wait_ge(dve_emptied, emptied(INDEX[("glu_w", 1)], "dve"))
                act.activation(flat(glu[:, :, :]), flat(glu[:, :, :]), ACT.Sigmoid)\
                    .then_inc(act_done, me.done("glu.sig"))

            steps = {"scalars": scalars, "decays": decays, "fourier": fourier, "conv_in": conv_in, "conv_norm": conv_norm,
                     "conv_back": conv_back, "decay": decay, "turn": turn, "solve_y": solve_y,
                     "scan_new": scan_new, "heads_norm": lambda: root("heads", 16), "heads_turn": lambda: jobs("heads"),
                     "y_turn": lambda: jobs("y"), "mlp_norm": lambda: (root("mlp", 2), jobs("mlp")),
                     "hidden": lambda p, j: jobs(f"hidden{p}.{j}"),
                     "mem_turn": lambda t: (root(f"mem{t}", 1), jobs(f"mem{t}")),
                     "final_norm": lambda: (root("final", 2), root("pre", 2), jobs("pre")),
                     "ssm_small": ssm_small, "ssm_u": ssm_u, "ssm": ssm,
                     "sg_norm": lambda: root("sgn", 2), "sg_turn": lambda: jobs("sg"), "gelu_turn": gelu_turn,
                     "xa_k": lambda: turned("km", kmT, 1.0), "xa_q": lambda: turned("xq", xqT, 1.0 / 16),
                     "xa_score": xa_score, "xa_prob": xa_prob, "xa_out": xa_out,
                     "xa_turn": lambda: jobs("xo"), "glu_rest": glu_rest, "glu_turn": lambda: jobs("glu"),
                     "merge_turn": lambda: jobs("merge")}
            act.wait_ge(loaded["level"], 16)
            act.activation(levels[:, :], level_in[:, :], ACT.Copy).then_inc(act_done, me.done("levels"))
            act.wait_ge(loaded["w_sc"], 16)
            act.activation(flat(w_sc_hi[:, :, :]), w_sc[:, :], ACT.Copy).then_inc(act_done, me.done("w_sc.hi"))
            root("x", 2)
            split(0)
            split(1)
            jobs("x")

            def slot_work(n):
                if n + SPLIT < UNITS:
                    split(n + SPLIT)
                if n in CHUNK_END:
                    empty(CHUNK_END[n])
                run_steps(me, steps, n)

            def after_loop():
                ts_user[:] = [f"hidden{NPIECE - 2}.1.0"] * 2

            drive(me, slot_work, after_loop)
            root("out", 2)

        @block.gpsimd
        def _(pool):
            me = Side("pool", pool, done, old, new)


            def pads(half):
                if half:
                    pool.wait_ge(pe_done, me.at("scan0.3.out.PE"))
                    pool.wait_ge(dve_done, me.at("scan0.3.out.DVE"))
                    pool.wait_ge(act_done, me.at("scan0.3.vnew1"))
                pool.memset(padT[:, :, 0:2], 0.0).then_inc(pool_done, me.done())
                pool.memset(padT[:, :, 258:260], 0.0).then_inc(pool_done, me.done("pad0" if half == 0 else "pad1"))

            def key_rows(half):
                pool.wait_ge(pe_done, me.at("fourier8.out"))
                pool.wait_ge(act_done, me.at("fourier7.P"))
                pool.memset(o_rows[:, :, 4 * half:4 * half + 4, :], 0.0).then_inc(pool_done, me.done(f"o_zero{half}"))

            def gram(half, t):
                pool.wait_ge(dve_done, me.at("decays.g", f"key{half}.1.0"))
                if (half, t) != (0, 0):
                    pool.wait_ge(pe_done, me.at(f"solve{prev(half, t)}5.Y1"))
                if half == 1 and t == 0:
                    pool.wait_ge(pe_done, me.at("scan0.3.out.PE"))
                for d in range(2):
                    g = g_log[:, bt(t, d, half)]
                    mask = cols["LE" if d == 0 else "GE"]
                    pool.tensor_tensor(four(RG(d)), many(mask, 4), wide(g, P), ALU.mult)\
                        .then_inc(pool_done, me.done(f"gram{half}{t}.R{d}"))

            def decay(half, t):
                for d in range(2):
                    pool.wait_ge(act_done, me.at(f"decay{half}{t}.E{d}"))
                    pool.tensor_tensor(four(EM(d)), four(EM(d)), many(cols["GE" if d == 0 else "LE"], 4), ALU.mult)\
                        .then_inc(pool_done, me.done(f"decay{half}{t}.Em{d}"))
                    pool.wait_ge(pool_done, me.here())
                    if half == 1 or t == 1:
                        pool.wait_ge(pool_done, me.at(f"solT{prev(half, t)}.{d}"))
                    pool.tensor_tensor(four(EB(d)), four(EM(d)), wide(beta[:, bt(t, d, half)], P), ALU.mult)\
                        .then_inc(pool_done, me.done(f"decay{half}{t}.Eb{d}"))

            def turn(half, t):
                for d in range(2):
                    pool.wait_ge(act_done, me.at(f"turn{half}{t}.MT{d}"))
                    pool.wait_ge(pe_done, me.at(f"decay{half}{t}.D{d}"))
                    pool.tensor_tensor(four(RG(d)), four(MT(d)), many(level[d][:, 1, :], 4), ALU.mult)\
                        .then_inc(pool_done, me.done(f"solve{half}{t}1.Mt{d}"))

            def solve_x(half, t, n):
                for d in range(2):
                    if n < len(LEVELS) - 1:
                        pool.wait_ge(pe_done, me.at(f"solve{half}{t}{n}.Y{d}"))
                        pool.tensor_tensor(four(RG(d)), four(MT(d)), many(level[d][:, n + 1, :], 4), ALU.mult)\
                            .then_inc(pool_done, me.done(f"solve{half}{t}{n + 1}.Mt{d}"))
                    else:
                        pool.wait_ge(dve_done, me.at(f"solve{half}{t}{n}.XT{d}"))
                        pool.tensor_tensor(solT[:, t, d], four(EM(d)), wide(beta[:, bt(t, d, half)], P), ALU.mult)\
                            .then_inc(pool_done, me.done(f"solT{half}{t}.{d}"))

            def scan_new(half, st):
                if st in (1, 2):
                    pool.wait_ge(pe_done, me.at(f"scan{half}.{st}.in.PE"))
                    for d in range(2):
                        c, t, rs = chunk_of(st, d)
                        pool.tensor_tensor(state[:, d], state[:, d], wide(sc[:, e_gl(c, d, half)], HD), ALU.mult)\
                            .then_inc(pool_done, me.done(f"scan{half}.{st}.decayed{d}"))

            def ssm(i):
                if i > 15:
                    return
                k, t0 = i % 2, 2 * i
                if i >= 2:
                    pool.wait_ge(dve_done, me.at(f"ssm{i - 2}.DVE"))
                if i == 0:
                    pool.wait_ge(dve_done, me.at("ssm.pow"))
                pa = [pow_a[:, z, t0:t0 + 2, :].unsqueeze(3).broadcast_to([P, 2, 16, 16]) for z in range(2)]
                pb = [pow_b[:, z, t0:t0 + 2, :].unsqueeze(2).broadcast_to([P, 2, 16, 16]) for z in range(2)]
                c_, s_ = [rot[:, k, z].rearrange("p g (a b) -> p g a b", a=16) for z in range(2)]
                x_ = ptmp[:, :].rearrange("p (g a b) -> p g a b", g=2, a=16)
                pool.wait_ge(pool_done, me.here())
                for g in range(2):
                    pool.tensor_tensor(c_[:, g], pa[0][:, g], pb[0][:, g], ALU.mult).then_inc(pool_done, me.done())
                    pool.tensor_tensor(x_[:, g], pa[1][:, g], pb[1][:, g], ALU.mult).then_inc(pool_done, me.done())
                pool.wait_ge(pool_done, me.here())
                pool.tensor_tensor(flat(rot[:, k, 0]), flat(rot[:, k, 0]), ptmp[:, :], ALU.subtract)\
                    .then_inc(pool_done, me.done())
                pool.wait_ge(pool_done, me.here())
                for g in range(2):
                    pool.tensor_tensor(s_[:, g], pa[0][:, g], pb[1][:, g], ALU.mult).then_inc(pool_done, me.done())
                    pool.tensor_tensor(x_[:, g], pa[1][:, g], pb[0][:, g], ALU.mult).then_inc(pool_done, me.done())
                pool.wait_ge(pool_done, me.here())
                pool.tensor_tensor(flat(rot[:, k, 1]), flat(rot[:, k, 1]), ptmp[:, :], ALU.add)\
                    .then_inc(pool_done, me.done(f"ssm{i}.rot"))
                me.new[f"ssm{i}.POOL"] = me.new[f"ssm{i}.rot"]
                if i % 2 == 0:
                    ct, kk = i // 2, (i // 2) % 2
                    if ct == 0:
                        pool.wait_ge(dve_done, me.at("ssm.ceff"))
                    if ct >= 2:
                        pool.wait_ge(pe_done, me.at(f"ssm{2 * ct - 2}.y"))
                    for u in range(2):
                        rs = slice(64 * u, 64 * u + 64)
                        pool.wait_ge(pool_done, me.here())
                        for z in range(2):
                            for a_ in range(4):
                                col = 160 * a_ + 16 * u
                                pool.tensor_copy(c_pad[rs, kk, z, col:col + 16], c_eff[rs, z, 4 * ct + a_, :])\
                                    .then_inc(pool_done, me.done(f"cpad{ct}"))
                    pool.wait_ge(pool_done, me.here())

            def sg_norm():
                pool.wait_ge(loaded["w_sg"], 16)
                pool.tensor_tensor(w_sg[:, :, :], w_sg[:, :, :], many(cols["causal"], 8), ALU.mult)\
                    .then_inc(pool_done, me.done("w_sg.masked"))

            def ssm_small():
                pool.wait_ge(act_done, me.at("pre.hi"))
                pool.wait_ge(dve_done, me.at("pre.lo"))
                pool.wait_ge(pe_used, end("xa_wk", 1))
                pool.wait_ge(spill_stored[3], spills_until("xa_wk", 1, 1))
                pool.wait_ge(spill_stored[2], spills_until("xa_wk", 1, 0))
                pool.memset(c_pad[:, :, :, :], 0.0).then_inc(pool_done, me.done("cpad.zero"))

            pool.wait_ge(act_done, me.at("levels"))
            pads(0)
            steps = {"conv_in": lambda half, x: pads(1) if half == 1 and x == 0 else None,
                     "key_rows": key_rows, "gram": gram, "decay": decay, "turn": turn, "solve_x": solve_x,
                     "scan_new": scan_new, "ssm": ssm, "sg_norm": sg_norm, "ssm_small": ssm_small}
            for n in range(UNITS):
                if not LOOP0 <= n < LOOP0 + LOOP_UNITS:
                    run_steps(me, steps, n)

        @block.vector
        def _(dve):
            me = Side("dve", dve, done, old, new)
            ts_user = [None, None]
            ts_turn = [0]


            def split(n):
                dve.wait_ge(hi_split, value(me, n + 1, LOOP_UNITS))
                dve.tensor_tensor(w_lo[:, n % SPLIT, :], raw[:, n % RAW, :], w_hi[:, n % SPLIT, :].bitcast(F32),
                                  ALU.subtract).then_inc(lo_split, 1)

            def jobs(tag):
                for j, (src, dst, mode, g) in enumerate(JOBS[tag]):
                    if mode == "plain":
                        dve.wait_ge(act_done, me.at(f"{tag}.{j}.hi"))
                        dve.tensor_tensor(dst[1], four(bank_of(tag, j)), dst[0].bitcast(F32), ALU.subtract)\
                            .then_inc(dve_done, me.done(f"{tag}.{j}.lo", f"{tag}.lo"))
                        continue
                    k = ts_turn[0] % 2
                    ts_turn[0] += 1
                    if mode == "gain":
                        if ts_user[k]:
                            dve.wait_ge(act_done, me.at(f"{ts_user[k]}.hi"))
                        dve.wait_ge(pe_done, me.at(f"{tag}.{j}.T"))
                        dve.tensor_tensor(four(ts[:, k, :]), four(bank_of(tag, j)), g, ALU.mult)\
                            .then_inc(dve_done, me.done(f"{tag}.{j}.tmp"))
                    dve.wait_ge(act_done, me.at(f"{tag}.{j}.hi"))
                    if mode == "gain":
                        dve.wait_ge(dve_done, me.here())
                    dve.tensor_tensor(dst[1], four(ts[:, k, :]), dst[0].bitcast(F32), ALU.subtract)\
                        .then_inc(dve_done, me.done(f"{tag}.{j}.lo", f"{tag}.lo"))
                    ts_user[k] = f"{tag}.{j}"

            def statistics(tag, rows, center=False):
                n = len(rows)
                for t, r in enumerate(rows):
                    k = r.shape[1] // NW
                    for c in range(k):
                        dve.bn_stats(st_[:, 24 * t + 6 * c:24 * t + 6 * c + 6], r[:, c * NW:(c + 1) * NW])\
                            .then_inc(dve_done, me.done())
                dve.wait_ge(dve_done, me.here())
                for t, r in enumerate(rows):
                    k = r.shape[1] // NW
                    dve.bn_aggr(st_[:, 48 + 2 * t:50 + 2 * t], st_[:, 24 * t:24 * t + 6 * k])\
                        .then_inc(dve_done, me.done())
                dve.wait_ge(dve_done, me.here())
                mv = st_[:, 48:48 + 2 * n].rearrange("p (t c) -> p t c", c=2)
                inv = st_[:, 64:64 + n].unsqueeze(2)
                if center:
                    dve.tensor_scalar(inv, mv[:, :, 1:2], EPS, None, ALU.add).then_inc(dve_done, me.done())
                else:
                    dve.tensor_tensor(inv, mv[:, :, 0:1], mv[:, :, 0:1], ALU.mult).then_inc(dve_done, me.done())
                    dve.wait_ge(dve_done, me.here())
                    dve.tensor_tensor(inv, inv, mv[:, :, 1:2], ALU.add).then_inc(dve_done, me.done())
                    dve.wait_ge(dve_done, me.here())
                    dve.tensor_scalar(inv, inv, EPS, None, ALU.add).then_inc(dve_done, me.done())
                dve.wait_ge(dve_done, me.here())
                dve.reciprocal(st_[:, 64:64 + n], st_[:, 64:64 + n]).then_inc(dve_done, me.done(tag + ".inv"))

            def scaled(tag, rows, dsts):
                dve.wait_ge(act_done, me.at(tag + ".rinv"))
                for t, (r, o) in enumerate(zip(rows, dsts)):
                    dve.tensor_scalar(o, r, st_[:, 64 + t:65 + t], None, ALU.mult)\
                        .then_inc(dve_done, me.done(f"{tag}.scaled{t}"))

            def empty(i):
                name, n, _, by = CHUNKS[i]
                if by != "dve":
                    return
                dve.wait_ge(pe_used, value(me, FIRST[i + 1], LOOP_UNITS))
                if me.it is not None or name[:10] == "w_mlp_down" or name == "w_o":
                    dve.wait_ge(dve_emptied, value(me, emptied(i, "dve") - NT, 8 * NT))
                cs = slice(n * NW, (n + 1) * NW)
                for t in range(NT):
                    src = acc[:, i % 2, t, :]
                    if name in ("w_fourier", "w_dn_up"):
                        k = n + (4 if name == "w_dn_up" else 0)
                        if t == 0:
                            dve.wait_ge(loaded[f"gate{k % 2}"], 16 * (k // 2 + 1))
                        dst = y_rows[:, t, cs] if k < 4 else gate_in[:, k % 2, t, :]
                        if k == 0 and t == 0:
                            dve.wait_ge(pe_done, me.at("scan1.3.out.PE"))
                            dve.wait_ge(act_done, me.at("scan1.3.vnew0", "scan1.3.vnew1"))
                        ins = dve.tensor_tensor(dst, src, gate_in[:, k % 2, t, :], ALU.mult)
                    elif name in ("w_o",) or name.startswith("w_mlp_down"):
                        if name == "w_o" and n == 0 and t == 0:
                            dve.wait_ge(loaded["x2"], 16)
                        ins = dve.tensor_tensor(x_rows[:, t, cs], x_rows[:, t, cs], src, ALU.add)
                    elif name == "glu_w":
                        if n == 0 and t == 0:
                            dve.wait_ge(loaded["glu_b"], 16)
                        ins = dve.tensor_tensor(glu[:, t, cs], src, glu_b[:, cs], ALU.add)
                    elif name.startswith("w_branch"):
                        k = 4 * (0, 2, 1).index(int(name[8:])) + n
                        if t == 0:
                            dve.wait_ge(loaded[f"gate{k % 2}"], 16 * (4 + k // 2 + 1))
                        if k == 0 and t == 0:
                            dve.wait_ge(pe_done, me.at("xo.T"))
                        if k < 4:
                            ins = dve.tensor_tensor(y_rows[:, t, cs], src, gate_in[:, k % 2, t, :], ALU.mult)
                        else:
                            ins = dve.tensor_tensor(gate_in[:, k % 2, t, :], src, gate_in[:, k % 2, t, :], ALU.mult)
                    else:
                        ins = dve.tensor_copy(y_rows[:, t, cs], src)
                    ins.then_inc(dve_emptied, 1)
                if name == "w_dn_up" or name.startswith("w_branch") and name != "w_branch0":
                    k = n % 2 if name == "w_dn_up" else n % 2
                    dve.wait_ge(dve_emptied, emptied(i, "dve"))
                    dve.tensor_tensor(y_rows[:, :, cs], y_rows[:, :, cs], gate_in[:, k, :, :], ALU.add)\
                        .then_inc(dve_done, me.done(f"{name}{n}.y"))
                elif name == "w_branch0":
                    new[f"{name}{n}.y"] = ("dve_emptied", emptied(i, "dve"))

            def scalars():
                dve.wait_ge(act_done, me.at("beta"))
                pr = bank_of("sc", 0)[:, 0:64].rearrange("p (t c) -> p t c", t=NT)
                x_ = lambda a_: a_.rearrange("p (t c) -> p t c", t=NT)
                dve.tensor_tensor(x_(xa), pr[:, :, 16:32], many(cols["dt_bias"], NT), ALU.add)\
                    .then_inc(dve_done, me.done("sc.xa"))
                dve.wait_ge(act_done, me.at("sc.exp"))
                dve.tensor_scalar(tmp_a, tmp_a, 1.0, None, ALU.add).then_inc(dve_done, me.done("sc.plus1"))
                dve.tensor_scalar(xa, xa, 0.0, -1.0, ALU.max, ALU.mult).then_inc(dve_done, me.done())
                dve.wait_ge(act_done, me.at("sc.ln", "sc.ealog"))
                dve.wait_ge(dve_done, me.here())
                dve.tensor_tensor(xa, xa, tmp_b, ALU.subtract).then_inc(dve_done, me.done())
                dve.wait_ge(dve_done, me.here())
                dve.tensor_tensor(x_(g_log), x_(xa), many(e_alog, NT), ALU.mult)\
                    .then_inc(dve_done, me.done("decays.g"))

            def fourier(g):
                if g >= 1:
                    dve.wait_ge(act_done, me.at(f"fourier{g}.hi"))
                    dve.tensor_tensor(b_lo[0][:, g - 1, :], bank_of("f_out", g)[:, 0:T],
                        b_hi[0][:, g - 1, :].bitcast(F32), ALU.subtract)\
                        .then_inc(dve_done, me.done(f"fourier{g}.lo"))

            def conv_in(half, x):
                dve.wait_ge(act_done, me.at(f"conv{half}{x}.pad0", f"conv{half}{x}.pad1"))
                dve.wait_ge(pool_done, me.at("pad1" if half else "pad0"))
                if (half, x) == (1, 0):
                    dve.wait_ge(pe_done, me.at("scan0.3.out.PE"))
                elif x:
                    dve.wait_ge(pe_done, me.at(f"conv{half}{x - 1}.T1"))
                    if x == 2:
                        dve.wait_ge(dve_done, me.here())
                for j in range(5):
                    for hd in range(4):
                        w = 5 * (8 * x + 4 * half + hd) + j
                        w = cols["conv_w"][:, w:w + 1]
                        u = padT[:, hd, j:j + T]
                        if j == 0:
                            dve.tensor_scalar(convT[:, hd, :], u, w, None, ALU.mult).then_inc(dve_done, me.done())
                        else:
                            dve.wait_ge(dve_done, me.count - 3)
                            dve.scalar_tensor_tensor(convT[:, hd, :], u, w, convT[:, hd, :], ALU.mult, ALU.add)\
                                .then_inc(dve_done, me.done(f"conv{half}{x}.sum"))

            def conv_norm(half, x):
                sq = flat(squares[:, :, :])
                for b in range(2):
                    dve.wait_ge(pe_done, me.at(f"norm{half}{x}.S{b}"))
                    dve.tensor_scalar(sq[:, b * NW:(b + 1) * NW], bank_of(f"norm{half}{x}", b), EPS, None, ALU.add)\
                        .then_inc(dve_done, me.done())
                dve.wait_ge(dve_done, me.here())
                dve.reciprocal(sq, sq).then_inc(dve_done, me.done(f"conv{half}{x}.inv"))
                dve.wait_ge(act_done, me.at(f"conv{half}{x}.rinv"))
                if half == 1:
                    dve.wait_ge(pe_done, me.at("scan0.3.out.PE"))
                dst = qT if x == 0 else kT
                dve.tensor_tensor(flat(dst[:, :, :]), flat(convT[:, :, :]), sq, ALU.mult)\
                    .then_inc(dve_done, me.done(f"{'qk'[x]}T{half}"))

            def key_rows(half):
                dve.wait_ge(act_done, me.at("e_sc"))
                for t in range(NT):
                    dve.wait_ge(pe_done, me.at(f"key{half}.T{t}"))
                    for d in range(2):
                        dve.tensor_tensor(k_dec[:, d, t], four(bank_of(f"key{half}", t)),
                            wide(sc[:, e_kd(t, d, half)], HD), ALU.mult)\
                            .then_inc(dve_done, me.done(f"key{half}.{t}.{d}"))

            def decay(half, t):
                for d in range(2):
                    dve.wait_ge(pool_done, me.at(f"decay{half}{t}.Eb{d}"))
                    dve.wait_ge(pe_done, me.at(f"gram{half}{t}.G", f"gram{half}{t}.Q"))
                    dve.tensor_tensor(MM(d), bank_of(f"gramG{half}{t}", 0), EB(d), ALU.mult)\
                        .then_inc(dve_done, me.done(f"decay{half}{t}.M{d}"))
                    dve.tensor_tensor(QK(d), bank_of(f"gramQ{half}{t}", 0), EM(d), ALU.mult)\
                        .then_inc(dve_done, me.done(f"decay{half}{t}.Q{d}"))

            def turn(half, t):
                dve.wait_ge(dve_done, me.here())
                for d in range(2):
                    dve.tensor_tensor(four(EB(d)), four(MM(d)), many(level[1 - d][:, 0, :], 4), ALU.mult)\
                        .then_inc(dve_done, me.done())
                    dve.wait_ge(act_done, me.at(f"turn{half}{t}.MT{d}"))
                    dve.tensor_tensor(four(EM(d)), four(MT(d)), many(level[d][:, 0, :], 4), ALU.mult)\
                        .then_inc(dve_done, me.done())
                dve.wait_ge(dve_done, me.here())
                for d in range(2):
                    dve.tensor_tensor(four(EB(d)), many(ident, 4), four(EB(d)), ALU.subtract)\
                        .then_inc(dve_done, me.done(f"turn{half}{t}.X{d}"))
                    dve.tensor_tensor(four(EM(d)), many(ident, 4), four(EM(d)), ALU.subtract)\
                        .then_inc(dve_done, me.done(f"turn{half}{t}.XT{d}"))

            def solve_x(half, t, n):
                dve.wait_ge(dve_done, me.here())
                for d in range(2):
                    dve.wait_ge(pe_done, me.at(f"solve{half}{t}{n}.ZT{d}"))
                    if n < len(LEVELS) - 1:
                        dve.wait_ge(pe_done, me.at(f"solve{half}{t}{n}.Z{d}"))
                    dve.tensor_tensor(EM(d), EM(d), bank_of(f"solveT{half}{t}{n}", d), ALU.subtract)\
                        .then_inc(dve_done, me.done(f"solve{half}{t}{n}.XT{d}"))
                    if n < len(LEVELS) - 1:
                        dve.tensor_tensor(EB(d), EB(d), bank_of(f"solveZ{half}{t}{n}", d), ALU.subtract)\
                            .then_inc(dve_done, me.done(f"solve{half}{t}{n}.X{d}"))

            def scan_in(half, st):
                if st == 0:
                    return
                for d in range(2):
                    c, t, rs = chunk_of(st, d)
                    e = wide(sc[rs, e_gc(t, d, half)], HD)
                    dve.wait_ge(pe_done, me.at(f"scan{half}.{st}.P{d}"))
                    dve.wait_ge(act_done, me.at(f"v{half}.rows{t}"))
                    dve.tensor_tensor(four(RG(d)[rs, :]), four(bank_of(f"scanP{half}{st}", d)[rs, :]), e, ALU.mult)\
                        .then_inc(dve_done, me.done())
                    dve.wait_ge(pe_done, me.at(f"scan{half}.{st}.O{d}"))
                    dve.tensor_tensor(four(EM(d)[rs, :]), four(bank_of(f"scanO{half}{st}", d)[rs, :]), e, ALU.mult)\
                        .then_inc(dve_done, me.done())
                    dve.wait_ge(dve_done, me.here())
                    dve.tensor_tensor(four(RG(d)[rs, :]), v_rows[rs, t], four(RG(d)[rs, :]), ALU.subtract)\
                        .then_inc(dve_done, me.done(f"scan{half}.{st}.r{d}"))
                    o_ = o_rows[rs, t, 4 * half:4 * half + 4, :]
                    dve.tensor_tensor(o_, o_, four(EM(d)[rs, :]), ALU.add).then_inc(dve_done, me.done())

            def scan_out(half, st):
                for d in range(2):
                    c, t, rs = chunk_of(st, d)
                    dve.wait_ge(pe_done, me.at(f"scan{half}.{st}.o2{d}"))
                    dve.wait_ge(pool_done, me.at(f"o_zero{half}"))
                    dve.wait_ge(dve_done, me.here())
                    o_ = o_rows[rs, t, 4 * half:4 * half + 4, :]
                    dve.tensor_tensor(o_, o_, four(bank_of(f"scanQ{half}{st}", d)[rs, :]), ALU.add)\
                        .then_inc(dve_done, me.done(f"scan{half}.{st}.out.DVE"))
                    if st < 3:
                        dve.wait_ge(pe_done, me.at(f"scan{half}.{st}.dS{d}"))
                        b = four(bank_of(f"scanS{half}{st}", d))
                        if st == 0:
                            if half:
                                dve.wait_ge(pe_done, me.at("scan0.3.out.PE"))
                            dve.tensor_copy(state[:, d], b).then_inc(dve_done, me.done(f"scan{half}.{st}.S{d}"))
                        else:
                            dve.wait_ge(pool_done, me.at(f"scan{half}.{st}.decayed{d}"))
                            dve.tensor_tensor(state[:, d], state[:, d], b, ALU.add)\
                                .then_inc(dve_done, me.done(f"scan{half}.{st}.S{d}"))

            def heads_norm():
                dve.wait_ge(dve_done, me.here())
                rows = lambda x: x[:, :, :, :].rearrange("p t h c -> p (t h) c")
                dve.wait_ge(pe_done, me.at("scan1.3.out.PE"))
                dve.tensor_tensor(rows(heads), rows(o_rows), rows(o_rows), ALU.mult).then_inc(dve_done, me.done())
                dve.wait_ge(dve_done, me.here())
                dve.tensor_reduce(st_[:, 64:80], rows(heads), AX.X, ALU.add).then_inc(dve_done, me.done())
                dve.wait_ge(dve_done, me.here())
                dve.tensor_scalar(st_[:, 64:80], st_[:, 64:80], 1.0 / HD, EPS, ALU.mult, ALU.add)\
                    .then_inc(dve_done, me.done())
                dve.wait_ge(dve_done, me.here())
                dve.reciprocal(st_[:, 64:80], st_[:, 64:80]).then_inc(dve_done, me.done("heads.inv"))
                dve.wait_ge(act_done, me.at("heads.rinv"))
                dve.wait_ge(loaded["z"], 32)
                dve.tensor_tensor(rows(heads), rows(o_rows), wide(st_[:, 64:80], HD), ALU.mult)\
                    .then_inc(dve_done, me.done())
                dve.wait_ge(dve_done, me.here())
                dve.tensor_tensor(rows(heads), rows(heads), rows(z_rows), ALU.mult)\
                    .then_inc(dve_done, me.done("heads.rows"))

            def mlp_norm():
                dve.wait_ge(dve_emptied, emptied(INDEX[("w_o", 3)], "dve"))
                dve.wait_ge(pe_done, me.at("y.T"))
                rows = [x_rows[:, t, :] for t in range(NT)]
                statistics("mlp", rows)
                scaled("mlp", rows, [y_rows[:, t, :] for t in range(NT)])
                jobs("mlp")

            def mem_turn(t):
                dve.wait_ge(loaded["mem"], 16 * (t + 1))
                statistics(f"mem{t}", [mem_rows[:, :]])
                scaled(f"mem{t}", [mem_rows[:, :]], [mem_rows[:, :]])
                jobs(f"mem{t}")

            def final_norm():
                dve.wait_ge(dve_emptied, emptied(INDEX[(f"w_mlp_down{NPIECE - 1}", 3)], "dve"))
                rows = [x_rows[:, t, :] for t in range(NT)]
                statistics("final", rows)
                dve.wait_ge(act_done, me.at("final.rinv"))
                dve.wait_ge(loaded["g_final"], 16)
                for t in range(NT):
                    dve.scalar_tensor_tensor(x_rows[:, t, :], x_rows[:, t, :], st_[:, 64 + t:65 + t], gain[:,
                        :], ALU.mult, ALU.mult)\
                        .then_inc(dve_done, me.done())
                dve.wait_ge(dve_done, me.here())
                statistics("pre", rows)
                scaled("pre", rows, [y_rows[:, t, :] for t in range(NT)])
                jobs("pre")

            def ssm_small():
                T_ = lambda i: ssm_t[:, i, :]


                dve.wait_ge(act_done, me.at("ssm.dt"))
                dve.wait_ge(pe_used, end("xa_wk", 1))
                re, im = T_(8), cols["a_im"]
                dve.wait_ge(dve_done, me.here())
                dve.tensor_scalar(re, cols["a_re"], -1e-4, None, ALU.min).then_inc(dve_done, me.done())
                dve.wait_ge(dve_done, me.here())
                dve.tensor_tensor(T_(1), re, T_(0), ALU.mult).then_inc(dve_done, me.done())
                dve.wait_ge(dve_done, me.here())
                dve.tensor_tensor(T_(2), im, T_(0), ALU.mult).then_inc(dve_done, me.done())
                dve.wait_ge(dve_done, me.here())
                dve.tensor_scalar(T_(9), T_(2), 1.0 / (2 * np.pi), None, ALU.mult).then_inc(dve_done, me.done())
                dve.wait_ge(dve_done, me.here())
                dve.tensor_scalar(T_(9), T_(9), MAGIC, MAGIC, ALU.add, ALU.subtract).then_inc(dve_done, me.done())
                for k, part in enumerate(TWO_PI):
                    dve.wait_ge(dve_done, me.here())
                    dve.tensor_scalar(T_(10), T_(9), part, None, ALU.mult).then_inc(dve_done, me.done())
                    dve.wait_ge(dve_done, me.here())
                    dve.tensor_tensor(T_(3), T_(2) if k == 0 else T_(3), T_(10), ALU.subtract)\
                        .then_inc(dve_done, me.done())
                dve.wait_ge(dve_done, me.here())
                dve.tensor_scalar(T_(3), T_(3), 3.1415925, -3.1415925, ALU.min, ALU.max)\
                    .then_inc(dve_done, me.done("ssm.ab"))
                dve.wait_ge(act_done, me.at("ssm.sin"))
                dve.wait_ge(dve_done, me.here())
                dve.tensor_tensor(T_(9), T_(7), T_(7), ALU.mult).then_inc(dve_done, me.done())
                dve.wait_ge(dve_done, me.here())
                dve.tensor_scalar(T_(9), T_(9), -2.0, None, ALU.mult).then_inc(dve_done, me.done())
                dve.wait_ge(dve_done, me.here())
                dve.tensor_scalar(T_(10), T_(9), 1.0, None, ALU.add).then_inc(dve_done, me.done())
                dve.wait_ge(dve_done, me.here())
                dve.tensor_scalar(T_(11), T_(4), 1.0, None, ALU.add).then_inc(dve_done, me.done())
                dve.wait_ge(dve_done, me.here())
                dve.tensor_tensor(T_(11), T_(11), T_(5), ALU.mult).then_inc(dve_done, me.done())
                dve.wait_ge(dve_done, me.here())
                dve.tensor_tensor(T_(12), T_(11), T_(10), ALU.mult).then_inc(dve_done, me.done())
                dve.wait_ge(dve_done, me.here())
                dve.tensor_tensor(T_(12), T_(12), T_(9), ALU.add).then_inc(dve_done, me.done())
                dve.wait_ge(dve_done, me.here())
                dve.tensor_tensor(T_(13), T_(4), T_(6), ALU.mult).then_inc(dve_done, me.done())
                dve.wait_ge(dve_done, me.here())
                dve.tensor_scalar(T_(14), im, -1.0, None, ALU.mult).then_inc(dve_done, me.done())
                dve.wait_ge(dve_done, me.here())
                dve.tensor_tensor(T_(14), T_(14), im, ALU.max).then_inc(dve_done, me.done())
                dve.wait_ge(dve_done, me.here())
                dve.tensor_scalar(T_(15), re, -1.0, None, ALU.mult).then_inc(dve_done, me.done())
                dve.wait_ge(dve_done, me.here())
                dve.tensor_tensor(T_(14), T_(14), T_(15), ALU.max).then_inc(dve_done, me.done())
                dve.wait_ge(dve_done, me.here())
                dve.reciprocal(T_(15), T_(14)).then_inc(dve_done, me.done())
                dve.wait_ge(dve_done, me.here())
                dve.tensor_tensor(T_(16), re, T_(15), ALU.mult).then_inc(dve_done, me.done())
                dve.wait_ge(dve_done, me.here())
                dve.tensor_tensor(T_(17), im, T_(15), ALU.mult).then_inc(dve_done, me.done())
                dve.wait_ge(dve_done, me.here())
                dve.tensor_tensor(T_(18), T_(16), T_(16), ALU.mult).then_inc(dve_done, me.done())
                dve.wait_ge(dve_done, me.here())
                dve.tensor_tensor(T_(19), T_(17), T_(17), ALU.mult).then_inc(dve_done, me.done())
                dve.wait_ge(dve_done, me.here())
                dve.tensor_tensor(T_(18), T_(18), T_(19), ALU.add).then_inc(dve_done, me.done())
                dve.wait_ge(dve_done, me.here())
                dve.reciprocal(T_(18), T_(18)).then_inc(dve_done, me.done())
                dve.wait_ge(dve_done, me.here())
                dve.tensor_tensor(T_(18), T_(18), T_(15), ALU.mult).then_inc(dve_done, me.done())
                dve.wait_ge(dve_done, me.here())
                dve.tensor_tensor(T_(19), T_(12), T_(16), ALU.mult).then_inc(dve_done, me.done())
                dve.wait_ge(dve_done, me.here())
                dve.tensor_tensor(T_(20), T_(13), T_(17), ALU.mult).then_inc(dve_done, me.done())
                dve.wait_ge(dve_done, me.here())
                dve.tensor_tensor(T_(19), T_(19), T_(20), ALU.add).then_inc(dve_done, me.done())
                dve.wait_ge(dve_done, me.here())
                dve.tensor_tensor(T_(19), T_(19), T_(18), ALU.mult).then_inc(dve_done, me.done())
                dve.wait_ge(dve_done, me.here())
                dve.tensor_tensor(T_(20), T_(13), T_(16), ALU.mult).then_inc(dve_done, me.done())
                dve.wait_ge(dve_done, me.here())
                dve.tensor_tensor(T_(21), T_(12), T_(17), ALU.mult).then_inc(dve_done, me.done())
                dve.wait_ge(dve_done, me.here())
                dve.tensor_tensor(T_(20), T_(20), T_(21), ALU.subtract).then_inc(dve_done, me.done())
                dve.wait_ge(dve_done, me.here())
                dve.tensor_tensor(T_(20), T_(20), T_(18), ALU.mult).then_inc(dve_done, me.done())
                dve.tensor_copy(rad[:, :], T_(4)).then_inc(dve_done, me.done("ssm.rad"))
                dve.wait_ge(loaded["c"], 32)
                f_ = [wide(T_(19), 16), wide(T_(20), 16)]
                dve.wait_ge(dve_done, me.here())
                dve.tensor_tensor(c_eff[:, 0], c_in[:, 0], f_[0], ALU.mult).then_inc(dve_done, me.done())
                dve.wait_ge(dve_done, me.here())
                dve.tensor_tensor(c_tmp[:, 0], c_in[:, 1], f_[1], ALU.mult).then_inc(dve_done, me.done())
                dve.wait_ge(dve_done, me.here())
                dve.tensor_tensor(c_eff[:, 1], c_in[:, 0], f_[1], ALU.mult).then_inc(dve_done, me.done())
                dve.wait_ge(dve_done, me.here())
                dve.tensor_tensor(c_tmp[:, 1], c_in[:, 1], f_[0], ALU.mult).then_inc(dve_done, me.done())
                dve.wait_ge(dve_done, me.here())
                dve.tensor_tensor(c_eff[:, 0], c_eff[:, 0], c_tmp[:, 0], ALU.subtract).then_inc(dve_done, me.done())
                dve.wait_ge(dve_done, me.here())
                dve.tensor_tensor(c_eff[:, 1], c_eff[:, 1], c_tmp[:, 1], ALU.add).then_inc(dve_done, me.done())
                dve.wait_ge(dve_done, me.here())
                dve.tensor_scalar(c_eff[:, 1], c_eff[:, 1], -1.0, None, ALU.mult)\
                    .then_inc(dve_done, me.done("ssm.ceff"))
                cur = (T_(10), T_(6))
                for tab in (pow_b, pow_a):
                    dve.memset(tab[:, 0, :, 0:1], 1.0).then_inc(dve_done, me.done())
                    dve.memset(tab[:, 1, :, 0:1], 0.0).then_inc(dve_done, me.done())
                    n = 1
                    while n < 16:
                        cw, sw = wide(cur[0], n), wide(cur[1], n)
                        x_ = scr[:, 0:32 * n].rearrange("p (g n) -> p g n", n=n)
                        dve.wait_ge(dve_done, me.here())
                        dve.tensor_tensor(tab[:, 0, :, n:2 * n], tab[:, 0, :, 0:n], cw, ALU.mult)\
                            .then_inc(dve_done, me.done())
                        dve.wait_ge(dve_done, me.here())
                        dve.tensor_tensor(x_, tab[:, 1, :, 0:n], sw, ALU.mult).then_inc(dve_done, me.done())
                        dve.wait_ge(dve_done, me.here())
                        dve.tensor_tensor(tab[:, 0, :, n:2 * n], tab[:, 0, :, n:2 * n], x_, ALU.subtract)\
                            .then_inc(dve_done, me.done())
                        dve.wait_ge(dve_done, me.here())
                        dve.tensor_tensor(tab[:, 1, :, n:2 * n], tab[:, 0, :, 0:n], sw, ALU.mult)\
                            .then_inc(dve_done, me.done())
                        dve.wait_ge(dve_done, me.here())
                        dve.tensor_tensor(x_, tab[:, 1, :, 0:n], cw, ALU.mult).then_inc(dve_done, me.done())
                        dve.wait_ge(dve_done, me.here())
                        dve.tensor_tensor(tab[:, 1, :, n:2 * n], tab[:, 1, :, n:2 * n], x_, ALU.add)\
                            .then_inc(dve_done, me.done("ssm.pow"))
                        a_, b_ = (22, 23) if n % 3 == 1 else (24, 25)
                        dve.wait_ge(dve_done, me.here())
                        dve.tensor_tensor(T_(26), cur[0], cur[0], ALU.mult).then_inc(dve_done, me.done())
                        dve.wait_ge(dve_done, me.here())
                        dve.tensor_tensor(T_(27), cur[1], cur[1], ALU.mult).then_inc(dve_done, me.done())
                        dve.wait_ge(dve_done, me.here())
                        dve.tensor_tensor(T_(28), cur[0], cur[1], ALU.mult).then_inc(dve_done, me.done())
                        dve.wait_ge(dve_done, me.here())
                        dve.tensor_tensor(T_(a_), T_(26), T_(27), ALU.subtract).then_inc(dve_done, me.done())
                        dve.wait_ge(dve_done, me.here())
                        dve.tensor_scalar(T_(b_), T_(28), 2.0, None, ALU.mult).then_inc(dve_done, me.done())
                        cur = (T_(a_), T_(b_))
                        n *= 2

            def ssm(i):
                if i <= 15:
                    k = i % 2
                    dve.wait_ge(pool_done, me.at(f"ssm{i}.rot"))
                    dve.wait_ge(dve_done, me.at("ssm.rad"))
                    pr = [prod[:, z] for z in range(4)]
                    c_, s_ = rot[:, k, 0], rot[:, k, 1]
                    bu = [bank_of(f"bu{i}", g)[:, :].rearrange("p (z t) -> p z t", z=2) for g in range(2)]
                    if i == 0:
                        dve.wait_ge(pe_done, me.at("uT.3.T"))
                        dve.wait_ge(dve_done, me.at("ssm.pow"))
                    dve.wait_ge(dve_done, me.here())
                    for g in range(2):
                        dve.wait_ge(pe_done, me.at(f"ssm{i}.bu{g}"))
                        dve.tensor_tensor(pr[0][:, g], bu[g][:, 0], c_[:, g], ALU.mult).then_inc(dve_done, me.done())
                        dve.tensor_tensor(pr[1][:, g], bu[g][:, 1], s_[:, g], ALU.mult).then_inc(dve_done, me.done())
                        dve.tensor_tensor(pr[2][:, g], bu[g][:, 1], c_[:, g], ALU.mult).then_inc(dve_done, me.done())
                        dve.tensor_tensor(pr[3][:, g], bu[g][:, 0], s_[:, g], ALU.mult).then_inc(dve_done, me.done())
                    dve.wait_ge(dve_done, me.here())
                    dve.tensor_tensor(flat(pr[0]), flat(pr[0]), flat(pr[1]), ALU.add).then_inc(dve_done, me.done())
                    dve.tensor_tensor(flat(pr[2]), flat(pr[2]), flat(pr[3]), ALU.subtract)\
                        .then_inc(dve_done, me.done())
                    dve.wait_ge(dve_done, me.here())
                    for g in range(2):
                        r_ = rad[:, 2 * i + g:2 * i + g + 1].broadcast_to([P, T])
                        for z in (0, 2):
                            dve.tensor_tensor_scan(pr[z + 1][:, g], r_, pr[z][:, g], 0.0, ALU.mult, ALU.add)\
                                .then_inc(dve_done, me.done())
                    dve.wait_ge(dve_done, me.here())
                    so = [s_out[:, k, z] for z in range(2)]
                    if i >= 2:
                        dve.wait_ge(pe_done, me.at(f"ssm{i - 1}.y"))
                    dve.tensor_tensor(flat(so[0]), flat(pr[1]), flat(c_), ALU.mult).then_inc(dve_done, me.done())
                    dve.tensor_tensor(flat(pr[0]), flat(pr[3]), flat(s_), ALU.mult).then_inc(dve_done, me.done())
                    dve.tensor_tensor(flat(so[1]), flat(pr[1]), flat(s_), ALU.mult).then_inc(dve_done, me.done())
                    dve.tensor_tensor(flat(pr[2]), flat(pr[3]), flat(c_), ALU.mult).then_inc(dve_done, me.done())
                    dve.wait_ge(dve_done, me.here())
                    dve.tensor_tensor(flat(so[0]), flat(so[0]), flat(pr[0]), ALU.subtract)\
                        .then_inc(dve_done, me.done())
                    dve.tensor_tensor(flat(so[1]), flat(so[1]), flat(pr[2]), ALU.add)\
                        .then_inc(dve_done, me.done(f"ssm{i}.DVE", f"ssm{i}.s"))
                if i >= 2 and i % 2 == 0:
                    ct = (i - 2) // 2
                    dve.wait_ge(pe_done, me.at(f"ssm{i}.y"))
                    if ct:
                        dve.wait_ge(act_done, me.at(f"gelu{ct - 1}"))
                    dve.scalar_tensor_tensor(prod_y(ct), uT[:, ct, :], cols["d"][:, ct:ct + 1],
                        bank_of(f"ssy{ct}", 0)[:, 0:T], ALU.mult, ALU.add)\
                        .then_inc(dve_done, me.done(f"ssm{i}.ysum"))

            def sg_norm():
                dve.wait_ge(loaded["av"], 32)
                rows = [av[:, t, :] for t in range(NT)]
                statistics("sgn", rows, center=True)
                dve.wait_ge(act_done, me.at("sgn.rinv"))
                dve.wait_ge(loaded["ln_gb"], 16)
                for t in range(NT):
                    dve.tensor_scalar(rows[t], rows[t], st_[:, 48 + 2 * t:49 + 2 * t], st_[:, 64 + t:65 + t],
                        ALU.subtract, ALU.mult)\
                        .then_inc(dve_done, me.done())
                dve.wait_ge(dve_done, me.here())
                dve.tensor_tensor(av[:, :, :], av[:, :, :], many(ln_gb[:, 0, :], NT), ALU.mult)\
                    .then_inc(dve_done, me.done())
                dve.wait_ge(dve_done, me.here())
                dve.tensor_tensor(av[:, :, :], av[:, :, :], many(ln_gb[:, 1, :], NT), ALU.add)\
                    .then_inc(dve_done, me.done("sg.vn"))

            def sg_mix():
                for j in range(4):
                    t, q = j // 2, j % 2
                    dve.wait_ge(pe_done, me.at(f"sg_mix.{j}"))
                    if j == 0:
                        dve.wait_ge(pe_done, me.at("sg_mix.PE"))
                    dve.tensor_tensor(four(av[:, t, q * NW:(q + 1) * NW]), four(bank_of("sgm", j)),
                        wide(cols["sg_b"][:, 4 * q:4 * q + 4], P), ALU.add)\
                        .then_inc(dve_done, me.done())
                dve.wait_ge(dve_done, me.here())
                dve.wait_ge(loaded["au"], 32)
                dve.wait_ge(loaded["ag"], 32)
                dve.tensor_tensor(flat(av[:, :, :]), flat(av[:, :, :]), flat(au[:, :, :]), ALU.mult)\
                    .then_inc(dve_done, me.done())
                dve.wait_ge(dve_done, me.here())
                dve.tensor_tensor(flat(av[:, :, :]), flat(av[:, :, :]), flat(ag[:, :, :]), ALU.mult)\
                    .then_inc(dve_done, me.done("sg.gated"))

            def gelu_turn():
                dve.wait_ge(act_done, me.at("gelu.hi"))
                dve.tensor_tensor(b_lo[1][:, :, :], uT[:, :, :], b_hi[1][:, :, :].bitcast(F32), ALU.subtract)\
                    .then_inc(dve_done, me.done("gelu.lo"))

            def xa_score(h):
                dve.wait_ge(pe_done, me.at(f"xa{h}.S"))
                dve.wait_ge(dve_done, me.here())
                if h:
                    dve.wait_ge(act_done, me.at(f"xa{h - 1}.exp"))
                dve.tensor_reduce(st_[:, 0:2], bank_of("xs", h).rearrange("p (t m) -> p t m", t=NT), AX.X, ALU.max)\
                    .then_inc(dve_done, me.done())
                dve.wait_ge(dve_done, me.here())
                dve.tensor_scalar(st_[:, 4:6], st_[:, 0:2], -1.0, None, ALU.mult)\
                    .then_inc(dve_done, me.done(f"xa{h}.max"))
                dve.wait_ge(act_done, me.at(f"xa{h}.exp"))
                dve.reciprocal(st_[:, 12:14], st_[:, 8:10]).then_inc(dve_done, me.done())
                dve.wait_ge(dve_done, me.here())
                dve.tensor_tensor(prob[:, :, :], prob[:, :, :], wide(st_[:, 12:14], T), ALU.mult)\
                    .then_inc(dve_done, me.done(f"xa{h}.prob"))

            def xa_turn():
                dve.wait_ge(act_done, me.at("xa3.out"))
                dve.wait_ge(loaded["xg"], 32)
                dve.tensor_tensor(xqT[:, :, :].rearrange("p (h t) c -> p h t c", t=NT), xqT[:, :, :].rearrange("p (h t) c -> p h t c", t=NT),
                    xg_rows[:, :, :].rearrange("p t (h c) -> p h t c", h=4), ALU.mult)\
                    .then_inc(dve_done, me.done("xo.rows"))
                jobs("xo")

            def glu_rest():
                dve.wait_ge(act_done, me.at("glu.sig"))
                for j in range(4):
                    t, q = j // 2, j % 2
                    dve.wait_ge(pe_done, me.at(f"gr.{j}.T"))
                    o = glu[:, t, q * NW:(q + 1) * NW]
                    dve.tensor_tensor(o, o, bank_of("gr", j), ALU.mult).then_inc(dve_done, me.done())

            def glu_turn():
                dve.wait_ge(dve_done, me.here())
                dve.wait_ge(loaded["bg"], 32)
                dve.tensor_tensor(flat(glu[:, :, :]), flat(glu[:, :, :]), flat(bg_rows[:, :, :]), ALU.mult)\
                    .then_inc(dve_done, me.done("glu.rows"))
                jobs("glu")

            steps = {"scalars": scalars, "fourier": fourier, "conv_in": conv_in, "conv_norm": conv_norm,
                     "key_rows": key_rows, "decay": decay, "turn": turn, "solve_x": solve_x,
                     "scan_in": scan_in, "scan_out": scan_out, "heads_norm": heads_norm,
                     "heads_turn": lambda: jobs("heads"), "y_turn": lambda: (jobs("y")), "mlp_norm": mlp_norm,
                     "hidden": lambda p, j: jobs(f"hidden{p}.{j}"), "mem_turn": mem_turn, "final_norm": final_norm,
                     "ssm_small": ssm_small, "ssm": ssm, "sg_norm": sg_norm, "sg_mix": sg_mix,
                     "sg_turn": lambda: jobs("sg"), "gelu_turn": gelu_turn, "xa_score": xa_score,
                     "xa_turn": xa_turn, "glu_rest": glu_rest, "glu_turn": glu_turn,
                     "merge_turn": lambda: jobs("merge")}
            dve.wait_ge(loaded["x"], 32)
            dve.wait_ge(loaded["small"], 16)
            rows0 = [x_rows[:, t, :] for t in range(NT)]
            statistics("x", rows0)
            scaled("x", rows0, rows0)
            jobs("x")
            dve.wait_ge(act_done, me.at("w_sc.hi"))
            dve.tensor_tensor(flat(w_sc_lo[:, :, :]), w_sc[:, :], flat(w_sc_hi[:, :, :]).bitcast(F32), ALU.subtract)\
                .then_inc(dve_done, me.done("w_sc.lo"))
            split(0)
            split(1)

            def slot_work(n):
                if n + SPLIT < UNITS:
                    split(n + SPLIT)
                if n in CHUNK_END:
                    empty(CHUNK_END[n])
                run_steps(me, steps, n)

            def after_loop():
                ts_user[:] = [f"hidden{NPIECE - 2}.1.0"] * 2

            drive(me, slot_work, after_loop)
            dve.wait_ge(dve_emptied, emptied(len(CHUNKS) - 1, "dve"))
            rows1 = [y_rows[:, t, :] for t in range(NT)]
            statistics("out", rows1)
            dve.wait_ge(act_done, me.at("out.rinv"))
            dve.wait_ge(loaded["post_g"], 16)
            for t in range(NT):
                dve.scalar_tensor_tensor(rows1[t], rows1[t], st_[:, 64 + t:65 + t], post_gain[:, :], ALU.mult,
                    ALU.mult)\
                    .then_inc(dve_done, me.done())
                dve.wait_ge(dve_done, me.here())
                dve.tensor_tensor(rows1[t], rows1[t], x_rows[:, t, :], ALU.add).then_inc(dve_done, me.done(f"out{t}"))

        @block.tensor
        def _(pe):
            me = Side("pe", pe, done, old, new)
            last_use = [None] * 4
            turn_of_banks = [0]

            def take_bank(tag, j, reader):
                i = turn_of_banks[0] % 4
                turn_of_banks[0] += 1
                new["bank"][(tag, j)] = i
                if last_use[i] and me.it is None:
                    pe.wait_ge(done[me.engine_of(last_use[i])], me.at(last_use[i]))
                last_use[i] = reader
                return bank(i)

            def operand_ready(name):
                tag = {"w_f": "x", "w_dn_up": "heads", "w_o": "y", "xa_wv": "mem1", "w2_bx": "pre",
                       "w_branch0": "sg", "w_branch2": "xo", "w_branch1": "glu", "w_out": "merge"}.get(name)
                if tag:
                    pe.wait_ge(act_done, me.at(f"{tag}.hi"))
                    pe.wait_ge(dve_done, me.at(f"{tag}.lo"))
                elif name == "w_mlp_up" and me.it is None:
                    pe.wait_ge(act_done, me.at("mlp.hi"))
                    pe.wait_ge(dve_done, me.at("mlp.lo"))
                elif name == "w_fourier":
                    pe.wait_ge(act_done, me.at("fourier8.hi"))
                    pe.wait_ge(dve_done, me.at("fourier8.lo"))
                elif name == "glu_w":
                    pe.wait_ge(act_done, me.at("gelu.hi"))
                    pe.wait_ge(dve_done, me.at("gelu.lo"))
                elif name.startswith("w_mlp_down"):
                    pe.wait_ge(act_done, me.at(f"hidden{name[10:]}.1.hi"))
                    pe.wait_ge(dve_done, me.at(f"hidden{name[10:]}.1.lo"))

            def unit(n):
                i = CHUNK_AT[n]
                name, col, units, _ = CHUNKS[i]
                u = n - FIRST[i]
                if u == 0:
                    if col == 0:
                        operand_ready(name)
                    if me.it is not None and n < LOOP0 + 8:
                        pe.wait_ge(dve_emptied,
                                   value(me, emptied(i - 2, "dve") - (NT if n == LOOP0 else 0), 8 * NT))
                    if i >= 2:
                        by = CHUNKS[i - 2][3]
                        pe.wait_ge(act_emptied if by == "act" else dve_emptied,
                                   value(me, emptied(i - 2, by), NT * (4 if by == "act" else 8)))
                pe.wait_ge(lo_split, value(me, n + 1, LOOP_UNITS))
                op = operand(name)
                for k in range(KU):
                    hi, lo = op(KU * u + k)
                    wh = w_hi[:, n % SPLIT, k * NW:(k + 1) * NW]
                    wl = w_lo[:, n % SPLIT, k * NW:(k + 1) * NW]
                    for t in range(NT):
                        tk = slice(t * P, (t + 1) * P)
                        o = acc[:, i % 2, t, :]
                        first, last = u == 0 and k == 0, u == units - 1 and k == KU - 1
                        pe.matmul(o, hi[:, tk], wh, start=first, stop=False)
                        pe.matmul(o, hi[:, tk], wl, start=False, stop=False)
                        ins = pe.matmul(o, lo[:, tk], wh, start=False, stop=last)
                ins.then_inc(pe_used, 1)

            def jobs(tag):
                for j, (src, dst, mode, g) in enumerate(JOBS[tag]):
                    b = take_bank(tag, j, f"{tag}.{j}." + ("lo" if mode == "plain" else "tmp"))
                    for q in range(4):
                        ins = pe.transpose(b[:, q * P:(q + 1) * P], src(q), ident)
                    ins.then_inc(pe_done, me.done(f"{tag}.{j}.T", f"{tag}.T"))

            def scalars():
                pe.wait_ge(act_done, me.at("w_sc.hi"))
                pe.wait_ge(dve_done, me.at("w_sc.lo"))
                b = take_bank("sc", 0, "sc.xa")
                for t in range(NT):
                    tk, o = slice(t * P, (t + 1) * P), b[:, 32 * t:32 * t + 32]
                    for k in range(KD):
                        pe.matmul(o, a_hi[:, k, tk], w_sc_hi[:, k, :], start=k == 0, stop=False)
                        pe.matmul(o, a_hi[:, k, tk], w_sc_lo[:, k, :], start=False, stop=False)
                        ins = pe.matmul(o, a_lo[:, k, tk], w_sc_hi[:, k, :], start=False, stop=k == KD - 1)
                ins.then_inc(pe_done, me.done("sc.proj"))

            def decays():
                pe.wait_ge(dve_done, me.at("decays.g"))
                b = take_bank("dec", 0, "e_sc")
                for t in range(NT):
                    g = g_log[:, 16 * t:16 * t + 16]
                    for d, (upto, rest) in enumerate((("LE", "GT"), ("GE", "LT"))):
                        gd = g[:, 8 * d:8 * d + 8]
                        for o0, m in ((0, upto), (32, rest)):
                            pe.matmul(b[:, o0 + 16 * t + 8 * d:o0 + 16 * t + 8 * d + 8], cols[m], gd, start=True, stop=True)
                    for c in range(2):
                        o0 = 64 + (2 * t + c) * 16
                        ins = pe.matmul(b[:, o0:o0 + 16], cols["chunk"][:, c * P:(c + 1) * P], g, start=True, stop=True)
                ins.then_inc(pe_done, me.done("sc.sums"))

            def fourier(g):
                if g == 0:
                    pe.wait_ge(act_emptied, emptied(INDEX[("w_f", 1)], "act"))
                    pe.wait_ge(loaded["dft"], 16)
                if g >= 1:
                    pe.wait_ge(act_done, me.at(f"fourier{g - 1}.P"))
                    b = take_bank("f_out", g, f"fourier{g}.lo")
                    x = fp[:, (g - 1) % 2, :]
                    pe.matmul(b[:, 0:T], dft[:, 1024:1152], x[:, 0:T], start=True, stop=False)
                    pe.matmul(b[:, 0:T], dft[:, 1152:1280], x[:, T:2 * T], start=False, stop=True)\
                        .then_inc(pe_done, me.done(f"fourier{g}.out"))
                if g < 8:
                    b = take_bank("f_time", g, f"fourier{g}.P")
                    for t in range(NT):
                        ins = pe.matmul(b, f_rows[:, t, g * P:(g + 1) * P], dft[:, t * NW:(t + 1) * NW],
                                        start=t == 0, stop=t == 1)
                    ins.then_inc(pe_done, me.done(f"fourier{g}.time"))

            def conv_in(half, x):
                pe.wait_ge(act_emptied, emptied(INDEX[(("w_q", "w_k", "w_v")[x], half)], "act"))
                for b_ in range(2):
                    b = take_bank(f"conv{half}{x}", b_, f"conv{half}{x}.pad{b_}")
                    for h in range(2):
                        for t in range(NT):
                            hd = 2 * b_ + h
                            ins = pe.transpose(b[:, h * T + t * P:h * T + (t + 1) * P], qkv[:, x, t, hd * P:(hd + 1) * P], ident)
                    ins.then_inc(pe_done, me.done(f"conv{half}{x}.T{b_}"))

            def conv_norm(half, x):
                pe.wait_ge(act_done, me.at(f"conv{half}{x}.sq"))
                for b_ in range(2):
                    b = take_bank(f"norm{half}{x}", b_, f"conv{half}{x}.inv")
                    pe.matmul(b, ones, flat(squares[:, 2 * b_:2 * b_ + 2, :]), start=True, stop=True)\
                        .then_inc(pe_done, me.done(f"norm{half}{x}.S{b_}"))

            def conv_back(half, x):
                pe.wait_ge(act_done, me.at(f"conv{half}{x}.silu"))
                for t in range(NT):
                    b = take_bank(f"v{half}", t, f"v{half}.rows{t}")
                    for hd in range(4):
                        ins = pe.transpose(b[:, hd * P:(hd + 1) * P], convT[:, hd, t * P:(t + 1) * P], ident)
                    ins.then_inc(pe_done, me.done(f"v{half}.T{t}"))

            def key_rows(half):
                pe.wait_ge(dve_done, me.at(f"kT{half}"))
                for t in range(NT):
                    b = take_bank(f"key{half}", t, f"key{half}.{t}.1")
                    for hd in range(4):
                        ins = pe.transpose(b[:, hd * P:(hd + 1) * P], kT[:, hd, t * P:(t + 1) * P], ident)
                    ins.then_inc(pe_done, me.done(f"key{half}.T{t}"))

            def gram(half, t):
                pe.wait_ge(dve_done, me.at(f"qT{half}", f"kT{half}"))
                for z, x in (("G", kT), ("Q", qT)):
                    b = take_bank(f"gram{z}{half}{t}", 0, f"decay{half}{t}.{'M' if z == 'G' else 'Q'}1")
                    for hd in range(4):
                        tk = slice(t * P, (t + 1) * P)
                        ins = pe.matmul(b[:, hd * P:(hd + 1) * P], x[:, hd, tk], kT[:, hd, tk], start=True, stop=True)
                    ins.then_inc(pe_done, me.done(f"gram{half}{t}.{z}"))

            def decay(half, t):
                for d in range(2):
                    pe.wait_ge(pool_done, me.at(f"gram{half}{t}.R{d}"))
                    b = take_bank(f"decay{half}{t}", d, f"decay{half}{t}.E{d}")
                    for hd in range(4):
                        ins = pe.matmul(b[:, hd * P:(hd + 1) * P], RG(d)[:, hd * P:(hd + 1) * P], cols["GT" if d == 0 else "LT"],
                                        start=True, stop=True)
                    ins.then_inc(pe_done, me.done(f"decay{half}{t}.D{d}"))

            def turn(half, t):
                for z, x, to in (("M", MM, "MT"), ("Q", QK, "QT")):
                    for d in range(2):
                        pe.wait_ge(dve_done, me.at(f"decay{half}{t}.{z}{d}"))
                        b = take_bank(f"turn{z}{half}{t}", d, f"turn{half}{t}.{to}{d}")
                        for hd in range(4):
                            ins = pe.transpose(b[:, hd * P:(hd + 1) * P], x(d)[:, hd * P:(hd + 1) * P], ident)
                        ins.then_inc(pe_done, me.done(f"turn{half}{t}.{z}{d}"))

            def four_products(b, lhs, rhs, name):
                for hd in range(4):
                    hs = slice(hd * P, (hd + 1) * P)
                    ins = pe.matmul(b[:, hs], lhs[:, hs], rhs[:, hs], start=True, stop=True)
                ins.then_inc(pe_done, me.done(name))

            def solve_y(half, t, n):
                for d in range(2):
                    before = f"turn{half}{t}.X{d}" if n == 1 else f"solve{half}{t}{n - 1}.X{d}"
                    pe.wait_ge(dve_done, me.at(before))
                    pe.wait_ge(pool_done, me.at(f"solve{half}{t}{n}.Mt{d}"))
                    b = take_bank(f"solveY{half}{t}{n}", d, f"solve{half}{t}{n}.Yc{d}")
                    four_products(b, RG(d), EB(d), f"solve{half}{t}{n}.Y{d}")

            def solve_x(half, t, n):
                for d in range(2):
                    pe.wait_ge(act_done, me.at(f"solve{half}{t}{n}.Yc{d}"))
                    pe.wait_ge(dve_done, me.at(f"turn{half}{t}.XT{d}" if n == 1 else f"solve{half}{t}{n - 1}.XT{d}"))
                    b = take_bank(f"solveT{half}{t}{n}", d, f"solve{half}{t}{n}.XT{d}")
                    four_products(b, MM(d), EM(d), f"solve{half}{t}{n}.ZT{d}")
                    if n < len(LEVELS) - 1:
                        b = take_bank(f"solveZ{half}{t}{n}", d, f"solve{half}{t}{n}.X{d}")
                        four_products(b, EM(d), MM(d), f"solve{half}{t}{n}.Z{d}")

            def rows_products(b, rs, lhs, rhs, name):
                for hd in range(4):
                    ins = pe.matmul(b[rs, hd * P:(hd + 1) * P], lhs(hd), rhs(hd), start=True, stop=True)
                ins.then_inc(pe_done, me.done(*([name] if isinstance(name, str) else name)))

            def scan_in(half, st):
                if st == 0:
                    return
                for d in range(2):
                    c, t, rs = chunk_of(st, d)
                    tk = slice(64 * c, 64 * c + 64)
                    pe.wait_ge(dve_done, me.at(f"scan{half}.{st - 1}.S{d}"))
                    b = take_bank(f"scanP{half}{st}", d, f"scan{half}.{st}.r{d}")
                    rows_products(b, rs, lambda hd: kT[:, hd, tk], lambda hd: state[:, d, hd, :], f"scan{half}.{st}.P{d}")
                    b = take_bank(f"scanO{half}{st}", d, f"scan{half}.{st}.r{d}")
                    rows_products(b, rs, lambda hd: qT[:, hd, tk], lambda hd: state[:, d, hd, :],
                                  [f"scan{half}.{st}.O{d}", f"scan{half}.{st}.in.PE"])

            def scan_new(half, st):
                for d in range(2):
                    c, t, rs = chunk_of(st, d)
                    pe.wait_ge(pool_done, me.at(f"solT{half}{t}.{d}"))
                    pe.wait_ge(act_done, me.at(f"v{half}.rows{t}"))
                    if st:
                        pe.wait_ge(dve_done, me.at(f"scan{half}.{st}.r{d}"))
                    r0 = 64 * (c % 2)
                    b = take_bank(f"scanN{half}{st}", d, f"scan{half}.{st}.vnew{d}")
                    rhs = (lambda hd: RG(d)[rs, hd * P:(hd + 1) * P]) if st else (lambda hd: v_rows[rs, t, hd, :])
                    rows_products(b, rs, lambda hd: solT[rs, t, d, hd, r0:r0 + 64], rhs, f"scan{half}.{st}.new{d}")

            def scan_out(half, st):
                for d in range(2):
                    c, t, rs = chunk_of(st, d)
                    r0 = 64 * (c % 2)
                    pe.wait_ge(act_done, me.at(f"scan{half}.{st}.vnew{d}", f"turn{half}{t}.QT{d}"))
                    pe.wait_ge(dve_done, me.at(f"key{half}.{t}.{d}"))
                    b = take_bank(f"scanQ{half}{st}", d, f"scan{half}.{st}.out.DVE")
                    v = lambda hd: EB(d)[rs, hd * P:(hd + 1) * P]
                    rows_products(b, rs, lambda hd: qkT[rs, t, d, hd, r0:r0 + 64], v, f"scan{half}.{st}.o2{d}")
                    if st < 3:
                        b = take_bank(f"scanS{half}{st}", d, f"scan{half}.{st}.S{d}")
                        rows_products(b, slice(0, P), lambda hd: k_dec[rs, d, t, hd, :], v, f"scan{half}.{st}.dS{d}")
                new[f"scan{half}.{st}.out.PE"] = ("pe", me.count)
                new[f"scan{half}.{st}.new.PE"] = ("pe", me.count)

            def turned(tag, src, readers="t"):
                for j in range(4):
                    t, q = j // 2, j % 2
                    b = take_bank(tag, j, f"{tag}.{j}.{readers}")
                    for r in range(4):
                        ins = pe.transpose(b[:, r * P:(r + 1) * P], src(t, 4 * q + r), ident)
                    ins.then_inc(pe_done, me.done(f"{tag}.{j}.T", f"{tag}.T"))

            def ssm_u():
                pe.wait_ge(loaded["u"], 32)
                for j in range(4):
                    t, q = j // 2, j % 2
                    b = take_bank("uT", j, f"uT.{j}")
                    for r in range(4):
                        k = 4 * q + r
                        ins = pe.transpose(b[:, r * P:(r + 1) * P], u_rows[:, t, k * P:(k + 1) * P], ident)
                    ins.then_inc(pe_done, me.done(f"uT.{j}.T"))

            def ssm(i):
                if i <= 15:
                    ct = i // 2
                    pe.wait_ge(loaded[f"b_pad{ct % 2}"], 16 * (ct // 2 + 1))
                    pe.wait_ge(act_done, me.at("uT.3"))
                    if ct >= 2:
                        pe.wait_ge(act_done, me.at(f"gelu{ct - 2}"))
                    for g in range(2):
                        b = take_bank(f"bu{i}", g, f"ssm{i}.DVE")
                        for z in range(2):
                            ins = pe.matmul(b[:, z * T:(z + 1) * T], b_pad[:, ct % 2, 2 * (i % 2) + g, z, :], uT[:, ct, :],
                                            start=True, stop=True)
                        ins.then_inc(pe_done, me.done(f"ssm{i}.bu{g}", f"ssm{i}.bu"))
                if i >= 1:
                    j = i - 1
                    ct = j // 2
                    pe.wait_ge(dve_done, me.at(f"ssm{j}.s"))
                    pe.wait_ge(pool_done, me.at(f"cpad{ct}"))
                    b = bank_of(f"ssy{ct}", 0)
                    if j % 2 == 0:
                        b = take_bank(f"ssy{ct}", 0, f"ssm{2 * ct + 2}.ysum")
                    for g in range(2):
                        a_ = 2 * (j % 2) + g
                        for z in range(2):
                            ins = pe.matmul(b[:, 0:T], c_pad[:, ct % 2, z, a_ * P:(a_ + 1) * P], s_out[:, j % 2, z, g, :],
                                            start=j % 2 == 0 and g == 0 and z == 0, stop=j % 2 == 1 and g == 1 and z == 1)
                    ins.then_inc(pe_done, me.done(f"ssm{i}.y"))

            def sg_mix():
                pe.wait_ge(dve_done, me.at("sg.vn"))
                pe.wait_ge(pool_done, me.at("w_sg.masked"))
                for j in range(4):
                    t, q = j // 2, j % 2
                    b = take_bank("sgm", j, "sg.gated")
                    for r in range(4):
                        g = 4 * q + r
                        ins = pe.matmul(b[:, r * P:(r + 1) * P], w_sg[:, g, :], av[:, t, g * P:(g + 1) * P], start=True, stop=True)
                    ins.then_inc(pe_done, me.done(f"sg_mix.{j}", "sg_mix.PE"))

            def xa_score(h):
                pe.wait_ge(act_done, me.at("km.3.t", "xq.3.t"))
                b = take_bank("xs", h, f"xa{h}.exp")
                for t in range(NT):
                    for k in range(2):
                        ins = pe.matmul(b[:, t * T:(t + 1) * T], xqT[:, 2 * h + k, t * P:(t + 1) * P], kmT[:, 2 * h + k, :],
                                        start=k == 0, stop=k == 1)
                ins.then_inc(pe_done, me.done(f"xa{h}.S", f"xa{h}.score"))

            def xa_prob(h):
                pe.wait_ge(dve_done, me.at(f"xa{h}.prob"))
                b = take_bank("xp", h, f"xa{h}.pT")
                for m in range(NT):
                    for t in range(NT):
                        ins = pe.transpose(b[:, m * T + t * P:m * T + (t + 1) * P], prob[:, t, m * P:(m + 1) * P], ident)
                ins.then_inc(pe_done, me.done(f"xa{h}.PT"))

            def xa_out(h):
                pe.wait_ge(act_done, me.at(f"xa{h}.pT"))
                pe.wait_ge(loaded["vm"], 32)
                b = take_bank("xo_", h, f"xa{h}.out")
                for t in range(NT):
                    for m in range(NT):
                        ins = pe.matmul(b[:, t * T:(t + 1) * T], probT[:, m, t * P:(t + 1) * P], vm[:, m, h * T:(h + 1) * T],
                                        start=m == 0, stop=m == 1)
                ins.then_inc(pe_done, me.done(f"xa{h}.O"))

            def glu_rest():
                for j in range(4):
                    t, q = j // 2, j % 2
                    b = take_bank("gr", j, "glu.rows")
                    for r in range(4):
                        ins = pe.transpose(b[:, r * P:(r + 1) * P], uT[:, 4 * q + r, t * P:(t + 1) * P], ident)
                    ins.then_inc(pe_done, me.done(f"gr.{j}.T", "gelu_rows.T"))

            def heads_turn():
                pe.wait_ge(dve_done, me.at("heads.rows"))
                jobs("heads")

            def y_turn():
                pe.wait_ge(dve_done, me.at("w_dn_up3.y"))
                jobs("y")

            def mlp_norm():
                pe.wait_ge(dve_done, me.at("mlp.scaled1"))
                jobs("mlp")

            def final_norm():
                pe.wait_ge(dve_done, me.at("pre.scaled1"))
                jobs("pre")

            def sg_turn():
                pe.wait_ge(dve_done, me.at("sg.gated"))
                jobs("sg")

            def xa_turn():
                pe.wait_ge(dve_done, me.at("xo.rows"))
                jobs("xo")

            def glu_turn():
                pe.wait_ge(dve_done, me.at("glu.rows"))
                jobs("glu")

            def merge_turn():
                pe.wait_ge(dve_done, me.at("w_branch13.y"))
                jobs("merge")

            def mem_turn(t):
                pe.wait_ge(dve_done, me.at(f"mem{t}.scaled0"))
                jobs(f"mem{t}")

            def xa_k():
                pe.wait_ge(loaded["km"], 32)
                turned("km", lambda t, k: km_rows[:, t, k * P:(k + 1) * P])

            def xa_q():
                pe.wait_ge(loaded["xq"], 32)
                turned("xq", lambda t, k: xq_rows[:, t, k * P:(k + 1) * P])

            def hidden_jobs(p, j):
                pe.wait_ge(act_emptied, value(me, emptied(INDEX[("w_mlp_up", 2 * p + j)], "act"), 4 * NT))
                jobs(f"hidden{p}.{j}")

            steps = {"scalars": scalars, "decays": decays, "fourier": fourier, "conv_in": conv_in, "conv_norm": conv_norm,
                     "conv_back": conv_back, "key_rows": key_rows, "gram": gram, "decay": decay, "turn": turn,
                     "solve_y": solve_y, "solve_x": solve_x, "scan_in": scan_in, "scan_new": scan_new,
                     "scan_out": scan_out,
                     "heads_turn": heads_turn, "y_turn": y_turn, "mlp_norm": mlp_norm, "hidden": hidden_jobs,
                     "mem_turn": mem_turn, "final_norm": final_norm, "ssm_u": ssm_u, "ssm": ssm, "sg_mix": sg_mix,
                     "sg_turn": sg_turn, "xa_k": xa_k, "xa_q": xa_q, "xa_score": xa_score, "xa_prob": xa_prob,
                     "xa_out": xa_out, "xa_turn": xa_turn, "glu_rest": glu_rest, "glu_turn": glu_turn,
                     "merge_turn": merge_turn}
            pe.wait_ge(dve_done, me.at("x.scaled1"))
            jobs("x")

            def slot_work(n):
                unit(n)
                run_steps(me, steps, n)

            def after_loop():
                last_use[:] = [f"hidden{NPIECE - 2}.1.0.hi"] * 4

            drive(me, slot_work, after_loop)


def prev(half, t):
    k = 2 * half + t - 1
    return f"{k // 2}{k % 2}"


def chunk_of(st, d):
    c = st if d == 0 else 3 - st
    return c, c // 2, slice(64 * (c % 2), 64 * (c % 2) + 64)


def stream(a):
    k, n = a.shape
    return a.reshape(k // (KU * P), KU, P, n // NW, NW).transpose(3, 0, 2, 1, 4).reshape(-1, P, UE)


def laid_out(i):
    m = {}
    w_in, w2 = i["w_in"][0], i["w_in_2"][0]
    for k, name in enumerate(("w_q", "w_k", "w_v", "w_z", "w_f")):
        m[name] = w_in[:, k * W:(k + 1) * W]
    m["w_gate_a"], m["w_gate_f"] = w_in[:, 5152:5152 + D], w_in[:, 5152 + D:5152 + 2 * D]
    m["w_dn_up"], m["w_fourier"], m["w_o"] = i["w_dn_up"][0], i["w_fourier"][0], i["w_o"][0]
    m["w_mlp_up"] = i["w_mlp_up"][0]
    for p in range(NPIECE):
        m[f"w_mlp_down{p}"] = i["w_mlp_down"][0][p * W:(p + 1) * W]
    for k, name in enumerate(("w2_au", "w2_av", "w2_ag", "w2_bx", "w2_bg", "w2_xq", "w2_xg")):
        m[name] = w2[:, k * W:(k + 1) * W]
    for k in range(3):
        m[f"w2_gate{k}"] = w2[:, 7 * W + k * D:7 * W + (k + 1) * D]
        m[f"w_branch{k}"] = i["w_branch_2"][0][k]
    m["xa_wk"], m["xa_wv"], m["glu_w"], m["w_out"] = \
        i["xa_wk_2"][0], i["xa_wv_2"][0], i["glu_w_2"][0], i["w_out_2"][0]
    units = {k: stream(v) for k, v in m.items()}
    w = np.concatenate([units[name][n * u:(n + 1) * u] for name, n, u, _ in CHUNKS])
    per_k = lambda a: a.reshape(-1, P).T
    every = lambda a: np.broadcast_to(a.reshape(1, -1), (P, a.size))
    masks, dft = mask_constants()
    state = lambda a: a[0].reshape(32, P).T
    small = {
        "g_mix": per_k(i["g_mix"][0]), "g_mlp": per_k(i["g_mlp"][0]), "pre_g": per_k(i["pre_norm_g_2"][0]),
        "mem_g": per_k(i["mem_norm_g_2"][0]), "g_head": i["g_dn_head"][0].reshape(P, 1),
        "conv_w": i["conv_w"][0].reshape(5, 24, P).transpose(2, 1, 0).reshape(P, 120),
        "a_log": every(np.concatenate([i["a_log_fwd"][0], i["a_log_bwd"][0]])),
        "dt_bias": every(np.concatenate([i["dt_bias_fwd"][0], i["dt_bias_bwd"][0]])),
        "a_re": state(i["ssm_a_re_2"]), "a_im": state(i["ssm_a_im_2"]),
        "log_dt": np.repeat(i["ssm_log_dt_2"][0].reshape(32, 2, 1), 64, axis=2).reshape(32, P).T,
        "d": per_k(i["ssm_d_2"][0].reshape(-1)), "sg_b": i["sg_b_2"][0].T}
    small.update(masks)
    b_pad = np.zeros((KW, P, 4, 2, P), np.float32)
    for z, name in enumerate(("ssm_b_re_2", "ssm_b_im_2")):
        b = i[name][0]
        for g in range(64):
            r, u = 16 * (g % 8), 64 * (g % 2)
            b_pad[g // 8, r:r + 16, g % 8 // 2, z, u:u + 64] = b[g].T
    c_rows = lambda a: a[0].transpose(0, 2, 1).reshape(32, P, 16).transpose(1, 0, 2)
    arrays = {
        "x": i["x"][0].reshape(NT, P, D), "mem": i["mem_2"][0].reshape(NT, P, D), "w": w,
        "w_sc": w_in[:, 5120:5152].reshape(KD, P, 32).transpose(1, 0, 2).reshape(P, KD * 32),
        "small": np.concatenate([small[n] for n, _ in SMALL if n[:5] != "level"], 1),
        "level": np.concatenate([small["level_f"], small["level_b"]], 1), "dft": dft,
        "b_pad": b_pad, "c_re": c_rows(i["ssm_c_re_2"]), "c_im": c_rows(i["ssm_c_im_2"]),
        "w_sg": i["sg_w_2"][0].transpose(2, 0, 1),
        "ln_gb": np.stack([every(i["sg_ln_g_2"][0]), every(i["sg_ln_b_2"][0])], 1),
        "glu_b": every(i["glu_b_2"][0]), "g_final": every(i["g_final"]), "post_g": every(i["post_norm_g_2"][0])}
    return {k: np.ascontiguousarray(v) for k, v in arrays.items()}


def program(nc, shapes, marks):
    t_in = {k: nc.dram_tensor(f"in_{k}", shape, F32, kind="ExternalInput").ap() for k, shape in shapes.items()}
    out = nc.dram_tensor("out_0", (1, T, D), F32, kind="ExternalOutput").ap()
    new = {"bank": {}}
    build(nc, t_in, out, marks, new)
    return new


def kernel(**inputs):
    import concourse.bacc as bacc
    from concourse.bass_utils import run_bass_kernel_spmd

    arrays = laid_out({k: np.asarray(v) for k, v in inputs.items()})
    marks = None
    for _ in range(2):
        nc = bacc.Bacc("TRN2", target_bir_lowering=False, num_devices=1)
        marks = program(nc, {k: a.shape for k, a in arrays.items()}, marks)
    r = run_bass_kernel_spmd(nc, [{f"in_{k}": a for k, a in arrays.items()}], core_ids=[0])
    return r.results[0]["out_0"]
```

```python
from contextlib import ExitStack

import numpy as np

import concourse.bass as bass
from concourse import mybir

F32 = mybir.dt.float32
F32R = mybir.dt.float32r
ALU = mybir.AluOpType
ACT = mybir.ActivationFunctionType
AX = mybir.AxisListType

P = 128
T = 256
NT = T // P
D = 2048
KD = D // P
W = 1024
KW = W // P
HD = 128
NW = 512
KU = 4
UE = KU * NW
RAW = 4
SPLIT = 2
EPS = 1e-6
NPIECE = 8
LEVELS = (1, 2, 4, 8, 16, 32)
MAGIC = 12582912.0
TWO_PI = (6.28125, 0.0019340515136718750, 1.2556659146e-06)


def weight_chunks():
    c = []
    add = lambda name, n0, n1, units, by: c.extend((name, n, units, by) for n in range(n0, n1))
    add("w_f", 0, 2, 4, "act")
    for half in (0, 1):
        for name in ("w_q", "w_k", "w_v"):
            add(name, half, half + 1, 4, "act")
        if half == 0:
            add("w_z", 0, 2, 4, "act")
            add("w_gate_f", 0, 3, 4, "act")
    add("w_gate_f", 3, 4, 4, "act")
    add("w_gate_a", 0, 4, 4, "act")
    add("w_fourier", 0, 4, 2, "dve")
    add("w_dn_up", 0, 4, 2, "dve")
    add("w_o", 0, 4, 4, "dve")
    add("w_mlp_up", 0, 2, 4, "act")
    for p in range(NPIECE):
        if p + 1 < NPIECE:
            add("w_mlp_up", 2 * p + 2, 2 * p + 4, 4, "act")
        c.extend((f"w_mlp_down{p}", n, 2, "dve") for n in range(4))
    add("xa_wv", 0, 2, 4, "act")
    add("xa_wk", 0, 2, 4, "act")
    for name in ("w2_bx", "w2_bg", "w2_av", "w2_au", "w2_ag", "w2_xq", "w2_xg"):
        add(name, 0, 2, 4, "act")
    for n in range(3):
        add(f"w2_gate{n}", 0, 4, 4, "act")
    add("glu_w", 0, 2, 2, "dve")
    for n in (0, 2, 1):
        add(f"w_branch{n}", 0, 4, 2, "dve")
    add("w_out", 0, 4, 4, "dve")
    return c


CHUNKS = weight_chunks()
INDEX = {(c[0], c[1]): i for i, c in enumerate(CHUNKS)}
FIRST = list(np.cumsum([0] + [c[2] for c in CHUNKS]))
FIRST = [int(f) for f in FIRST]
UNITS = FIRST[-1]
EMPTIED = [sum(1 for c in CHUNKS[:i + 1] if c[3] == by) * NT for i in range(len(CHUNKS))
           for by in ("act", "dve")]


def emptied(i, by):
    return EMPTIED[2 * i + (by == "dve")]


def end(name, n):
    return FIRST[INDEX[(name, n)] + 1]


SPILLED = {"w_z": ACT.Silu, "w_gate_f": ACT.Sigmoid, "w_gate_a": ACT.Sigmoid,
           "xa_wv": ACT.Copy, "xa_wk": ACT.Copy, "w2_bg": ACT.Silu, "w2_av": ACT.Copy,
           "w2_au": ACT.Copy, "w2_ag": ACT.Silu, "w2_xq": ACT.Copy, "w2_xg": ACT.Silu,
           "w2_bx": ACT.Copy,
           "w2_gate0": ACT.Sigmoid, "w2_gate1": ACT.Sigmoid, "w2_gate2": ACT.Sigmoid}
SPILLS = [i for i, c in enumerate(CHUNKS) if c[0] in SPILLED]
SPILL_OF = {i: k for k, i in enumerate(SPILLS)}

SMALL = [("ident", 128), ("g_mix", 16), ("ones", 128), ("LE", 128), ("GE", 128), ("GT", 128), ("LT", 128), ("causal", 128),
         ("chunk", 256), ("level_f", 768), ("level_b", 768),
         ("g_mlp", 16), ("pre_g", 16), ("mem_g", 16), ("g_final", 16), ("g_head", 1),
         ("conv_w", 120), ("a_log", 16), ("dt_bias", 16),
         ("a_re", 32), ("a_im", 32), ("log_dt", 32), ("d", 8), ("sg_b", 8)]
AT, _n = {}, 0
for _name, _w in SMALL:
    AT[_name] = (_n, _n + _w)
    _n += _w
NSMALL = _n


def mask_constants():
    r, c = np.meshgrid(np.arange(P), np.arange(P), indexing="ij")
    same = r // 64 == c // 64
    out = {"ident": r == c, "ones": r >= 0, "LE": same & (r <= c), "GE": same & (r >= c),
           "GT": same & (r > c), "LT": same & (r < c), "causal": r <= c,
           "chunk": np.concatenate([r // 64 == 0, r // 64 == 1], 1)}
    lower = [(r // (2 * s) == c // (2 * s)) & (r // s % 2 == 1) & (c // s % 2 == 0) for s in LEVELS]
    out["level_f"] = np.concatenate([m.T for m in lower], 1)
    out["level_b"] = np.concatenate(lower, 1)
    out = {k: v.astype(np.float32) for k, v in out.items()}
    t = np.arange(T)
    a = 2 * np.pi * np.outer(t, t) / T
    cs = np.concatenate([np.cos(a), np.sin(a)], 1) / np.sqrt(T)
    d = np.arange(P)
    b = 2 * np.pi * np.outer(d, d) / P
    dft = np.concatenate([cs.reshape(NT, P, 2 * T)[0], cs.reshape(NT, P, 2 * T)[1],
                          np.cos(b) / np.sqrt(P), -np.sin(b) / np.sqrt(P)], 1)
    return out, dft.astype(np.float32)


def delta_steps(half):
    s = [("conv_in", half, 2, 0), ("conv_in", half, 2, 1), ("key_rows", half), ("pause",), ("conv_back", half, 2)]
    for t in range(NT):
        s += [("gram", half, t), ("decay", half, t), ("pause",), ("turn", half, t)]
        for n in range(1, len(LEVELS)):
            s += [("solve_y", half, t, n), ("solve_x", half, t, n)]
    for st in range(4):
        s += [("scan_in", half, st), ("scan_new", half, st), ("scan_out", half, st)]
    return s


SSM_STRIDE = 3


def schedule():
    s = {}
    put_at = lambda place, *step: s.setdefault(place, []).append(step)
    put = lambda slot, *step: put_at(2 * slot + 1, *step)
    f = end("w_f", 1)
    for part in range(4):
        put_at(2 * f + 2 * part, "scalars", part)
    put(f + 4, "decays")
    for g in range(9):
        put(f + g, "fourier", g)
    for half in (0, 1):
        for x, name in enumerate(("w_q", "w_k")):
            at = 2 * end(name, half) + 1
            put_at(at, "conv_in", half, x, 0)
            put_at(at + 2, "conv_in", half, x, 1)
            put_at(at + 6, "conv_norm", half, x)
        at = end("w_v", half)
        steps = delta_steps(half)
        places = 2 * ((end("w_q", 1) - 4 if half == 0 else end("w_gate_a", 3) - 1) - at) - 1
        for i, step in enumerate(steps):
            put_at(2 * at + 1 + i * places // len(steps), *step)
    put(end("w_gate_a", 3) - 1, "load_z")
    for k in range(8):
        put(end("w_gate_a", 3) - 1 if k < 2 else end("w_fourier" if k < 6 else "w_dn_up", (k - 2) % 4) - 1,
            "load_gate", k)
    at = 2 * end("w_gate_a", 3) - 1
    for part, place in enumerate((0, 2, 4, 6)):
        put_at(at + place, "heads_norm", part)
    for j in range(4):
        put_at(at + 8 + 2 * j, "heads_in", j)
    put(end("w_dn_up", 0), "load_x")
    for n in range(4):
        if n:
            put_at(2 * n - 2, "x_in", n)
        put_at(2 * end("w_dn_up", n) + 2, "y_in", n)
        put(end("w_o", n), "mlp_in", n)
        put_at(2 * end(f"w_mlp_down{NPIECE - 1}", n) + 2, "pre_in", n)
        put_at(2 * end("w_branch1", n) + 2, "merge_in", n)
    put_at(6, "x_root")
    put_at(8, "tables")
    f = end("w_dn_up", 3)
    put(f + 1, "load_mem", 0)
    put(f + 9, "load_mem", 1)
    for t, slots in enumerate(((5, 6, 7, 9), (13, 14, 17, 18))):
        for n in range(4):
            put(f + slots[n], "mem_in", t, n)
        put(f + slots[3], "mem_root", t)
    put(end("w_o", 3) + 1, "mlp_root")
    put(end("w_mlp_up", 0), "hidden", 0, 0)
    put(end("w_mlp_up", 1) - 1, "hidden", 0, 1)
    a = end(f"w_mlp_down{NPIECE - 1}", 3)
    put(a + 1, "final_root")
    for k in range(4):
        put(a + 2 + k, "final_scale", k)
    put(a + 6, "pre_root")
    p = NPIECE - 1
    put(end(f"w_mlp_down{p}", 2) - 2, "load_g_final")
    put(end("w_mlp_up", 2 * p), "hidden", p, 0)
    put(end("w_mlp_up", 2 * p + 1), "hidden", p, 1)
    put(end("xa_wv", 1) + 2, "ssm_small", 0)
    put(end("xa_wv", 1) + 4, "ssm_small", 1)
    for part in range(2, 11):
        put_at(2 * end("xa_wk", 1) - 2 + 2 * part, "ssm_small", part)
    put(end("xa_wk", 1) - 1, "load_c")
    a = end("w2_bx", 1) + 1
    put(a - 1, "load_u")
    for ct in range(KW):
        put(a + 2 * SSM_STRIDE * ct, "load_b_pad", ct)
    put(a, "ssm_u")
    for i in range(17):
        for part, place in enumerate((0, 2, 3, 5)):
            put_at(2 * (a + 3 + SSM_STRIDE * i) + 1 + place, "ssm", i, part)
    a += 3 + SSM_STRIDE * 17
    put(a - 1, "load_gating")
    for part in range(3):
        put_at(2 * a + 1 + 2 * part, "sg_norm", part)
        put_at(2 * a + 8 + 2 * part, "sg_mix", part)
    for j in range(4):
        put_at(2 * a + 14 + 2 * j, "sg_in", j)
    put(a + 11, "gelu_turn")
    a = max(a + 12, end("w2_xg", 1) + 1)
    put(a - 1, "load_memory")
    put(a, "xa_k")
    put(a + 1, "load_xq")
    put(a + 2, "xa_q")
    for h in range(4):
        put(a + 4 + 3 * h, "xa_score", h)
        put(a + 5 + 3 * h, "xa_prob", h)
        put(a + 6 + 3 * h, "xa_out", h)
    assert a + 16 < end("w2_gate2", 3)
    put(a + 16, "load_xg")
    for k in range(12):
        j, n = (0, 2, 1)[(k - 2) // 4], (k - 2) % 4
        put(end("w2_gate2", 3) if k < 2 else end(f"w_branch{j}", n) - 1, "load_gate2", k)
    put(end("glu_w", 1), "load_bg")
    put(end("w_branch1", 0), "load_post_g")
    put(end("w2_gate2", 3) - 3, "xa_gate")
    for j in range(4):
        put(end("w2_gate2", 3) - 1 + j, "xo_in", j)
        put(end("glu_w", 1) + 4 + j, "glu_in", j)
    put(end("glu_w", 1), "glu_rest")
    put(end("glu_w", 1) + 2, "glu_gate")
    return s


SCHED = schedule()
LOOP0 = FIRST[INDEX[("w_mlp_up", 2)]]
LOOP_UNITS = 32
LOOPS = 3


class Side:

    def __init__(self, key, eng, sems, old, new):
        self.key, self.eng, self.sems, self.old, self.new = key, eng, sems, old, new
        self.count, self.it, self.per = 0, None, None

    def done(self, *names):
        self.count += 1
        for n in names:
            self.new[n] = (self.key, self.count)
        return 1

    def _in_loop(self, key, value):
        return value if self.it is None else value + self.it * self.per[key]

    def engine_of(self, name):
        return self.old[name][0] if self.old else "act"

    def at(self, *names):
        marks = [self.old[n] if self.old else ("act", 1) for n in names]
        assert len({key for key, _ in marks}) == 1, names
        return self._in_loop(marks[0][0], max(value for _, value in marks))

    def here(self):
        assert self.count > 0
        return self._in_loop(self.key, self.count)


KB = 1024


def build(nc, t_in, out, old, new):
    with ExitStack() as ctx:
        sem = lambda n: ctx.enter_context(nc.semaphore(n))
        base = -(-nc.sbuf_base // 64) * 64
        ctx.enter_context(nc.sbuf_tensor("arena", [P, 52984], F32))
        top = [0]

        def at(name, off, shape, dt=F32):
            return nc.alloc_sbuf_tensor_at(name, shape, dt, offset=base + off)

        def take(name, shape, dt=F32):
            n = int(np.prod(shape[1:])) * (2 if dt == mybir.dt.bfloat16 else 4)
            off = top[0]
            top[0] += -(-n // 64) * 64
            return at(name, off, shape, dt)

        raw = take("raw", [P, RAW, UE])
        w_hi = take("w_hi", [P, SPLIT, UE], F32R)
        w_lo = take("w_lo", [P, SPLIT, UE], F32R)
        a_hi = take("a_hi", [P, KD, T], F32R)
        a_lo = take("a_lo", [P, KD, T], F32R)
        bb = top[0]
        b_hi, b_lo = [], []
        for i in range(2):
            b_hi.append(take(f"b{i}_hi", [P, KW, T], F32R))
            b_lo.append(take(f"b{i}_lo", [P, KW, T], F32R))
        small = take("small", [P, NSMALL - 1536])
        levels = take("levels", [P, 2 * 6 * P], mybir.dt.bfloat16)
        ts = take("ts", [P, 2, NW])
        sc = take("sc", [P, 320])
        st_ = take("stats", [P, 144])
        dr = top[0]
        cols = {}
        off = 0
        for name, w in SMALL:
            if name in ("level_f", "level_b"):
                continue
            cols[name] = small[:, off:off + w]
            off += w
        ident, ones = cols["ident"], cols["ones"]
        level = [levels[:, 0:768].rearrange("p (n c) -> p n c", n=6),
                 levels[:, 768:1536].rearrange("p (n c) -> p n c", n=6)]

        def region(name, kb, shape, dt=F32):
            assert dr + kb * KB + int(np.prod(shape[1:])) * 4 <= 52984 * 4, name
            return at(name, dr + kb * KB, shape, dt)

        qT = region("qT", 0, [P, 4, T])
        kT = region("kT", 4, [P, 4, T])
        v_rows = region("v_rows", 8, [P, NT, 4, HD])
        k_dec = region("k_dec", 12, [P, 2, NT, 4, HD])
        solT = region("solT", 20, [P, NT, 2, 4, P])
        qkT = region("qkT", 28, [P, NT, 2, 4, P])
        qkv = region("qkv", 20, [P, 3, NT, NW])
        state = region("state", 36, [P, 2, 4, HD])
        o_rows = region("o_rows", 40, [P, NT, 8, HD])
        f_rows = region("f_rows", 48, [P, NT, W])
        work_c = region("work_c", 48, [P, 4, NW])
        stage = region("stage", 56, [P, 4, NW])
        gate_in = region("gate_in", 56, [P, 2, NT, NW])
        work_b = at("work_b", bb + 16 * KB, [P, 8, NW])
        dft = region("dft", 40, [P, 1280])
        fp = region("fp", 36, [P, 2, NW])
        padT = at("padT", bb + 16 * KB, [P, 4, 260])
        convT = at("convT", bb + 16 * KB + 4160, [P, 4, T])
        squares = at("squares", bb + 16 * KB + 4160 + 4096, [P, 4, T])
        scT = region("scT", 6, [P, T])
        w_sc = region("w_sc", 0, [P, KD * 32])
        w_sc_hi = region("w_sc_hi", 2, [P, KD, 32], F32R)
        w_sc_lo = region("w_sc_lo", 4, [P, KD, 32], F32R)
        level_in = at("level_in", bb + 16 * KB, [P, 1536])
        z_rows = region("z_rows", 16, [P, NT, 8, HD])
        heads = region("heads", 24, [P, NT, 8, HD])
        y_rows = region("y_rows", 0, [P, NT, D])
        x_rows = region("x_rows", 16, [P, NT, D])
        hidden = region("hidden", 0, [P, NT, W])
        mem_rows = region("mem_rows", 8, [P, D])
        m_hi = region("m_hi", 32, [P, KD, T], F32R)
        m_lo = region("m_lo", 48, [P, KD, T], F32R)
        stage_b = at("stage_b", bb, [P, 4, NW])
        gain = at("gain", bb + 8 * KB, [P, D])
        post_gain = region("post_gain", 40, [P, D])
        b_pad = at("b_pad", bb, [P, 2, 4, 2, P])
        c_pad = at("c_pad", bb + 8 * KB, [P, 2, 2, 640])
        rot = at("rot", bb + 18 * KB, [P, 2, 2, 2, T])
        ssm_t = at("ssm_t", bb + 26 * KB, [P, 40, 32])
        s_out = region("s_out", 0, [P, 2, 2, 2, T])
        prod = region("prod", 8, [P, 4, 2, T])
        c_in = region("c_in", 8, [P, 2, 32, 16])
        c_tmp = region("c_tmp", 12, [P, 2, 32, 16])
        pow_a = region("pow_a", 32, [P, 2, 32, 16])
        pow_b = region("pow_b", 36, [P, 2, 32, 16])
        c_eff = region("c_eff", 40, [P, 2, 32, 16])
        rad = region("rad", 44, [P, 32])
        u_rows = region("u_rows", 0, [P, NT, W])
        uT = region("uT", 48, [P, KW, T])
        av = region("av", 0, [P, NT, W])
        au = region("au", 8, [P, NT, W])
        ag = at("ag", bb + 16 * KB, [P, NT, W])
        ln_gb = at("ln_gb", bb + 24 * KB, [P, 2, W])
        w_sg = region("w_sg", 32, [P, 8, P])
        km_rows = region("km_rows", 8, [P, NT, W])
        kmT = region("kmT", 0, [P, KW, T])
        vm = region("vm", 40, [P, NT, W])
        xq_rows = region("xq_rows", 8, [P, NT, W])
        xqT = region("xqT", 32, [P, KW, T])
        prob = region("prob", 8, [P, NT, T])
        probT = region("probT", 10, [P, NT, T])
        xg_rows = region("xg_rows", 8, [P, NT, W])
        glu_b = region("glu_b", 0, [P, W])
        glu = region("glu", 40, [P, NT, W])
        bg_rows = region("bg_rows", 48, [P, NT, W])
        acc = ctx.enter_context(nc.psum_tensor("acc", [P, 2, NT, NW], F32))
        banks = ctx.enter_context(nc.psum_tensor("banks", [P, 4, NW], F32))
        spilled = nc.dram_tensor("spilled", [len(SPILLS), NT, P, NW], F32).ap()

        act_done, dve_done, pool_done, pe_done = (sem(f"{e}_done") for e in ("act", "dve", "pool", "pe"))
        done = {"act": act_done, "dve": dve_done, "pool": pool_done, "pe": pe_done}
        landed = [sem(f"landed{i}") for i in range(RAW)]
        hi_split, lo_split = sem("hi_split"), sem("lo_split")
        pe_used = sem("pe_used")
        act_emptied, dve_emptied = sem("act_emptied"), sem("dve_emptied")
        spill_stored = [sem(f"spill_stored{i}") for i in range(RAW)]
        out_stored = sem("out_stored")
        loaded = {n: sem(f"loaded_{n}") for n in (
            "x_0", "x_1", "x_2", "x_3", "small", "rest", "w_sc", "level", "dft", "z", "gate0", "gate1", "x2", "mem", "g_final", "c",
            "u", "b_pad0", "b_pad1", "av", "au", "ag", "ln_gb", "w_sg", "km", "vm", "xq", "xg",
            "glu_b", "bg", "post_g")}

        beta, g_log, e_sc = sc[:, 0:32], sc[:, 32:64], sc[:, 64:192]
        xa, tmp_a, tmp_b, e_alog = sc[:, 192:224], sc[:, 224:256], sc[:, 256:288], sc[:, 288:304]
        e_gc = lambda t, d, half: slice(64 + t * 16 + d * 8 + 4 * half, 68 + t * 16 + d * 8 + 4 * half)
        e_kd = lambda t, d, half: slice(96 + t * 16 + d * 8 + 4 * half, 100 + t * 16 + d * 8 + 4 * half)
        e_gl = lambda c, d, half: slice(128 + c * 16 + d * 8 + 4 * half, 132 + c * 16 + d * 8 + 4 * half)
        bt = lambda t, d, half: slice(t * 16 + d * 8 + 4 * half, t * 16 + d * 8 + 4 * half + 4)

        def wide(ap, m):
            return ap.unsqueeze(2).broadcast_to([ap.shape[0], ap.shape[1], m])

        def many(ap, n):
            return ap.unsqueeze(1).broadcast_to([ap.shape[0], n, ap.shape[1]])

        def four(ap):
            return ap.rearrange("p (h c) -> p h c", h=4)

        def flat(ap):
            return ap.rearrange("p a b -> p (a b)")

        BANK_OF = old["bank"] if old else {}
        bank_of = lambda tag, j: banks[:, BANK_OF.get((tag, j), 0), :]
        prod_y = lambda ct: ts[:, ct % 2, 0:T]
        ptmp = region("ptmp", 45, [P, 2 * T])
        scr = region("scr", 47, [P, 256])

        wb = [work_b[:, i, :] for i in range(8)] + [work_c[:, i, :] for i in range(4)]
        RG, EM, EB, MM = (lambda d: wb[d]), (lambda d: wb[2 + d]), (lambda d: wb[4 + d]), (lambda d: wb[6 + d])
        QK, MT = (lambda d: wb[8 + d]), (lambda d: wb[10 + d])
        bank = lambda i: banks[:, i, :]

        def b_dst(kt, t, parts=(b_hi, b_lo)):
            return [x[kt // KW][:, kt % KW:kt % KW + 4, t * P:(t + 1) * P] for x in parts]

        def a_dst(kt, t):
            return [x[:, kt:kt + 4, t * P:(t + 1) * P] for x in (a_hi, a_lo)]

        def rows_src(rows, t, kt):
            return lambda q: rows[:, t, (kt + q) * P:(kt + q + 1) * P]

        def wide_jobs(rows, dst, mode, gains=None, ts_=range(NT), kts=KD):
            return [(rows_src(rows, t, kt), dst(kt, t), mode, gains and wide(gains[:, kt:kt + 4], P))
                    for kt in range(0, kts, 4) for t in ts_]

        RMS = {"x": 80, "mlp": 82, "pre": 84, "mem": 86, "final": 88, "out": 90}
        rms = lambda tag, t: st_[:, RMS[tag] + t:RMS[tag] + t + 1]
        pre_gain = st_[:, 124:140]

        A_FREE = {"heads": end("w_gate_a", 3), "mlp": end("w_dn_up", 3), "pre": end("w_mlp_up", 2 * NPIECE - 1)}

        JOBS = {
            "x": wide_jobs(x_rows, a_dst, "gain", cols["g_mix"]),
            "heads": [((lambda t, kt: lambda q: heads[:, t, kt + q, :])(t, kt), a_dst(kt, t), "gain",
                       cols["g_head"].unsqueeze(2).broadcast_to([P, 4, P]))
                      for t in range(NT) for kt in (0, 4)],
            "y": wide_jobs(y_rows, b_dst, "plain"),
            "mlp": wide_jobs(x_rows, a_dst, "gain", cols["g_mlp"]),
            "pre": wide_jobs(x_rows, a_dst, "gain", pre_gain),
            "sg": wide_jobs(av, b_dst, "plain", kts=KW),
            "glu": wide_jobs(glu, lambda kt, t: a_dst(KW + kt, t), "plain", kts=KW),
            "xo": [((lambda t, kt: lambda q: xqT[:, 2 * ((kt + q) // 2) + t, (q % 2) * P:(q % 2 + 1) * P])(t, kt),
                    a_dst(kt, t), "plain", None) for t in range(NT) for kt in (0, 4)],
            "merge": wide_jobs(y_rows, b_dst, "plain"),
        }
        for t in range(NT):
            JOBS[f"mem{t}"] = [
                ((lambda kt: lambda q: mem_rows[:, (kt + q) * P:(kt + q + 1) * P])(kt),
                 [x[:, kt:kt + 4, t * P:(t + 1) * P] for x in (m_hi, m_lo)], "gain",
                 wide(cols["mem_g"][:, kt:kt + 4], P)) for kt in range(0, KD, 4)]
        for p in range(NPIECE):
            for j in range(2):
                JOBS[f"hidden{p}.{j}"] = [
                    (rows_src(hidden, t, 4 * j), b_dst(KW * (p % 2) + 4 * j, t), "square", None)
                    for t in range(NT)]

        def operand(name):
            if name in ("w_o", "w_out"):
                return lambda k: (b_hi[k // KW][:, k % KW, :], b_lo[k // KW][:, k % KW, :])
            if name in ("w_fourier", "w_branch0"):
                return lambda k: (b_hi[0][:, k, :], b_lo[0][:, k, :])
            if name in ("glu_w",):
                return lambda k: (b_hi[1][:, k, :], b_lo[1][:, k, :])
            if name.startswith("w_mlp_down"):
                i = int(name[10:]) % 2
                return lambda k: (b_hi[i][:, k, :], b_lo[i][:, k, :])
            if name.startswith("xa_w"):
                return lambda k: (m_hi[:, k, :], m_lo[:, k, :])
            first = KW if name == "w_branch1" else 0
            return lambda k: (a_hi[:, first + k, :], a_lo[:, first + k, :])

        spill = lambda name, n: spilled[SPILL_OF[INDEX[(name, n)]]].rearrange("t p n -> p t n")
        spills_until = lambda name, n, t: 16 * ((NT * SPILL_OF[INDEX[(name, n)]] + t) // RAW + 1)

        block = ctx.enter_context(nc.Block())

        def value(me, static, per):
            return static if me.it is None else static + me.it * per

        def drive(me, slot_work, after_loop):
            n = 0
            while n < UNITS:
                if n == LOOP0:
                    start = me.count
                    me.per = {k: v for k, v in (old or {}).get("per", {}).items()} if old else \
                        {"act": 0, "dve": 0, "pe": 0, "pool": 0}
                    with me.eng.Fori(0, LOOPS) as it:
                        me.it = it
                        for m in range(LOOP_UNITS):
                            slot_work(n + m)
                    me.it = None
                    per = me.count - start
                    new.setdefault("per", {})[me.key] = per
                    me.count += per * (LOOPS - 1)
                    for j in range(2):
                        for key, x in (("act", "hi"), ("dve", "lo")):
                            if me.key == key:
                                new[f"hidden{NPIECE - 2}.{j}.{x}"] = (key, me.count)
                                for k in range(NT):
                                    new[f"hidden{NPIECE - 2}.{j}.{k}.{x}"] = (key, me.count)
                    after_loop()
                    n += LOOPS * LOOP_UNITS
                    continue
                slot_work(n)
                n += 1

        def run_steps(me, steps, place):
            if 2 * LOOP0 <= place < 2 * (LOOP0 + LOOP_UNITS):
                local = (place - 2 * LOOP0 - 1) / 2
                for s, piece, j in ((4, 1, 0), (8, 1, 1), (20, 2, 0), (24, 2, 1)):
                    if local == s:
                        steps["hidden"](piece, j)
                return
            for step in SCHED.get(place, []):
                if step[0] in steps:
                    steps[step[0]](*step[1:])

        CHUNK_END = {FIRST[i + 1] - 1: i for i in range(len(CHUNKS))}
        CHUNK_AT = {}
        for i in range(len(CHUNKS)):
            for u in range(CHUNKS[i][2]):
                CHUNK_AT[FIRST[i] + u] = i

        @block.sync
        def _(sp):
            me = Side("sp", sp, done, old, new)

            def weight(n, it=None):
                if n >= RAW:
                    value = n - RAW + 1
                    sp.wait_ge(lo_split, value if it is None else value + it * LOOP_UNITS)
                if it is None:
                    src = t_in["w"][n]
                else:
                    src = t_in["w"][bass.ds(n + it * LOOP_UNITS, 1)].rearrange("a p n -> (a p) n")
                sp.dma_start(raw[:, n % RAW, :], src).then_inc(landed[n % RAW], 16)

            def load(dst, src, landing):
                sp.dma_start(dst, src).then_inc(landing, 16)

            def load_spilled(dst, matrix, n, landing):
                for t in range(NT):
                    k = (NT * SPILL_OF[INDEX[(matrix, n)]] + t) % RAW
                    sp.wait_ge(spill_stored[k], spills_until(matrix, n, t))
                sp.dma_start(dst, spill(matrix, n)).then_inc(landing, 16)

            def load_rows(dst, matrix, landing):
                for n in range(2):
                    load_spilled(dst[:, :, n * NW:(n + 1) * NW], matrix, n, landing)

            def load_z():
                sp.wait_ge(pe_done, me.at("scan1.3.out.PE"))
                sp.wait_ge(dve_done, me.at("scan1.3.out.DVE"))
                load_rows(z_rows[:, :, :, :].rearrange("p t h c -> p t (h c)"), "w_z", loaded["z"])

            def load_gate(k):
                m = "w_gate_f" if k < 4 else "w_gate_a"
                if k < 2:
                    for n in (2, 3):
                        for t in range(NT):
                            sp.wait_ge(spill_stored[(2 * n + t) % RAW], spills_until("w_gate_a", n, t))
                elif k < 6:
                    sp.wait_ge(dve_emptied, emptied(INDEX[("w_fourier", k - 2)], "dve"))
                else:
                    sp.wait_ge(dve_done, me.at(f"w_dn_up{k - 6}.y"))
                load_spilled(gate_in[:, k % 2], m, k % 4, loaded[f"gate{k % 2}"])

            def load_x():
                sp.wait_ge(act_done, me.at("heads.hi"))
                sp.wait_ge(dve_done, me.at("heads.lo"))
                load(x_rows[:, :, :], t_in["x"].rearrange("t p n -> p t n"), loaded["x2"])

            def load_mem(t):
                if t == 0:
                    sp.wait_ge(pe_done, me.at("y.T"))
                else:
                    sp.wait_ge(pe_done, me.at("mem0.T"))
                    sp.wait_ge(dve_done, me.at("mem0.inv"))
                load(mem_rows[:, :], t_in["mem"][t], loaded["mem"])

            def load_g_final():
                sp.wait_ge(pe_used, end(f"w_mlp_down{NPIECE - 2}", 3))
                load(gain[:, :], t_in["g_final"], loaded["g_final"])

            def load_c():
                sp.wait_ge(pe_done, me.at("pre.T"))
                load(c_in[:, 0], t_in["c_re"], loaded["c"])
                load(c_in[:, 1], t_in["c_im"], loaded["c"])

            def load_u():
                sp.wait_ge(pe_done, me.at("pre.T"))
                load_rows(u_rows, "w2_bx", loaded["u"])

            def load_b_pad(ct):
                if ct >= 2:
                    sp.wait_ge(pe_done, me.at(f"ssm{2 * ct - 3}.bu"))
                else:
                    for t in range(NT):
                        sp.wait_ge(spill_stored[2 + t], spills_until("xa_wk", 1, t))
                load(b_pad[:, ct % 2], t_in["b_pad"][ct], loaded[f"b_pad{ct % 2}"])

            def load_gating():
                sp.wait_ge(pe_done, me.at("ssm16.y"))
                sp.wait_ge(dve_done, me.at("ssm15.DVE"))
                sp.wait_ge(pool_done, me.at("ssm15.POOL"))
                load_rows(av, "w2_av", loaded["av"])
                load_rows(au, "w2_au", loaded["au"])
                load_rows(ag, "w2_ag", loaded["ag"])
                load(ln_gb[:, :, :], t_in["ln_gb"], loaded["ln_gb"])
                load(w_sg[:, :, :], t_in["w_sg"], loaded["w_sg"])

            def load_memory():
                sp.wait_ge(act_done, me.at("sg.hi"))
                sp.wait_ge(dve_done, me.at("sg.lo"))
                load_rows(km_rows, "xa_wk", loaded["km"])
                load_rows(vm, "xa_wv", loaded["vm"])

            def load_xq():
                sp.wait_ge(pe_done, me.at("km.T"))
                load_rows(xq_rows, "w2_xq", loaded["xq"])

            def load_xg():
                sp.wait_ge(act_done, me.at("xa3.out"))
                sp.wait_ge(pe_done, me.at("xa3.score"))
                load_rows(xg_rows, "w2_xg", loaded["xg"])
                load(glu_b[:, :], t_in["glu_b"], loaded["glu_b"])

            def load_gate2(k):
                j, n = (0, 2, 1)[k // 4], k % 4
                if k < 2:
                    for c in (2, 3):
                        for t in range(NT):
                            sp.wait_ge(spill_stored[(2 * c + t) % RAW], spills_until("w2_gate2", c, t))
                elif k < 6:
                    sp.wait_ge(dve_emptied, emptied(INDEX[("w_branch0", k - 2)], "dve"))
                else:
                    sp.wait_ge(dve_done, me.at(f"w_branch{(0, 2, 1)[(k - 2) // 4]}{(k - 2) % 4}.y"))
                load_spilled(gate_in[:, k % 2], f"w2_gate{j}", n, loaded[f"gate{k % 2}"])

            def load_bg():
                sp.wait_ge(pe_done, me.at("gelu_rows.T"))
                load_rows(bg_rows, "w2_bg", loaded["bg"])

            def load_post_g():
                sp.wait_ge(pe_done, me.at("glu.T"))
                load(post_gain[:, :], t_in["post_g"], loaded["post_g"])

            def store(i):
                k = SPILL_OF[i]
                for t in range(NT):
                    sp.wait_ge(act_emptied, emptied(i, "act") - NT + t + 1)
                    b = (NT * k + t) % RAW
                    src = stage_b if CHUNKS[i][0].startswith("xa_w") else stage
                    sp.dma_start(spilled[k, t], src[:, b, :]).then_inc(spill_stored[b], 16)

            steps = {"load_z": load_z, "load_gate": load_gate, "load_x": load_x, "load_mem": load_mem,
                     "load_g_final": load_g_final, "load_c": load_c, "load_u": load_u,
                     "load_b_pad": load_b_pad, "load_gating": load_gating, "load_memory": load_memory,
                     "load_xq": load_xq, "load_xg": load_xg, "load_gate2": load_gate2,
                     "load_bg": load_bg, "load_post_g": load_post_g}
            for n in range(KU):
                load(x_rows[:, :, n * NW:(n + 1) * NW],
                     t_in["x"].rearrange("t p n -> p t n")[:, :, n * NW:(n + 1) * NW], loaded[f"x_{n}"])
                if n == 0:
                    load(small[:, 0:P + KD], t_in["small"][:, 0:P + KD], loaded["small"])
                weight(n)
            load(small[:, P + KD:], t_in["small"][:, P + KD:], loaded["rest"])
            load(w_sc[:, :], t_in["w_sc"], loaded["w_sc"])
            load(dft[:, :], t_in["dft"], loaded["dft"])
            load(level_in[:, :], t_in["level"], loaded["level"])
            ends = {FIRST[i + 1] - 1: i for i in SPILLS}
            n = 0
            while n < UNITS:
                if n == LOOP0:
                    with sp.Fori(0, LOOPS) as it:
                        for m in range(LOOP_UNITS):
                            weight(n + m + RAW, it)
                    n += LOOPS * LOOP_UNITS
                    continue
                if n + RAW < UNITS:
                    weight(n + RAW)
                if n in ends:
                    store(ends[n])
                run_steps(me, steps, 2 * n)
                run_steps(me, steps, 2 * n + 1)
                n += 1
            for t in range(NT):
                for h in range(2):
                    sp.wait_ge(dve_done, me.at(f"out{t}{h}"))
                    sp.dma_start(out[0, t * P:(t + 1) * P, h * W:(h + 1) * W], y_rows[:, t, h * W:(h + 1) * W])\
                        .then_inc(out_stored, 16)
            sp.wait_ge(out_stored, 16 * 2 * NT)

        @block.scalar
        def _(act):
            me = Side("act", act, done, old, new)
            ts_user = [None, None]
            ts_turn = [0]

            def split(n):
                act.wait_ge(landed[n % RAW], value(me, 16 * (n // RAW + 1), 16 * LOOP_UNITS // RAW))
                if n >= SPLIT:
                    act.wait_ge(pe_used, value(me, n - SPLIT + 1, LOOP_UNITS))
                act.activation(w_hi[:, n % SPLIT, :], raw[:, n % RAW, :], ACT.Copy)\
                   .then_inc(hi_split, 1)

            def job(tag, j):
                src, dst, mode, g = JOBS[tag][j]
                if mode == "plain":
                    act.wait_ge(pe_done, me.at(f"{tag}.{j}.T"))
                    act.activation(dst[0], four(bank_of(tag, j)), ACT.Copy)\
                        .then_inc(act_done, me.done(f"{tag}.{j}.hi", f"{tag}.hi"))
                    return
                k = ts_turn[0] % 2
                ts_turn[0] += 1
                if mode == "square":
                    if ts_user[k] and me.it is None:
                        act.wait_ge(dve_done, me.at(f"{ts_user[k]}.lo"))
                    act.wait_ge(pe_done, me.at(f"{tag}.{j}.T"))
                    act.activation(ts[:, k, :], bank_of(tag, j), ACT.Square)\
                        .then_inc(act_done, me.done(f"{tag}.{j}.tmp"))
                    act.wait_ge(act_done, me.here())
                else:
                    act.wait_ge(dve_done, me.at(f"{tag}.{j}.tmp"))
                act.activation(dst[0], four(ts[:, k, :]), ACT.Copy)\
                    .then_inc(act_done, me.done(f"{tag}.{j}.hi", f"{tag}.hi"))
                ts_user[k] = f"{tag}.{j}"

            def jobs(tag):
                for j in range(len(JOBS[tag])):
                    job(tag, j)

            def rows_in(tag, n):
                if tag in A_FREE:
                    act.wait_ge(pe_used, A_FREE[tag])
                job(tag, 2 * n)
                job(tag, 2 * n + 1)

            def heads_in(j):
                act.wait_ge(pe_used, A_FREE["heads"])
                job("heads", j)

            def root(tag, c, n):
                act.wait_ge(dve_done, me.at(tag + ".inv"))
                act.activation(st_[:, c:c + n], st_[:, c:c + n], ACT.Sqrt)\
                    .then_inc(act_done, me.done(tag + ".rinv"))

            def empty(i):
                name, n, _, by = CHUNKS[i]
                if by != "act":
                    return
                act.wait_ge(pe_used, value(me, FIRST[i + 1], LOOP_UNITS))
                norm = "x" if i <= INDEX[("w_gate_a", 3)] else "mlp" if name == "w_mlp_up" else \
                    "mem" if name.startswith("xa_w") else "pre"
                if n == 0 and me.it is None:
                    ready = {"w_f": "x.rinv", "w_mlp_up": "mlp.rinv", "xa_wv": "mem1.rinv"}.get(name)
                    if ready:
                        act.wait_ge(act_done, me.at(ready))
                    elif name == "w2_bx":
                        act.wait_ge(dve_done, me.at("pre.scale"))
                for t in range(NT):
                    src, func = acc[:, i % 2, t, :], ACT.Copy
                    if name == "w_f":
                        dst = f_rows[:, t, n * NW:(n + 1) * NW]
                    elif name in ("w_q", "w_k", "w_v"):
                        dst = qkv[:, ("w_q", "w_k", "w_v").index(name), t, :]
                        if n == 1 and name == "w_q" and t == 0:
                            act.wait_ge(pe_done, me.at("scan0.3.out.PE"))
                            act.wait_ge(dve_done, me.at("scan0.3.out.DVE"))
                    elif name == "w_mlp_up":
                        dst, func = hidden[:, t, (n % 2) * NW:(n % 2 + 1) * NW], ACT.Relu
                    else:
                        k, func = NT * SPILL_OF[i] + t, SPILLED[name]
                        dst = (stage_b if name.startswith("xa_w") else stage)[:, k % RAW, :]
                        if k >= RAW:
                            act.wait_ge(spill_stored[k % RAW], 16 * (k // RAW))
                    act.activation(dst, src, func, scale=rms(norm, t)).then_inc(act_emptied, 1)

            def tables():
                act.wait_ge(loaded["rest"], 16)
                act.wait_ge(loaded["w_sc"], 16)
                act.activation(flat(w_sc_hi[:, :, :]), w_sc[:, :], ACT.Copy).then_inc(act_done, me.done("w_sc.hi"))
                act.wait_ge(loaded["level"], 16)
                act.activation(levels[:, :], level_in[:, :], ACT.Copy).then_inc(act_done, me.done("levels"))

            def xo_in(j):
                act.wait_ge(pe_used, end("w2_gate2", 3))
                job("xo", j)

            def scalars(part):
                if part == 0:
                    act.wait_ge(pe_done, me.at("scT.proj"))
                    act.activation(scT[0:32, :], bank_of("scT", 0)[0:32, 0:T], ACT.Copy)\
                        .then_inc(act_done, me.done("scT"))
                if part == 1:
                    act.wait_ge(pe_done, me.at("sc.proj"))
                    b = bank_of("sc", 0)
                    act.wait_ge(act_done, me.at("x.rinv"))
                    for t in range(NT):
                        act.activation(beta[:, 16 * t:16 * t + 16], b[:, 32 * t:32 * t + 16], ACT.Sigmoid, scale=rms("x", t))\
                            .then_inc(act_done, me.done("beta"))
                if part == 2:
                    act.wait_ge(dve_done, me.at("sc.xa"))
                    act.activation(tmp_a, xa, ACT.Abs).then_inc(act_done, me.done())
                    act.wait_ge(act_done, me.here())
                    act.activation(tmp_a, tmp_a, ACT.Exp, scale=-1.0).then_inc(act_done, me.done("sc.exp"))
                    act.activation(e_alog, cols["a_log"], ACT.Exp).then_inc(act_done, me.done("sc.ealog"))
                if part == 3:
                    act.wait_ge(dve_done, me.at("sc.plus1"))
                    act.activation(tmp_b, tmp_a, ACT.Ln).then_inc(act_done, me.done("sc.ln"))

            def decays():
                act.wait_ge(pe_done, me.at("sc.sums"))
                act.activation(e_sc, bank_of("dec", 0)[:, 0:128], ACT.Exp).then_inc(act_done, me.done("e_sc"))

            def fourier(g):
                if g >= 1:
                    act.wait_ge(pe_done, me.at(f"fourier{g}.out"))
                    act.activation(b_hi[0][:, g - 1, :], bank_of("f_out", g)[:, 0:T], ACT.Copy)\
                        .then_inc(act_done, me.done(f"fourier{g}.hi"))
                if g < 8:
                    act.wait_ge(pe_done, me.at(f"fourier{g}.time"))
                    act.activation(fp[:, g % 2, :], bank_of("f_time", g), ACT.Copy)\
                        .then_inc(act_done, me.done(f"fourier{g}.P"))

            def conv_in(half, x, part):
                for b in range(2 if part == 0 else 0):
                    act.wait_ge(pe_done, me.at(f"conv{half}{x}.T{b}"))
                    act.wait_ge(pool_done, me.at(f"pad{half}"))
                    if (half, x) != (0, 0):
                        act.wait_ge(dve_done, me.at(f"conv{half}{x - 1}.sum" if x else f"conv{half - 1}2.sum"))
                    act.activation(padT[:, 2 * b:2 * b + 2, 2:2 + T], bank_of(f"conv{half}{x}",
                        b).rearrange("p (h c) -> p h c", h=2), ACT.Copy)\
                        .then_inc(act_done, me.done(f"conv{half}{x}.pad{b}"))
                if part == 0:
                    return
                act.wait_ge(dve_done, me.at(f"conv{half}{x}.sum"))
                act.activation(flat(convT[:, :, :]), flat(convT[:, :, :]), ACT.Silu)\
                    .then_inc(act_done, me.done(f"conv{half}{x}.silu"))
                if x < 2:
                    act.wait_ge(act_done, me.here())
                    act.activation(flat(squares[:, :, :]), flat(convT[:, :, :]), ACT.Square)\
                        .then_inc(act_done, me.done(f"conv{half}{x}.sq"))

            def conv_norm(half, x):
                act.wait_ge(dve_done, me.at(f"conv{half}{x}.inv"))
                act.activation(flat(squares[:, :, :]), flat(squares[:, :, :]), ACT.Sqrt,
                    scale=1.0 / HD if x == 0 else 1.0)\
                    .then_inc(act_done, me.done(f"conv{half}{x}.rinv"))

            def conv_back(half, x):
                for t in range(NT):
                    act.wait_ge(pe_done, me.at(f"v{half}.T{t}"))
                    act.activation(v_rows[:, t].rearrange("p h c -> p (h c)"), bank_of(f"v{half}", t), ACT.Copy)\
                        .then_inc(act_done, me.done(f"v{half}.rows{t}"))

            def decay(half, t):
                for d in range(2):
                    act.wait_ge(pe_done, me.at(f"decay{half}{t}.D{d}"))
                    if (half, t) != (0, 0):
                        act.wait_ge(pool_done, me.at(f"solT{prev(half, t)}.{d}"))
                    if (half, t) == (1, 0):
                        act.wait_ge(dve_done, me.at("scan0.3.out.DVE"))
                    act.activation(EM(d), bank_of(f"decay{half}{t}", d), ACT.Exp)\
                        .then_inc(act_done, me.done(f"decay{half}{t}.E{d}"))

            def turn(half, t):
                for d in range(2):
                    act.wait_ge(pe_done, me.at(f"turn{half}{t}.M{d}"))
                    act.activation(MT(d), bank_of(f"turnM{half}{t}", d), ACT.Copy)\
                        .then_inc(act_done, me.done(f"turn{half}{t}.MT{d}"))
                for d in range(2):
                    act.wait_ge(pe_done, me.at(f"turn{half}{t}.Q{d}"))
                    act.activation(qkT[:, t, d].rearrange("p h c -> p (h c)"), bank_of(f"turnQ{half}{t}", d),
                        ACT.Copy)\
                        .then_inc(act_done, me.done(f"turn{half}{t}.QT{d}"))

            def solve_y(half, t, n):
                for d in range(2):
                    act.wait_ge(pe_done, me.at(f"solve{half}{t}{n}.Y{d}"))
                    if n == 1:
                        act.wait_ge(dve_done, me.at(f"turn{half}{t}.X{d}"))
                    act.activation(MM(d), bank_of(f"solveY{half}{t}{n}", d), ACT.Copy)\
                        .then_inc(act_done, me.done(f"solve{half}{t}{n}.Yc{d}"))

            def scan_new(half, st):
                for d in range(2):
                    c, t, rs = chunk_of(st, d)
                    act.wait_ge(pe_done, me.at(f"scan{half}.{st}.new{d}"))
                    act.activation(EB(d)[rs, :], bank_of(f"scanN{half}{st}", d)[rs, :], ACT.Copy)\
                        .then_inc(act_done, me.done(f"scan{half}.{st}.vnew{d}"))

            def ssm_small(part):
                T_ = lambda i: ssm_t[:, i, :]
                if part == 0:
                    act.wait_ge(act_done, me.at("pre.hi"))
                    act.activation(T_(0), cols["log_dt"], ACT.Exp).then_inc(act_done, me.done("ssm.dt"))
                if part == 1:
                    act.wait_ge(dve_done, me.at("ssm.ab"))
                    act.activation(T_(4), T_(1), ACT.Exp).then_inc(act_done, me.done())
                    act.activation(T_(5), T_(1), ACT.Tanh, scale=0.5).then_inc(act_done, me.done())
                    act.activation(T_(6), T_(3), ACT.Sin).then_inc(act_done, me.done())
                    act.activation(T_(7), T_(3), ACT.Sin, scale=0.5).then_inc(act_done, me.done("ssm.sin"))

            def ssm_u():
                for j in range(4):
                    t, q = j // 2, j % 2
                    act.wait_ge(pe_done, me.at(f"uT.{j}.T"))
                    act.activation(uT[:, 4 * q:4 * q + 4, t * P:(t + 1) * P], four(bank_of("uT", j)), ACT.Copy)\
                        .then_inc(act_done, me.done(f"uT.{j}"))

            def ssm(i, part):
                if part == 3 and i >= 2 and i % 2 == 0:
                    ct = (i - 2) // 2
                    act.wait_ge(dve_done, me.at(f"ssm{i}.ysum"))
                    act.activation(uT[:, ct, :], prod_y(ct), ACT.Gelu_apprx_tanh)\
                        .then_inc(act_done, me.done(f"gelu{ct}"))

            def gelu_turn():
                act.wait_ge(act_done, me.here())
                act.wait_ge(pe_done, me.at("sg_mix.PE"))
                act.wait_ge(dve_done, me.at("sg.gated"))
                act.activation(b_hi[1][:, :, :], uT[:, :, :], ACT.Copy).then_inc(act_done, me.done("gelu.hi"))

            def turned(tag, dst, scale):
                for j in range(4):
                    t, q = j // 2, j % 2
                    act.wait_ge(pe_done, me.at(f"{tag}.{j}.T"))
                    act.activation(dst[:, 4 * q:4 * q + 4, t * P:(t + 1) * P], four(bank_of(tag, j)), ACT.Copy,
                        scale=scale)\
                        .then_inc(act_done, me.done(f"{tag}.{j}.t"))

            def xa_score(h):
                act.wait_ge(dve_done, me.at(f"xa{h}.max"))
                if h:
                    act.wait_ge(pe_done, me.at(f"xa{h - 1}.PT"))
                for t in range(NT):
                    act.activation(prob[:, t, :], bank_of("xs", h)[:, t * T:(t + 1) * T], ACT.Exp, bias=st_[:,
                        4 + t:5 + t], accum_out=st_[:, 8 + t:9 + t])\
                        .then_inc(act_done, me.done(f"xa{h}.exp"))

            def xa_prob(h):
                act.wait_ge(pe_done, me.at(f"xa{h}.PT"))
                act.activation(flat(probT[:, :, :]), bank_of("xp", h), ACT.Copy)\
                    .then_inc(act_done, me.done(f"xa{h}.pT"))

            def xa_out(h):
                act.wait_ge(pe_done, me.at(f"xa{h}.O"))
                act.activation(flat(xqT[:, 2 * h:2 * h + 2, :]), bank_of("xo_", h), ACT.Copy)\
                    .then_inc(act_done, me.done(f"xa{h}.out"))

            def glu_rest():
                act.wait_ge(dve_emptied, emptied(INDEX[("glu_w", 1)], "dve"))
                act.activation(flat(glu[:, :, :]), flat(glu[:, :, :]), ACT.Sigmoid)\
                    .then_inc(act_done, me.done("glu.sig"))

            steps = {"tables": tables, "scalars": scalars, "decays": decays, "fourier": fourier, "conv_in": conv_in, "conv_norm": conv_norm,
                     "conv_back": conv_back, "decay": decay, "turn": turn, "solve_y": solve_y,
                     "scan_new": scan_new, "heads_norm": lambda part: root("heads", 64, 16) if part == 1 else None,
                     "heads_in": heads_in,
                     "x_in": lambda n: rows_in("x", n), "y_in": lambda n: rows_in("y", n),
                     "mlp_in": lambda n: rows_in("mlp", n), "pre_in": lambda n: rows_in("pre", n),
                     "merge_in": lambda n: rows_in("merge", n), "mem_in": lambda t, n: job(f"mem{t}", n),
                     "x_root": lambda: root("x", RMS["x"], NT), "mlp_root": lambda: root("mlp", RMS["mlp"], NT),
                     "mem_root": lambda t: root(f"mem{t}", RMS["mem"] + t, 1),
                     "final_root": lambda: root("final", RMS["final"], NT),
                     "pre_root": lambda: root("pre", RMS["pre"], NT),
                     "hidden": lambda p, j: jobs(f"hidden{p}.{j}"),
                     "ssm_small": ssm_small, "ssm_u": ssm_u, "ssm": ssm,
                     "sg_norm": lambda part: root("sgn", 64, NT) if part == 0 else None,
                     "sg_in": lambda j: job("sg", j), "gelu_turn": gelu_turn,
                     "xa_k": lambda: turned("km", kmT, 1.0), "xa_q": lambda: turned("xq", xqT, 1.0 / 16),
                     "xa_score": xa_score, "xa_prob": xa_prob, "xa_out": xa_out,
                     "xo_in": xo_in, "glu_rest": glu_rest, "glu_in": lambda j: job("glu", j)}
            rows_in("x", 0)
            split(0)
            split(1)

            def slot_work(n):
                run_steps(me, steps, 2 * n)
                if n + SPLIT < UNITS:
                    split(n + SPLIT)
                if n in CHUNK_END:
                    empty(CHUNK_END[n])
                run_steps(me, steps, 2 * n + 1)

            def after_loop():
                ts_user[:] = [f"hidden{NPIECE - 2}.1.0"] * 2

            drive(me, slot_work, after_loop)
            root("out", RMS["out"], NT)

        @block.gpsimd
        def _(pool):
            me = Side("pool", pool, done, old, new)

            def pads(half):
                if half == 0:
                    pool.wait_ge(act_done, me.at("levels"))
                else:
                    pool.wait_ge(pe_done, me.at("scan0.3.out.PE"))
                    pool.wait_ge(dve_done, me.at("scan0.3.out.DVE"))
                    pool.wait_ge(act_done, me.at("scan0.3.vnew1"))
                pool.memset(padT[:, :, 0:2], 0.0).then_inc(pool_done, me.done())
                pool.memset(padT[:, :, 258:260], 0.0).then_inc(pool_done, me.done("pad0" if half == 0 else "pad1"))

            def key_rows(half):
                pool.wait_ge(pe_done, me.at("fourier8.out"))
                pool.wait_ge(act_done, me.at("fourier7.P"))
                pool.memset(o_rows[:, :, 4 * half:4 * half + 4, :], 0.0).then_inc(pool_done, me.done(f"o_zero{half}"))

            def gram(half, t):
                pool.wait_ge(dve_done, me.at("decays.g", f"key{half}.1.0", f"conv{half}2.sum"))
                if (half, t) != (0, 0):
                    pool.wait_ge(pe_done, me.at(f"solve{prev(half, t)}5.Y1"))
                if half == 1 and t == 0:
                    pool.wait_ge(pe_done, me.at("scan0.3.out.PE"))
                for d in range(2):
                    g = g_log[:, bt(t, d, half)]
                    mask = cols["LE" if d == 0 else "GE"]
                    pool.tensor_tensor(four(RG(d)), many(mask, 4), wide(g, P), ALU.mult)\
                        .then_inc(pool_done, me.done(f"gram{half}{t}.R{d}"))

            def decay(half, t):
                for d in (0,):
                    pool.wait_ge(act_done, me.at(f"decay{half}{t}.E{d}"))
                    pool.tensor_tensor(four(EM(d)), four(EM(d)), many(cols["GE" if d == 0 else "LE"], 4), ALU.mult)\
                        .then_inc(pool_done, me.done(f"decay{half}{t}.Em{d}"))
                    pool.wait_ge(pool_done, me.here())
                    if half == 1 or t == 1:
                        pool.wait_ge(pool_done, me.at(f"solT{prev(half, t)}.{d}"))
                    pool.tensor_tensor(four(EB(d)), four(EM(d)), wide(beta[:, bt(t, d, half)], P), ALU.mult)\
                        .then_inc(pool_done, me.done(f"decay{half}{t}.Eb{d}"))

            def turn(half, t):
                for d in range(2):
                    pool.wait_ge(act_done, me.at(f"turn{half}{t}.MT{d}"))
                    pool.wait_ge(pe_done, me.at(f"decay{half}{t}.D{d}"))
                    pool.tensor_tensor(four(RG(d)), four(MT(d)), many(level[d][:, 1, :], 4), ALU.mult)\
                        .then_inc(pool_done, me.done(f"solve{half}{t}1.Mt{d}"))

            def solve_x(half, t, n):
                for d in range(2):
                    if n < len(LEVELS) - 1:
                        pool.wait_ge(pe_done, me.at(f"solve{half}{t}{n}.Y{d}"))
                        pool.tensor_tensor(four(RG(d)), four(MT(d)), many(level[d][:, n + 1, :], 4), ALU.mult)\
                            .then_inc(pool_done, me.done(f"solve{half}{t}{n + 1}.Mt{d}"))
                    else:
                        pool.wait_ge(dve_done, me.at(f"solve{half}{t}{n}.XT{d}"))
                        pool.tensor_tensor(solT[:, t, d], four(EM(d)), wide(beta[:, bt(t, d, half)], P), ALU.mult)\
                            .then_inc(pool_done, me.done(f"solT{half}{t}.{d}"))

            def scan_new(half, st):
                if st in (1, 2):
                    pool.wait_ge(pe_done, me.at(f"scan{half}.{st}.in.PE"))
                    for d in range(2):
                        c, t, rs = chunk_of(st, d)
                        pool.tensor_tensor(state[:, d], state[:, d], wide(sc[:, e_gl(c, d, half)], HD), ALU.mult)\
                            .then_inc(pool_done, me.done(f"scan{half}.{st}.decayed{d}"))

            def ssm(i, part):
                if i > 15 or part:
                    return
                k, t0 = i % 2, 2 * i
                if i >= 2:
                    pool.wait_ge(dve_done, me.at(f"ssm{i - 2}.DVE"))
                if i == 0:
                    pool.wait_ge(dve_done, me.at("ssm.pow"))
                pa = [pow_a[:, z, t0:t0 + 2, :].unsqueeze(3).broadcast_to([P, 2, 16, 16]) for z in range(2)]
                pb = [pow_b[:, z, t0:t0 + 2, :].unsqueeze(2).broadcast_to([P, 2, 16, 16]) for z in range(2)]
                c_, s_ = [rot[:, k, z].rearrange("p g (a b) -> p g a b", a=16) for z in range(2)]
                x_ = ptmp[:, :].rearrange("p (g a b) -> p g a b", g=2, a=16)
                pool.wait_ge(pool_done, me.here())
                for g in range(2):
                    pool.tensor_tensor(c_[:, g], pa[0][:, g], pb[0][:, g], ALU.mult).then_inc(pool_done, me.done())
                    pool.tensor_tensor(x_[:, g], pa[1][:, g], pb[1][:, g], ALU.mult).then_inc(pool_done, me.done())
                pool.wait_ge(pool_done, me.here())
                pool.tensor_tensor(flat(rot[:, k, 0]), flat(rot[:, k, 0]), ptmp[:, :], ALU.subtract)\
                    .then_inc(pool_done, me.done())
                pool.wait_ge(pool_done, me.here())
                for g in range(2):
                    pool.tensor_tensor(s_[:, g], pa[0][:, g], pb[1][:, g], ALU.mult).then_inc(pool_done, me.done())
                    pool.tensor_tensor(x_[:, g], pa[1][:, g], pb[0][:, g], ALU.mult).then_inc(pool_done, me.done())
                pool.wait_ge(pool_done, me.here())
                pool.tensor_tensor(flat(rot[:, k, 1]), flat(rot[:, k, 1]), ptmp[:, :], ALU.add)\
                    .then_inc(pool_done, me.done(f"ssm{i}.rot"))
                me.new[f"ssm{i}.POOL"] = me.new[f"ssm{i}.rot"]
                if i % 2 == 0:
                    ct, kk = i // 2, (i // 2) % 2
                    if ct == 0:
                        pool.wait_ge(dve_done, me.at("ssm.ceff"))
                    if ct >= 2:
                        pool.wait_ge(pe_done, me.at(f"ssm{2 * ct - 2}.y"))
                    for u in range(2):
                        rs = slice(64 * u, 64 * u + 64)
                        pool.wait_ge(pool_done, me.here())
                        for z in range(2):
                            for a_ in range(4):
                                col = 160 * a_ + 16 * u
                                pool.tensor_copy(c_pad[rs, kk, z, col:col + 16], c_eff[rs, z, 4 * ct + a_, :])\
                                    .then_inc(pool_done, me.done(f"cpad{ct}"))
                    pool.wait_ge(pool_done, me.here())

            def sg_norm(part):
                if part:
                    return
                pool.wait_ge(loaded["w_sg"], 16)
                pool.tensor_tensor(w_sg[:, :, :], w_sg[:, :, :], many(cols["causal"], 8), ALU.mult)\
                    .then_inc(pool_done, me.done("w_sg.masked"))

            def ssm_small(part):
                if part != 2:
                    return
                pool.wait_ge(act_done, me.at("pre.hi"))
                pool.wait_ge(dve_done, me.at("pre.lo"))
                pool.wait_ge(pe_used, end("xa_wk", 1))
                pool.wait_ge(spill_stored[3], spills_until("xa_wk", 1, 1))
                pool.wait_ge(spill_stored[2], spills_until("xa_wk", 1, 0))
                pool.wait_ge(dve_done, me.at("pre.scale"))
                pool.memset(c_pad[:, :, :, :], 0.0).then_inc(pool_done, me.done("cpad.zero"))

            steps = {"conv_in": lambda half, x, part: pads(half) if (x, part) == (0, 0) else None,
                     "key_rows": key_rows, "gram": gram, "decay": decay, "turn": turn, "solve_x": solve_x,
                     "scan_new": scan_new, "ssm": ssm, "sg_norm": sg_norm, "ssm_small": ssm_small}
            for n in range(UNITS):
                if not LOOP0 <= n < LOOP0 + LOOP_UNITS:
                    run_steps(me, steps, 2 * n)
                    run_steps(me, steps, 2 * n + 1)

        @block.vector
        def _(dve):
            me = Side("dve", dve, done, old, new)
            ts_user = [None, None]
            ts_turn = [0]

            def split(n):
                dve.wait_ge(hi_split, value(me, n + 1, LOOP_UNITS))
                dve.tensor_tensor(w_lo[:, n % SPLIT, :], raw[:, n % RAW, :], w_hi[:, n % SPLIT, :].bitcast(F32),
                                  ALU.subtract).then_inc(lo_split, 1)

            def job(tag, j):
                src, dst, mode, g = JOBS[tag][j]
                if mode == "plain":
                    dve.wait_ge(act_done, me.at(f"{tag}.{j}.hi"))
                    dve.tensor_tensor(dst[1], four(bank_of(tag, j)), dst[0].bitcast(F32), ALU.subtract)\
                        .then_inc(dve_done, me.done(f"{tag}.{j}.lo", f"{tag}.lo"))
                    return
                k = ts_turn[0] % 2
                ts_turn[0] += 1
                if mode == "gain":
                    if ts_user[k]:
                        dve.wait_ge(act_done, me.at(f"{ts_user[k]}.hi"))
                    dve.wait_ge(pe_done, me.at(f"{tag}.{j}.T"))
                    dve.tensor_tensor(four(ts[:, k, :]), four(bank_of(tag, j)), g, ALU.mult)\
                        .then_inc(dve_done, me.done(f"{tag}.{j}.tmp"))
                dve.wait_ge(act_done, me.at(f"{tag}.{j}.hi"))
                if mode == "gain":
                    dve.wait_ge(dve_done, me.here())
                dve.tensor_tensor(dst[1], four(ts[:, k, :]), dst[0].bitcast(F32), ALU.subtract)\
                    .then_inc(dve_done, me.done(f"{tag}.{j}.lo", f"{tag}.lo"))
                ts_user[k] = f"{tag}.{j}"

            def jobs(tag):
                for j in range(len(JOBS[tag])):
                    job(tag, j)

            def heads_in(j):
                dve.wait_ge(pe_used, A_FREE["heads"])
                job("heads", j)

            def stats_in(rows, n, base=0):
                for t, r in enumerate(rows):
                    o = base + 24 * t + 6 * n
                    dve.bn_stats(st_[:, o:o + 6], r[:, n * NW:(n + 1) * NW]).then_inc(dve_done, me.done())

            def inverse(tag, n, k, out_, base=0, center=False):
                dve.wait_ge(dve_done, me.here())
                for t in range(n):
                    o = base + 24 * t
                    dve.bn_aggr(st_[:, 48 + 2 * t:50 + 2 * t], st_[:, o:o + 6 * k]).then_inc(dve_done, me.done())
                dve.wait_ge(dve_done, me.here())
                mv = st_[:, 48:48 + 2 * n].rearrange("p (t c) -> p t c", c=2)
                inv = st_[:, out_:out_ + n].unsqueeze(2)
                if center:
                    dve.tensor_scalar(inv, mv[:, :, 1:2], EPS, None, ALU.add).then_inc(dve_done, me.done())
                else:
                    dve.tensor_tensor(inv, mv[:, :, 0:1], mv[:, :, 0:1], ALU.mult).then_inc(dve_done, me.done())
                    dve.wait_ge(dve_done, me.here())
                    dve.tensor_tensor(inv, inv, mv[:, :, 1:2], ALU.add).then_inc(dve_done, me.done())
                    dve.wait_ge(dve_done, me.here())
                    dve.tensor_scalar(inv, inv, EPS, None, ALU.add).then_inc(dve_done, me.done())
                dve.wait_ge(dve_done, me.here())
                dve.reciprocal(st_[:, out_:out_ + n], st_[:, out_:out_ + n]).then_inc(dve_done, me.done(tag + ".inv"))

            def rows_in(tag, n):
                if tag == "x":
                    dve.wait_ge(loaded[f"x_{n}"], 16)
                elif tag == "mlp":
                    dve.wait_ge(dve_emptied, emptied(INDEX[("w_o", n)], "dve"))
                elif tag == "pre":
                    dve.wait_ge(dve_emptied, emptied(INDEX[(f"w_mlp_down{NPIECE - 1}", n)], "dve"))
                if tag in A_FREE:
                    dve.wait_ge(pe_used, A_FREE[tag])
                job(tag, 2 * n)
                job(tag, 2 * n + 1)
                if tag in ("x", "mlp", "pre"):
                    stats_in([x_rows[:, t, :] for t in range(NT)], n)

            def mem_in(t, n):
                dve.wait_ge(loaded["mem"], 16 * (t + 1))
                job(f"mem{t}", n)
                stats_in([mem_rows[:, :]], n, 96)

            def final_scale(k):
                t, h = k // 2, k % 2
                if k == 0:
                    dve.wait_ge(act_done, me.at("final.rinv"))
                    dve.wait_ge(loaded["g_final"], 16)
                    dve.wait_ge(pe_done, me.at("pre.T"))
                c = slice(h * W, (h + 1) * W)
                dve.scalar_tensor_tensor(x_rows[:, t, c], x_rows[:, t, c], rms("final", t), gain[:, c], ALU.mult, ALU.mult)\
                    .then_inc(dve_done, me.done())
                dve.wait_ge(dve_done, me.here())
                for n in (2 * h, 2 * h + 1):
                    o = 24 * t + 6 * n
                    dve.bn_stats(st_[:, o:o + 6], x_rows[:, t, n * NW:(n + 1) * NW]).then_inc(dve_done, me.done())

            def final_root():
                inverse("final", NT, 4, RMS["final"])

            def pre_root():
                inverse("pre", NT, 4, RMS["pre"])
                dve.wait_ge(act_done, me.at("pre.rinv"))
                c, f = RMS["pre"], RMS["final"]
                dve.tensor_tensor(st_[:, c:c + NT], st_[:, c:c + NT], st_[:, f:f + NT], ALU.mult)\
                    .then_inc(dve_done, me.done("pre.scale"))

            def empty(i):
                name, n, _, by = CHUNKS[i]
                if by != "dve":
                    return
                dve.wait_ge(pe_used, value(me, FIRST[i + 1], LOOP_UNITS))
                if me.it is not None or name[:10] == "w_mlp_down" or name == "w_o":
                    dve.wait_ge(dve_emptied, value(me, emptied(i, "dve") - NT, 8 * NT))
                cs = slice(n * NW, (n + 1) * NW)
                for t in range(NT):
                    src = acc[:, i % 2, t, :]
                    if name in ("w_fourier", "w_dn_up"):
                        k = n + (4 if name == "w_dn_up" else 0)
                        if t == 0:
                            dve.wait_ge(loaded[f"gate{k % 2}"], 16 * (k // 2 + 1))
                        dst = y_rows[:, t, cs] if k < 4 else gate_in[:, k % 2, t, :]
                        if k == 0 and t == 0:
                            dve.wait_ge(pe_done, me.at("scan1.3.out.PE"))
                            dve.wait_ge(act_done, me.at("scan1.3.vnew0", "scan1.3.vnew1"))
                        ins = dve.tensor_tensor(dst, src, gate_in[:, k % 2, t, :], ALU.mult)
                    elif name in ("w_o",) or name.startswith("w_mlp_down"):
                        if name == "w_o" and n == 0 and t == 0:
                            dve.wait_ge(loaded["x2"], 16)
                        ins = dve.tensor_tensor(x_rows[:, t, cs], x_rows[:, t, cs], src, ALU.add)
                    elif name == "glu_w":
                        if n == 0 and t == 0:
                            dve.wait_ge(loaded["glu_b"], 16)
                        ins = dve.tensor_tensor(glu[:, t, cs], src, glu_b[:, cs], ALU.add)
                    elif name.startswith("w_branch"):
                        k = 4 * (0, 2, 1).index(int(name[8:])) + n
                        if t == 0:
                            dve.wait_ge(loaded[f"gate{k % 2}"], 16 * (4 + k // 2 + 1))
                        if k == 0 and t == 0:
                            dve.wait_ge(pe_done, me.at("xo.T"))
                        if k < 4:
                            ins = dve.tensor_tensor(y_rows[:, t, cs], src, gate_in[:, k % 2, t, :], ALU.mult)
                        else:
                            ins = dve.tensor_tensor(gate_in[:, k % 2, t, :], src, gate_in[:, k % 2, t, :], ALU.mult)
                    else:
                        if n == 0 and t == 0:
                            dve.wait_ge(loaded["post_g"], 16)
                            dve.wait_ge(pe_done, me.at("merge.T"))
                        o = 24 * t + 6 * n
                        dve.bn_stats(st_[:, o:o + 6], src).then_inc(dve_done, me.done())
                        ins = dve.tensor_tensor(y_rows[:, t, cs], src, post_gain[:, cs], ALU.mult)
                    ins.then_inc(dve_emptied, 1)
                if name == "w_dn_up" or name.startswith("w_branch") and name != "w_branch0":
                    k = n % 2
                    dve.wait_ge(dve_emptied, emptied(i, "dve"))
                    dve.tensor_tensor(y_rows[:, :, cs], y_rows[:, :, cs], gate_in[:, k, :, :], ALU.add)\
                        .then_inc(dve_done, me.done(f"{name}{n}.y"))
                elif name == "w_branch0":
                    new[f"{name}{n}.y"] = ("dve_emptied", emptied(i, "dve"))

            def scalars(part):
                x_ = lambda a_: a_.rearrange("p (t c) -> p t c", t=NT)
                if part == 1:
                    dve.wait_ge(act_done, me.at("beta"))
                    for t in range(NT):
                        dve.scalar_tensor_tensor(xa[:, 16 * t:16 * t + 16], bank_of("sc", 0)[:, 32 * t + 16:32 * t + 32],
                                                 rms("x", t), cols["dt_bias"], ALU.mult, ALU.add)\
                            .then_inc(dve_done, me.done("sc.xa"))
                if part == 2:
                    dve.wait_ge(act_done, me.at("sc.exp"))
                    dve.tensor_scalar(tmp_a, tmp_a, 1.0, None, ALU.add).then_inc(dve_done, me.done("sc.plus1"))
                    dve.tensor_scalar(xa, xa, 0.0, -1.0, ALU.max, ALU.mult).then_inc(dve_done, me.done())
                if part == 3:
                    dve.wait_ge(act_done, me.at("sc.ln", "sc.ealog"))
                    dve.wait_ge(dve_done, me.here())
                    dve.tensor_tensor(xa, xa, tmp_b, ALU.subtract).then_inc(dve_done, me.done())
                    dve.wait_ge(dve_done, me.here())
                    dve.tensor_tensor(x_(g_log), x_(xa), many(e_alog, NT), ALU.mult)\
                        .then_inc(dve_done, me.done("decays.g"))

            def fourier(g):
                if g >= 1:
                    dve.wait_ge(act_done, me.at(f"fourier{g}.hi"))
                    dve.tensor_tensor(b_lo[0][:, g - 1, :], bank_of("f_out", g)[:, 0:T],
                        b_hi[0][:, g - 1, :].bitcast(F32), ALU.subtract)\
                        .then_inc(dve_done, me.done(f"fourier{g}.lo"))

            def conv_in(half, x, part):
                dve.wait_ge(act_done, me.at(f"conv{half}{x}.pad0", f"conv{half}{x}.pad1"))
                dve.wait_ge(pool_done, me.at("pad1" if half else "pad0"))
                if (half, x) == (1, 0):
                    dve.wait_ge(pe_done, me.at("scan0.3.out.PE"))
                elif x:
                    dve.wait_ge(pe_done, me.at(f"conv{half}{x - 1}.T1"))
                    if part == 0:
                        dve.wait_ge(dve_done, me.here())
                for j in range(5):
                    for hd in (2 * part, 2 * part + 1):
                        w = 5 * (8 * x + 4 * half + hd) + j
                        w = cols["conv_w"][:, w:w + 1]
                        u = padT[:, hd, j:j + T]
                        if j == 0:
                            dve.tensor_scalar(convT[:, hd, :], u, w, None, ALU.mult).then_inc(dve_done, me.done())
                        else:
                            dve.wait_ge(dve_done, me.count - 1)
                            dve.scalar_tensor_tensor(convT[:, hd, :], u, w, convT[:, hd, :], ALU.mult, ALU.add)\
                                .then_inc(dve_done, me.done(f"conv{half}{x}.sum"))

            def conv_norm(half, x):
                sq = flat(squares[:, :, :])
                for b in range(2):
                    dve.wait_ge(pe_done, me.at(f"norm{half}{x}.S{b}"))
                    dve.tensor_scalar(sq[:, b * NW:(b + 1) * NW], bank_of(f"norm{half}{x}", b), EPS, None, ALU.add)\
                        .then_inc(dve_done, me.done())
                dve.wait_ge(dve_done, me.here())
                dve.reciprocal(sq, sq).then_inc(dve_done, me.done(f"conv{half}{x}.inv"))
                dve.wait_ge(act_done, me.at(f"conv{half}{x}.rinv"))
                if half == 1:
                    dve.wait_ge(pe_done, me.at("scan0.3.out.PE"))
                dst = qT if x == 0 else kT
                dve.tensor_tensor(flat(dst[:, :, :]), flat(convT[:, :, :]), sq, ALU.mult)\
                    .then_inc(dve_done, me.done(f"{'qk'[x]}T{half}"))

            def key_rows(half):
                dve.wait_ge(act_done, me.at("e_sc"))
                for t in range(NT):
                    dve.wait_ge(pe_done, me.at(f"key{half}.T{t}"))
                    for d in range(2):
                        dve.tensor_tensor(k_dec[:, d, t], four(bank_of(f"key{half}", t)),
                            wide(sc[:, e_kd(t, d, half)], HD), ALU.mult)\
                            .then_inc(dve_done, me.done(f"key{half}.{t}.{d}"))

            def decay(half, t):
                dve.wait_ge(act_done, me.at(f"decay{half}{t}.E1"))
                dve.tensor_tensor(four(EM(1)), four(EM(1)), many(cols["LE"], 4), ALU.mult).then_inc(dve_done, me.done())
                if (half, t) != (0, 0):
                    dve.wait_ge(pool_done, me.at(f"solT{prev(half, t)}.1"))
                dve.wait_ge(dve_done, me.here())
                dve.tensor_tensor(four(EB(1)), four(EM(1)), wide(beta[:, bt(t, 1, half)], P), ALU.mult)\
                    .then_inc(dve_done, me.done())
                dve.wait_ge(pe_done, me.at(f"gram{half}{t}.G", f"gram{half}{t}.Q"))
                dve.wait_ge(dve_done, me.here())
                for d in (1, 0):
                    if d == 0:
                        dve.wait_ge(pool_done, me.at(f"decay{half}{t}.Eb0"))
                    dve.tensor_tensor(MM(d), bank_of(f"gramG{half}{t}", 0), EB(d), ALU.mult)\
                        .then_inc(dve_done, me.done(f"decay{half}{t}.M{d}"))
                    dve.tensor_tensor(QK(d), bank_of(f"gramQ{half}{t}", 0), EM(d), ALU.mult)\
                        .then_inc(dve_done, me.done(f"decay{half}{t}.Q{d}"))

            def turn(half, t):
                dve.wait_ge(dve_done, me.here())
                for d in range(2):
                    dve.tensor_tensor(four(EB(d)), four(MM(d)), many(level[1 - d][:, 0, :], 4), ALU.mult)\
                        .then_inc(dve_done, me.done())
                    dve.wait_ge(act_done, me.at(f"turn{half}{t}.MT{d}"))
                    dve.tensor_tensor(four(EM(d)), four(MT(d)), many(level[d][:, 0, :], 4), ALU.mult)\
                        .then_inc(dve_done, me.done())
                dve.wait_ge(dve_done, me.here())
                for d in range(2):
                    dve.tensor_tensor(four(EB(d)), many(ident, 4), four(EB(d)), ALU.subtract)\
                        .then_inc(dve_done, me.done(f"turn{half}{t}.X{d}"))
                    dve.tensor_tensor(four(EM(d)), many(ident, 4), four(EM(d)), ALU.subtract)\
                        .then_inc(dve_done, me.done(f"turn{half}{t}.XT{d}"))

            def solve_x(half, t, n):
                dve.wait_ge(dve_done, me.here())
                for d in range(2):
                    dve.wait_ge(pe_done, me.at(f"solve{half}{t}{n}.ZT{d}"))
                    if n < len(LEVELS) - 1:
                        dve.wait_ge(pe_done, me.at(f"solve{half}{t}{n}.Z{d}"))
                    dve.tensor_tensor(EM(d), EM(d), bank_of(f"solveT{half}{t}{n}", d), ALU.subtract)\
                        .then_inc(dve_done, me.done(f"solve{half}{t}{n}.XT{d}"))
                    if n < len(LEVELS) - 1:
                        dve.tensor_tensor(EB(d), EB(d), bank_of(f"solveZ{half}{t}{n}", d), ALU.subtract)\
                            .then_inc(dve_done, me.done(f"solve{half}{t}{n}.X{d}"))

            def scan_in(half, st):
                if st == 0:
                    return
                for d in range(2):
                    c, t, rs = chunk_of(st, d)
                    e = wide(sc[rs, e_gc(t, d, half)], HD)
                    dve.wait_ge(pe_done, me.at(f"scan{half}.{st}.P{d}"))
                    dve.wait_ge(act_done, me.at(f"v{half}.rows{t}"))
                    dve.tensor_tensor(four(RG(d)[rs, :]), four(bank_of(f"scanP{half}{st}", d)[rs, :]), e, ALU.mult)\
                        .then_inc(dve_done, me.done())
                    dve.wait_ge(pe_done, me.at(f"scan{half}.{st}.O{d}"))
                    dve.tensor_tensor(four(EM(d)[rs, :]), four(bank_of(f"scanO{half}{st}", d)[rs, :]), e, ALU.mult)\
                        .then_inc(dve_done, me.done())
                    dve.wait_ge(dve_done, me.here())
                    dve.tensor_tensor(four(RG(d)[rs, :]), v_rows[rs, t], four(RG(d)[rs, :]), ALU.subtract)\
                        .then_inc(dve_done, me.done(f"scan{half}.{st}.r{d}"))
                    o_ = o_rows[rs, t, 4 * half:4 * half + 4, :]
                    dve.tensor_tensor(o_, o_, four(EM(d)[rs, :]), ALU.add).then_inc(dve_done, me.done())

            def scan_out(half, st):
                for d in range(2):
                    c, t, rs = chunk_of(st, d)
                    dve.wait_ge(pe_done, me.at(f"scan{half}.{st}.o2{d}"))
                    dve.wait_ge(pool_done, me.at(f"o_zero{half}"))
                    dve.wait_ge(dve_done, me.here())
                    o_ = o_rows[rs, t, 4 * half:4 * half + 4, :]
                    dve.tensor_tensor(o_, o_, four(bank_of(f"scanQ{half}{st}", d)[rs, :]), ALU.add)\
                        .then_inc(dve_done, me.done(f"scan{half}.{st}.out.DVE"))
                    if st < 3:
                        dve.wait_ge(pe_done, me.at(f"scan{half}.{st}.dS{d}"))
                        b = four(bank_of(f"scanS{half}{st}", d))
                        if st == 0:
                            if half:
                                dve.wait_ge(pe_done, me.at("scan0.3.out.PE"))
                            dve.tensor_copy(state[:, d], b).then_inc(dve_done, me.done(f"scan{half}.{st}.S{d}"))
                        else:
                            dve.wait_ge(pool_done, me.at(f"scan{half}.{st}.decayed{d}"))
                            dve.tensor_tensor(state[:, d], state[:, d], b, ALU.add)\
                                .then_inc(dve_done, me.done(f"scan{half}.{st}.S{d}"))

            def heads_norm(part):
                rows = lambda x: x[:, :, :, :].rearrange("p t h c -> p (t h) c")
                dve.wait_ge(dve_done, me.here())
                if part == 0:
                    dve.wait_ge(pe_done, me.at("scan1.3.out.PE"))
                    dve.tensor_tensor(rows(heads), rows(o_rows), rows(o_rows), ALU.mult).then_inc(dve_done, me.done())
                if part == 1:
                    dve.tensor_reduce(st_[:, 64:80], rows(heads), AX.X, ALU.add).then_inc(dve_done, me.done())
                    dve.wait_ge(dve_done, me.here())
                    dve.tensor_scalar(st_[:, 64:80], st_[:, 64:80], 1.0 / HD, EPS, ALU.mult, ALU.add)\
                        .then_inc(dve_done, me.done())
                    dve.wait_ge(dve_done, me.here())
                    dve.reciprocal(st_[:, 64:80], st_[:, 64:80]).then_inc(dve_done, me.done("heads.inv"))
                if part == 2:
                    dve.wait_ge(act_done, me.at("heads.rinv"))
                    dve.tensor_tensor(rows(heads), rows(o_rows), wide(st_[:, 64:80], HD), ALU.mult)\
                        .then_inc(dve_done, me.done())
                if part == 3:
                    dve.wait_ge(loaded["z"], 32)
                    dve.tensor_tensor(rows(heads), rows(heads), rows(z_rows), ALU.mult)\
                        .then_inc(dve_done, me.done("heads.rows"))

            def ssm_small(part):
                T_ = lambda i: ssm_t[:, i, :]
                re, im = T_(8), cols["a_im"]
                if part == 0:
                    dve.wait_ge(act_done, me.at("ssm.dt"))
                    dve.wait_ge(dve_done, me.here())
                    dve.tensor_scalar(re, cols["a_re"], -1e-4, None, ALU.min).then_inc(dve_done, me.done())
                    dve.wait_ge(dve_done, me.here())
                    dve.tensor_tensor(T_(1), re, T_(0), ALU.mult).then_inc(dve_done, me.done())
                    dve.wait_ge(dve_done, me.here())
                    dve.tensor_tensor(T_(2), im, T_(0), ALU.mult).then_inc(dve_done, me.done())
                    dve.wait_ge(dve_done, me.here())
                    dve.tensor_scalar(T_(9), T_(2), 1.0 / (2 * np.pi), None, ALU.mult).then_inc(dve_done, me.done())
                    dve.wait_ge(dve_done, me.here())
                    dve.tensor_scalar(T_(9), T_(9), MAGIC, MAGIC, ALU.add, ALU.subtract).then_inc(dve_done, me.done())
                    for k, part in enumerate(TWO_PI):
                        dve.wait_ge(dve_done, me.here())
                        dve.tensor_scalar(T_(10), T_(9), part, None, ALU.mult).then_inc(dve_done, me.done())
                        dve.wait_ge(dve_done, me.here())
                        dve.tensor_tensor(T_(3), T_(2) if k == 0 else T_(3), T_(10), ALU.subtract)\
                            .then_inc(dve_done, me.done())
                    dve.wait_ge(dve_done, me.here())
                    dve.tensor_scalar(T_(3), T_(3), 3.1415925, -3.1415925, ALU.min, ALU.max)\
                        .then_inc(dve_done, me.done("ssm.ab"))
                if part == 1:
                    dve.wait_ge(act_done, me.at("ssm.sin"))
                    dve.wait_ge(dve_done, me.here())
                    dve.tensor_tensor(T_(9), T_(7), T_(7), ALU.mult).then_inc(dve_done, me.done())
                    dve.wait_ge(dve_done, me.here())
                    dve.tensor_scalar(T_(9), T_(9), -2.0, None, ALU.mult).then_inc(dve_done, me.done())
                    dve.wait_ge(dve_done, me.here())
                    dve.tensor_scalar(T_(10), T_(9), 1.0, None, ALU.add).then_inc(dve_done, me.done())
                    dve.wait_ge(dve_done, me.here())
                    dve.tensor_scalar(T_(11), T_(4), 1.0, None, ALU.add).then_inc(dve_done, me.done())
                    dve.wait_ge(dve_done, me.here())
                    dve.tensor_tensor(T_(11), T_(11), T_(5), ALU.mult).then_inc(dve_done, me.done())
                    dve.wait_ge(dve_done, me.here())
                    dve.tensor_tensor(T_(12), T_(11), T_(10), ALU.mult).then_inc(dve_done, me.done())
                    dve.wait_ge(dve_done, me.here())
                    dve.tensor_tensor(T_(12), T_(12), T_(9), ALU.add).then_inc(dve_done, me.done())
                    dve.wait_ge(dve_done, me.here())
                    dve.tensor_tensor(T_(13), T_(4), T_(6), ALU.mult).then_inc(dve_done, me.done())
                    dve.wait_ge(dve_done, me.here())
                    dve.tensor_scalar(T_(14), im, -1.0, None, ALU.mult).then_inc(dve_done, me.done())
                    dve.wait_ge(dve_done, me.here())
                    dve.tensor_tensor(T_(14), T_(14), im, ALU.max).then_inc(dve_done, me.done())
                    dve.wait_ge(dve_done, me.here())
                    dve.tensor_scalar(T_(15), re, -1.0, None, ALU.mult).then_inc(dve_done, me.done())
                    dve.wait_ge(dve_done, me.here())
                    dve.tensor_tensor(T_(14), T_(14), T_(15), ALU.max).then_inc(dve_done, me.done())
                    dve.wait_ge(dve_done, me.here())
                    dve.reciprocal(T_(15), T_(14)).then_inc(dve_done, me.done())
                    dve.wait_ge(dve_done, me.here())
                    dve.tensor_tensor(T_(16), re, T_(15), ALU.mult).then_inc(dve_done, me.done())
                    dve.wait_ge(dve_done, me.here())
                    dve.tensor_tensor(T_(17), im, T_(15), ALU.mult).then_inc(dve_done, me.done())
                    dve.wait_ge(dve_done, me.here())
                    dve.tensor_tensor(T_(18), T_(16), T_(16), ALU.mult).then_inc(dve_done, me.done())
                    dve.wait_ge(dve_done, me.here())
                    dve.tensor_tensor(T_(19), T_(17), T_(17), ALU.mult).then_inc(dve_done, me.done())
                    dve.wait_ge(dve_done, me.here())
                    dve.tensor_tensor(T_(18), T_(18), T_(19), ALU.add).then_inc(dve_done, me.done())
                    dve.wait_ge(dve_done, me.here())
                    dve.reciprocal(T_(18), T_(18)).then_inc(dve_done, me.done())
                    dve.wait_ge(dve_done, me.here())
                    dve.tensor_tensor(T_(18), T_(18), T_(15), ALU.mult).then_inc(dve_done, me.done())
                    dve.wait_ge(dve_done, me.here())
                    dve.tensor_tensor(T_(19), T_(12), T_(16), ALU.mult).then_inc(dve_done, me.done())
                    dve.wait_ge(dve_done, me.here())
                    dve.tensor_tensor(T_(20), T_(13), T_(17), ALU.mult).then_inc(dve_done, me.done())
                    dve.wait_ge(dve_done, me.here())
                    dve.tensor_tensor(T_(19), T_(19), T_(20), ALU.add).then_inc(dve_done, me.done())
                    dve.wait_ge(dve_done, me.here())
                    dve.tensor_tensor(T_(19), T_(19), T_(18), ALU.mult).then_inc(dve_done, me.done())
                    dve.wait_ge(dve_done, me.here())
                    dve.tensor_tensor(T_(20), T_(13), T_(16), ALU.mult).then_inc(dve_done, me.done())
                    dve.wait_ge(dve_done, me.here())
                    dve.tensor_tensor(T_(21), T_(12), T_(17), ALU.mult).then_inc(dve_done, me.done())
                    dve.wait_ge(dve_done, me.here())
                    dve.tensor_tensor(T_(20), T_(20), T_(21), ALU.subtract).then_inc(dve_done, me.done())
                    dve.wait_ge(dve_done, me.here())
                    dve.tensor_tensor(T_(20), T_(20), T_(18), ALU.mult).then_inc(dve_done, me.done())
                if part == 2:
                    dve.wait_ge(pe_used, end("xa_wk", 1))
                    dve.wait_ge(dve_done, me.here())
                    dve.tensor_copy(rad[:, :], T_(4)).then_inc(dve_done, me.done("ssm.rad"))
                    dve.wait_ge(loaded["c"], 32)
                    f_ = [wide(T_(19), 16), wide(T_(20), 16)]
                    dve.wait_ge(dve_done, me.here())
                    dve.tensor_tensor(c_eff[:, 0], c_in[:, 0], f_[0], ALU.mult).then_inc(dve_done, me.done())
                    dve.wait_ge(dve_done, me.here())
                    dve.tensor_tensor(c_tmp[:, 0], c_in[:, 1], f_[1], ALU.mult).then_inc(dve_done, me.done())
                    dve.wait_ge(dve_done, me.here())
                    dve.tensor_tensor(c_eff[:, 1], c_in[:, 0], f_[1], ALU.mult).then_inc(dve_done, me.done())
                    dve.wait_ge(dve_done, me.here())
                    dve.tensor_tensor(c_tmp[:, 1], c_in[:, 1], f_[0], ALU.mult).then_inc(dve_done, me.done())
                    dve.wait_ge(dve_done, me.here())
                    dve.tensor_tensor(c_eff[:, 0], c_eff[:, 0], c_tmp[:, 0], ALU.subtract).then_inc(dve_done, me.done())
                    dve.wait_ge(dve_done, me.here())
                    dve.tensor_tensor(c_eff[:, 1], c_eff[:, 1], c_tmp[:, 1], ALU.add).then_inc(dve_done, me.done())
                    dve.wait_ge(dve_done, me.here())
                    dve.tensor_scalar(c_eff[:, 1], c_eff[:, 1], -1.0, None, ALU.mult)\
                        .then_inc(dve_done, me.done("ssm.ceff"))
                if part >= 3:
                    tab, n = (pow_b, pow_a)[(part - 3) // 4], 2 ** ((part - 3) % 4)
                    odd, even = (T_(22), T_(23)), (T_(24), T_(25))
                    cur = (T_(10), T_(6)) if part == 3 else even if n in (1, 4) else odd
                    new_cur = even if n in (2, 8) else odd
                    if n == 1:
                        dve.memset(tab[:, 0, :, 0:1], 1.0).then_inc(dve_done, me.done())
                        dve.memset(tab[:, 1, :, 0:1], 0.0).then_inc(dve_done, me.done())
                    cw, sw = wide(cur[0], n), wide(cur[1], n)
                    x_ = scr[:, 0:32 * n].rearrange("p (g n) -> p g n", n=n)
                    dve.wait_ge(dve_done, me.here())
                    dve.tensor_tensor(tab[:, 0, :, n:2 * n], tab[:, 0, :, 0:n], cw, ALU.mult)\
                        .then_inc(dve_done, me.done())
                    dve.wait_ge(dve_done, me.here())
                    dve.tensor_tensor(x_, tab[:, 1, :, 0:n], sw, ALU.mult).then_inc(dve_done, me.done())
                    dve.wait_ge(dve_done, me.here())
                    dve.tensor_tensor(tab[:, 0, :, n:2 * n], tab[:, 0, :, n:2 * n], x_, ALU.subtract)\
                        .then_inc(dve_done, me.done())
                    dve.wait_ge(dve_done, me.here())
                    dve.tensor_tensor(tab[:, 1, :, n:2 * n], tab[:, 0, :, 0:n], sw, ALU.mult)\
                        .then_inc(dve_done, me.done())
                    dve.wait_ge(dve_done, me.here())
                    dve.tensor_tensor(x_, tab[:, 1, :, 0:n], cw, ALU.mult).then_inc(dve_done, me.done())
                    dve.wait_ge(dve_done, me.here())
                    dve.tensor_tensor(tab[:, 1, :, n:2 * n], tab[:, 1, :, n:2 * n], x_, ALU.add)\
                        .then_inc(dve_done, me.done("ssm.pow"))
                    dve.wait_ge(dve_done, me.here())
                    dve.tensor_tensor(T_(26), cur[0], cur[0], ALU.mult).then_inc(dve_done, me.done())
                    dve.wait_ge(dve_done, me.here())
                    dve.tensor_tensor(T_(27), cur[1], cur[1], ALU.mult).then_inc(dve_done, me.done())
                    dve.wait_ge(dve_done, me.here())
                    dve.tensor_tensor(T_(28), cur[0], cur[1], ALU.mult).then_inc(dve_done, me.done())
                    dve.wait_ge(dve_done, me.here())
                    dve.tensor_tensor(new_cur[0], T_(26), T_(27), ALU.subtract).then_inc(dve_done, me.done())
                    dve.wait_ge(dve_done, me.here())
                    dve.tensor_scalar(new_cur[1], T_(28), 2.0, None, ALU.mult).then_inc(dve_done, me.done())

            def ssm(i, part):
                k = i % 2
                pr = [prod[:, z] for z in range(4)]
                c_, s_ = rot[:, k, 0], rot[:, k, 1]
                so = [s_out[:, k, z] for z in range(2)]
                if i <= 15 and part == 0:
                    dve.wait_ge(pool_done, me.at(f"ssm{i}.rot"))
                    dve.wait_ge(dve_done, me.at("ssm.rad"))
                    bu = [bank_of(f"bu{i}", g)[:, :].rearrange("p (z t) -> p z t", z=2) for g in range(2)]
                    if i == 0:
                        dve.wait_ge(pe_done, me.at("uT.3.T"))
                        dve.wait_ge(dve_done, me.at("ssm.pow"))
                    dve.wait_ge(dve_done, me.here())
                    for g in range(2):
                        dve.wait_ge(pe_done, me.at(f"ssm{i}.bu{g}"))
                        dve.tensor_tensor(pr[0][:, g], bu[g][:, 0], c_[:, g], ALU.mult).then_inc(dve_done, me.done())
                        dve.tensor_tensor(pr[1][:, g], bu[g][:, 1], s_[:, g], ALU.mult).then_inc(dve_done, me.done())
                        dve.tensor_tensor(pr[2][:, g], bu[g][:, 1], c_[:, g], ALU.mult).then_inc(dve_done, me.done())
                        dve.tensor_tensor(pr[3][:, g], bu[g][:, 0], s_[:, g], ALU.mult)\
                            .then_inc(dve_done, me.done(f"ssm{i}.turned"))
                if i <= 15 and part == 1:
                    dve.wait_ge(dve_done, me.here())
                    dve.tensor_tensor(flat(pr[0]), flat(pr[0]), flat(pr[1]), ALU.add).then_inc(dve_done, me.done())
                    dve.tensor_tensor(flat(pr[2]), flat(pr[2]), flat(pr[3]), ALU.subtract)\
                        .then_inc(dve_done, me.done())
                    dve.wait_ge(dve_done, me.here())
                    for g in range(2):
                        r_ = rad[:, 2 * i + g:2 * i + g + 1].broadcast_to([P, T])
                        for z in (0, 2):
                            dve.tensor_tensor_scan(pr[z + 1][:, g], r_, pr[z][:, g], 0.0, ALU.mult, ALU.add)\
                                .then_inc(dve_done, me.done())
                if i <= 15 and part == 2:
                    dve.wait_ge(dve_done, me.here())
                    if i >= 2:
                        dve.wait_ge(pe_done, me.at(f"ssm{i - 1}.y"))
                    dve.tensor_tensor(flat(so[0]), flat(pr[1]), flat(c_), ALU.mult).then_inc(dve_done, me.done())
                    dve.tensor_tensor(flat(pr[0]), flat(pr[3]), flat(s_), ALU.mult).then_inc(dve_done, me.done())
                    dve.tensor_tensor(flat(so[1]), flat(pr[1]), flat(s_), ALU.mult).then_inc(dve_done, me.done())
                    dve.tensor_tensor(flat(pr[2]), flat(pr[3]), flat(c_), ALU.mult).then_inc(dve_done, me.done())
                if i <= 15 and part == 3:
                    dve.wait_ge(dve_done, me.here())
                    dve.tensor_tensor(flat(so[0]), flat(so[0]), flat(pr[0]), ALU.subtract)\
                        .then_inc(dve_done, me.done())
                    dve.tensor_tensor(flat(so[1]), flat(so[1]), flat(pr[2]), ALU.add)\
                        .then_inc(dve_done, me.done(f"ssm{i}.DVE", f"ssm{i}.s"))
                if part == 2 and i >= 2 and i % 2 == 0:
                    ct = (i - 2) // 2
                    dve.wait_ge(pe_done, me.at(f"ssm{i}.y"))
                    if ct:
                        dve.wait_ge(act_done, me.at(f"gelu{ct - 1}"))
                    dve.scalar_tensor_tensor(prod_y(ct), uT[:, ct, :], cols["d"][:, ct:ct + 1],
                        bank_of(f"ssy{ct}", 0)[:, 0:T], ALU.mult, ALU.add)\
                        .then_inc(dve_done, me.done(f"ssm{i}.ysum"))

            def sg_norm(part):
                rows = [av[:, t, :] for t in range(NT)]
                if part == 0:
                    dve.wait_ge(loaded["av"], 32)
                    for n in range(W // NW):
                        stats_in(rows, n)
                    inverse("sgn", NT, W // NW, 64, center=True)
                if part == 1:
                    dve.wait_ge(act_done, me.at("sgn.rinv"))
                    for t in range(NT):
                        dve.tensor_scalar(rows[t], rows[t], st_[:, 48 + 2 * t:49 + 2 * t], st_[:, 64 + t:65 + t],
                                          ALU.subtract, ALU.mult).then_inc(dve_done, me.done())
                    dve.wait_ge(dve_done, me.here())
                    dve.wait_ge(loaded["ln_gb"], 16)
                    dve.tensor_tensor(av[:, :, :], av[:, :, :], many(ln_gb[:, 0, :], NT), ALU.mult)\
                        .then_inc(dve_done, me.done())
                if part == 2:
                    dve.wait_ge(dve_done, me.here())
                    dve.tensor_tensor(av[:, :, :], av[:, :, :], many(ln_gb[:, 1, :], NT), ALU.add)\
                        .then_inc(dve_done, me.done("sg.vn"))

            def sg_mix(part):
                if part == 0:
                    dve.wait_ge(pe_done, me.at("sg_mix.PE"))
                    for j in range(4):
                        t, q = j // 2, j % 2
                        dve.tensor_tensor(four(av[:, t, q * NW:(q + 1) * NW]), four(bank_of("sgm", j)),
                                          wide(cols["sg_b"][:, 4 * q:4 * q + 4], P), ALU.add)\
                            .then_inc(dve_done, me.done("sg.biased"))
                if part == 1:
                    dve.wait_ge(dve_done, me.here())
                    dve.wait_ge(loaded["au"], 32)
                    dve.tensor_tensor(flat(av[:, :, :]), flat(av[:, :, :]), flat(au[:, :, :]), ALU.mult)\
                        .then_inc(dve_done, me.done())
                if part == 2:
                    dve.wait_ge(dve_done, me.here())
                    dve.wait_ge(loaded["ag"], 32)
                    dve.tensor_tensor(flat(av[:, :, :]), flat(av[:, :, :]), flat(ag[:, :, :]), ALU.mult)\
                        .then_inc(dve_done, me.done("sg.gated"))

            def gelu_turn():
                dve.wait_ge(act_done, me.at("gelu.hi"))
                dve.tensor_tensor(b_lo[1][:, :, :], uT[:, :, :], b_hi[1][:, :, :].bitcast(F32), ALU.subtract)\
                    .then_inc(dve_done, me.done("gelu.lo"))

            def xa_score(h):
                dve.wait_ge(pe_done, me.at(f"xa{h}.S"))
                dve.wait_ge(dve_done, me.here())
                if h:
                    dve.wait_ge(act_done, me.at(f"xa{h - 1}.exp"))
                dve.tensor_reduce(st_[:, 0:2], bank_of("xs", h).rearrange("p (t m) -> p t m", t=NT), AX.X, ALU.max)\
                    .then_inc(dve_done, me.done())
                dve.wait_ge(dve_done, me.here())
                dve.tensor_scalar(st_[:, 4:6], st_[:, 0:2], -1.0, None, ALU.mult)\
                    .then_inc(dve_done, me.done(f"xa{h}.max"))
                dve.wait_ge(act_done, me.at(f"xa{h}.exp"))
                dve.reciprocal(st_[:, 12:14], st_[:, 8:10]).then_inc(dve_done, me.done())
                dve.wait_ge(dve_done, me.here())
                dve.tensor_tensor(prob[:, :, :], prob[:, :, :], wide(st_[:, 12:14], T), ALU.mult)\
                    .then_inc(dve_done, me.done(f"xa{h}.prob"))

            def xa_gate():
                dve.wait_ge(act_done, me.at("xa3.out"))
                dve.wait_ge(loaded["xg"], 32)
                dve.tensor_tensor(xqT[:, :, :].rearrange("p (h t) c -> p h t c", t=NT), xqT[:, :, :].rearrange("p (h t) c -> p h t c", t=NT),
                    xg_rows[:, :, :].rearrange("p t (h c) -> p h t c", h=4), ALU.mult)\
                    .then_inc(dve_done, me.done("xo.rows"))

            def xo_in(j):
                dve.wait_ge(pe_used, end("w2_gate2", 3))
                job("xo", j)

            def glu_rest():
                dve.wait_ge(act_done, me.at("glu.sig"))
                for j in range(4):
                    t, q = j // 2, j % 2
                    dve.wait_ge(pe_done, me.at(f"gr.{j}.T"))
                    o = glu[:, t, q * NW:(q + 1) * NW]
                    dve.tensor_tensor(o, o, bank_of("gr", j), ALU.mult).then_inc(dve_done, me.done())

            def glu_gate():
                dve.wait_ge(dve_done, me.here())
                dve.wait_ge(loaded["bg"], 32)
                dve.tensor_tensor(flat(glu[:, :, :]), flat(glu[:, :, :]), flat(bg_rows[:, :, :]), ALU.mult)\
                    .then_inc(dve_done, me.done("glu.rows"))

            def tables():
                dve.wait_ge(loaded["rest"], 16)
                dve.tensor_tensor(pre_gain, cols["g_final"], cols["pre_g"], ALU.mult).then_inc(dve_done, me.done())
                dve.wait_ge(act_done, me.at("w_sc.hi"))
                dve.tensor_tensor(flat(w_sc_lo[:, :, :]), w_sc[:, :], flat(w_sc_hi[:, :, :]).bitcast(F32), ALU.subtract)\
                    .then_inc(dve_done, me.done("w_sc.lo"))

            steps = {"tables": tables, "scalars": scalars, "fourier": fourier, "conv_in": conv_in,
                     "conv_norm": conv_norm, "key_rows": key_rows, "decay": decay, "turn": turn, "solve_x": solve_x,
                     "scan_in": scan_in, "scan_out": scan_out, "heads_norm": heads_norm, "heads_in": heads_in,
                     "x_in": lambda n: rows_in("x", n), "y_in": lambda n: rows_in("y", n),
                     "mlp_in": lambda n: rows_in("mlp", n), "pre_in": lambda n: rows_in("pre", n),
                     "merge_in": lambda n: rows_in("merge", n), "mem_in": mem_in,
                     "x_root": lambda: inverse("x", NT, 4, RMS["x"]),
                     "mlp_root": lambda: inverse("mlp", NT, 4, RMS["mlp"]),
                     "mem_root": lambda t: inverse(f"mem{t}", 1, 4, RMS["mem"] + t, 96),
                     "final_root": final_root, "final_scale": final_scale, "pre_root": pre_root,
                     "hidden": lambda p, j: jobs(f"hidden{p}.{j}"),
                     "ssm_small": ssm_small, "ssm": ssm, "sg_norm": sg_norm, "sg_mix": sg_mix,
                     "sg_in": lambda j: job("sg", j), "gelu_turn": gelu_turn, "xa_score": xa_score,
                     "xa_gate": xa_gate, "xo_in": xo_in, "glu_rest": glu_rest, "glu_gate": glu_gate,
                     "glu_in": lambda j: job("glu", j)}
            dve.wait_ge(loaded["small"], 16)
            rows_in("x", 0)
            split(0)
            split(1)

            def slot_work(n):
                run_steps(me, steps, 2 * n)
                if n + SPLIT < UNITS:
                    split(n + SPLIT)
                if n in CHUNK_END:
                    empty(CHUNK_END[n])
                run_steps(me, steps, 2 * n + 1)

            def after_loop():
                ts_user[:] = [f"hidden{NPIECE - 2}.1.0"] * 2

            drive(me, slot_work, after_loop)
            inverse("out", NT, 4, RMS["out"])
            dve.wait_ge(act_done, me.at("out.rinv"))
            dve.wait_ge(dve_emptied, emptied(len(CHUNKS) - 1, "dve"))
            for t in range(NT):
                for h in range(2):
                    c = slice(h * W, (h + 1) * W)
                    dve.scalar_tensor_tensor(y_rows[:, t, c], y_rows[:, t, c], rms("out", t), x_rows[:, t, c],
                                             ALU.mult, ALU.add).then_inc(dve_done, me.done(f"out{t}{h}"))

        @block.tensor
        def _(pe):
            me = Side("pe", pe, done, old, new)
            last_use = [None] * 4
            turn_of_banks = [0]

            def take_bank(tag, j, reader):
                i = turn_of_banks[0] % 4
                turn_of_banks[0] += 1
                new["bank"][(tag, j)] = i
                if last_use[i] and me.it is None:
                    pe.wait_ge(done[me.engine_of(last_use[i])], me.at(last_use[i]))
                last_use[i] = reader
                return bank(i)

            def operand_ready(name, u):
                tag = {"w_f": "x", "w_o": "y", "w_mlp_up": "mlp", "w2_bx": "pre", "w_out": "merge"}.get(name)
                if tag and me.it is None:
                    pe.wait_ge(act_done, me.at(f"{tag}.{2 * u + 1}.hi"))
                    pe.wait_ge(dve_done, me.at(f"{tag}.{2 * u + 1}.lo"))
                if u:
                    return
                tag = {"w_fourier": "fourier8", "w_dn_up": "heads", "xa_wv": "mem1", "glu_w": "gelu",
                       "w_branch0": "sg", "w_branch2": "xo", "w_branch1": "glu"}.get(name)
                if name.startswith("w_mlp_down"):
                    tag = f"hidden{name[10:]}.1"
                if tag:
                    pe.wait_ge(act_done, me.at(f"{tag}.hi"))
                    pe.wait_ge(dve_done, me.at(f"{tag}.lo"))

            def unit(n, part):
                i = CHUNK_AT[n]
                name, col, units, _ = CHUNKS[i]
                u = n - FIRST[i]
                if col == 0 and part == 0:
                    operand_ready(name, u)
                if u == 0 and part == 0:
                    if me.it is not None and n < LOOP0 + 8:
                        pe.wait_ge(dve_emptied,
                                   value(me, emptied(i - 2, "dve") - (NT if n == LOOP0 else 0), 8 * NT))
                    if i >= 2:
                        by = CHUNKS[i - 2][3]
                        pe.wait_ge(act_emptied if by == "act" else dve_emptied,
                                   value(me, emptied(i - 2, by), NT * (4 if by == "act" else 8)))
                if part == 0:
                    pe.wait_ge(lo_split, value(me, n + 1, LOOP_UNITS))
                op = operand(name)
                for k in range(part * KU // 2, (part + 1) * KU // 2):
                    hi, lo = op(KU * u + k)
                    wh = w_hi[:, n % SPLIT, k * NW:(k + 1) * NW]
                    wl = w_lo[:, n % SPLIT, k * NW:(k + 1) * NW]
                    for t in range(NT):
                        tk = slice(t * P, (t + 1) * P)
                        o = acc[:, i % 2, t, :]
                        first, last = u == 0 and k == 0, u == units - 1 and k == KU - 1
                        pe.matmul(o, hi[:, tk], wh, start=first, stop=False)
                        pe.matmul(o, hi[:, tk], wl, start=False, stop=False)
                        ins = pe.matmul(o, lo[:, tk], wh, start=False, stop=last)
                if part == 1:
                    ins.then_inc(pe_used, 1)

            def job(tag, j):
                src, _, mode, _ = JOBS[tag][j]
                b = take_bank(tag, j, f"{tag}.{j}." + ("lo" if mode == "plain" else "tmp"))
                for q in range(4):
                    ins = pe.transpose(b[:, q * P:(q + 1) * P], src(q), ident)
                ins.then_inc(pe_done, me.done(f"{tag}.{j}.T", f"{tag}.T"))

            def jobs(tag):
                for j in range(len(JOBS[tag])):
                    job(tag, j)

            def x_in(n):
                pe.wait_ge(loaded[f"x_{n}"], 16)
                job("x", 2 * n)
                job("x", 2 * n + 1)

            def y_in(n):
                pe.wait_ge(dve_done, me.at(f"w_dn_up{n}.y"))
                job("y", 2 * n)
                job("y", 2 * n + 1)

            def mlp_in(n):
                pe.wait_ge(dve_emptied, emptied(INDEX[("w_o", n)], "dve"))
                job("mlp", 2 * n)
                job("mlp", 2 * n + 1)

            def pre_in(n):
                pe.wait_ge(dve_emptied, emptied(INDEX[(f"w_mlp_down{NPIECE - 1}", n)], "dve"))
                job("pre", 2 * n)
                job("pre", 2 * n + 1)

            def merge_in(n):
                pe.wait_ge(dve_done, me.at(f"w_branch1{n}.y"))
                job("merge", 2 * n)
                job("merge", 2 * n + 1)

            def mem_in(t, n):
                pe.wait_ge(loaded["mem"], 16 * (t + 1))
                job(f"mem{t}", n)

            def heads_in(j):
                pe.wait_ge(dve_done, me.at("heads.rows"))
                job("heads", j)

            def sg_in(j):
                pe.wait_ge(dve_done, me.at("sg.gated"))
                job("sg", j)

            def xo_in(j):
                pe.wait_ge(dve_done, me.at("xo.rows"))
                job("xo", j)

            def glu_in(j):
                pe.wait_ge(dve_done, me.at("glu.rows"))
                job("glu", j)

            def scalars(part):
                if part == 0:
                    pe.wait_ge(loaded["rest"], 16)
                    pe.wait_ge(act_done, me.at("w_sc.hi"))
                    pe.wait_ge(dve_done, me.at("w_sc.lo"))
                    b = take_bank("scT", 0, "scT")
                    for k in range(KD):
                        pe.matmul(b[0:32, 0:T], w_sc_hi[:, k, :], a_hi[:, k, :], start=k == 0, stop=False)
                        pe.matmul(b[0:32, 0:T], w_sc_lo[:, k, :], a_hi[:, k, :], start=False, stop=False)
                        ins = pe.matmul(b[0:32, 0:T], w_sc_hi[:, k, :], a_lo[:, k, :], start=False, stop=k == KD - 1)
                    ins.then_inc(pe_done, me.done("scT.proj"))
                if part == 1:
                    pe.wait_ge(act_done, me.at("scT"))
                    b = take_bank("sc", 0, "sc.xa")
                    for t in range(NT):
                        ins = pe.transpose(b[:, 32 * t:32 * t + 32], scT[0:32, t * P:(t + 1) * P], ident[0:32, 0:32])
                    ins.then_inc(pe_done, me.done("sc.proj"))

            def decays():
                pe.wait_ge(dve_done, me.at("decays.g"))
                b = take_bank("dec", 0, "e_sc")
                for t in range(NT):
                    g = g_log[:, 16 * t:16 * t + 16]
                    for d, (upto, rest) in enumerate((("LE", "GT"), ("GE", "LT"))):
                        gd = g[:, 8 * d:8 * d + 8]
                        for o0, m in ((0, upto), (32, rest)):
                            pe.matmul(b[:, o0 + 16 * t + 8 * d:o0 + 16 * t + 8 * d + 8], cols[m], gd, start=True, stop=True)
                    for c in range(2):
                        o0 = 64 + (2 * t + c) * 16
                        ins = pe.matmul(b[:, o0:o0 + 16], cols["chunk"][:, c * P:(c + 1) * P], g, start=True, stop=True)
                ins.then_inc(pe_done, me.done("sc.sums"))

            def fourier(g):
                if g == 0:
                    pe.wait_ge(act_emptied, emptied(INDEX[("w_f", 1)], "act"))
                    pe.wait_ge(loaded["dft"], 16)
                if g >= 1:
                    pe.wait_ge(act_done, me.at(f"fourier{g - 1}.P"))
                    b = take_bank("f_out", g, f"fourier{g}.lo")
                    x = fp[:, (g - 1) % 2, :]
                    pe.matmul(b[:, 0:T], dft[:, 1024:1152], x[:, 0:T], start=True, stop=False)
                    pe.matmul(b[:, 0:T], dft[:, 1152:1280], x[:, T:2 * T], start=False, stop=True)\
                        .then_inc(pe_done, me.done(f"fourier{g}.out"))
                if g < 8:
                    b = take_bank("f_time", g, f"fourier{g}.P")
                    for t in range(NT):
                        ins = pe.matmul(b, f_rows[:, t, g * P:(g + 1) * P], dft[:, t * NW:(t + 1) * NW],
                                        start=t == 0, stop=t == 1)
                    ins.then_inc(pe_done, me.done(f"fourier{g}.time"))

            def conv_in(half, x, part):
                if part:
                    return
                pe.wait_ge(act_emptied, emptied(INDEX[(("w_q", "w_k", "w_v")[x], half)], "act"))
                for b_ in range(2):
                    b = take_bank(f"conv{half}{x}", b_, f"conv{half}{x}.pad{b_}")
                    for h in range(2):
                        for t in range(NT):
                            hd = 2 * b_ + h
                            ins = pe.transpose(b[:, h * T + t * P:h * T + (t + 1) * P], qkv[:, x, t, hd * P:(hd + 1) * P], ident)
                    ins.then_inc(pe_done, me.done(f"conv{half}{x}.T{b_}"))

            def conv_norm(half, x):
                pe.wait_ge(act_done, me.at(f"conv{half}{x}.sq"))
                for b_ in range(2):
                    b = take_bank(f"norm{half}{x}", b_, f"conv{half}{x}.inv")
                    pe.matmul(b, ones, flat(squares[:, 2 * b_:2 * b_ + 2, :]), start=True, stop=True)\
                        .then_inc(pe_done, me.done(f"norm{half}{x}.S{b_}"))

            def conv_back(half, x):
                pe.wait_ge(act_done, me.at(f"conv{half}{x}.silu"))
                for t in range(NT):
                    b = take_bank(f"v{half}", t, f"v{half}.rows{t}")
                    for hd in range(4):
                        ins = pe.transpose(b[:, hd * P:(hd + 1) * P], convT[:, hd, t * P:(t + 1) * P], ident)
                    ins.then_inc(pe_done, me.done(f"v{half}.T{t}"))

            def key_rows(half):
                pe.wait_ge(dve_done, me.at(f"kT{half}"))
                for t in range(NT):
                    b = take_bank(f"key{half}", t, f"key{half}.{t}.1")
                    for hd in range(4):
                        ins = pe.transpose(b[:, hd * P:(hd + 1) * P], kT[:, hd, t * P:(t + 1) * P], ident)
                    ins.then_inc(pe_done, me.done(f"key{half}.T{t}"))

            def gram(half, t):
                pe.wait_ge(dve_done, me.at(f"qT{half}", f"kT{half}"))
                for z, x in (("G", kT), ("Q", qT)):
                    b = take_bank(f"gram{z}{half}{t}", 0, f"decay{half}{t}.{'M' if z == 'G' else 'Q'}0")
                    for hd in range(4):
                        tk = slice(t * P, (t + 1) * P)
                        ins = pe.matmul(b[:, hd * P:(hd + 1) * P], x[:, hd, tk], kT[:, hd, tk], start=True, stop=True)
                    ins.then_inc(pe_done, me.done(f"gram{half}{t}.{z}"))

            def decay(half, t):
                for d in range(2):
                    pe.wait_ge(pool_done, me.at(f"gram{half}{t}.R{d}"))
                    b = take_bank(f"decay{half}{t}", d, f"decay{half}{t}.E{d}")
                    for hd in range(4):
                        ins = pe.matmul(b[:, hd * P:(hd + 1) * P], RG(d)[:, hd * P:(hd + 1) * P], cols["GT" if d == 0 else "LT"],
                                        start=True, stop=True)
                    ins.then_inc(pe_done, me.done(f"decay{half}{t}.D{d}"))

            def turn(half, t):
                for z, x, to in (("M", MM, "MT"), ("Q", QK, "QT")):
                    for d in range(2):
                        pe.wait_ge(dve_done, me.at(f"decay{half}{t}.{z}{d}"))
                        b = take_bank(f"turn{z}{half}{t}", d, f"turn{half}{t}.{to}{d}")
                        for hd in range(4):
                            ins = pe.transpose(b[:, hd * P:(hd + 1) * P], x(d)[:, hd * P:(hd + 1) * P], ident)
                        ins.then_inc(pe_done, me.done(f"turn{half}{t}.{z}{d}"))

            def four_products(b, lhs, rhs, name):
                for hd in range(4):
                    hs = slice(hd * P, (hd + 1) * P)
                    ins = pe.matmul(b[:, hs], lhs[:, hs], rhs[:, hs], start=True, stop=True)
                ins.then_inc(pe_done, me.done(name))

            def solve_y(half, t, n):
                for d in range(2):
                    before = f"turn{half}{t}.X{d}" if n == 1 else f"solve{half}{t}{n - 1}.X{d}"
                    pe.wait_ge(dve_done, me.at(before))
                    pe.wait_ge(pool_done, me.at(f"solve{half}{t}{n}.Mt{d}"))
                    b = take_bank(f"solveY{half}{t}{n}", d, f"solve{half}{t}{n}.Yc{d}")
                    four_products(b, RG(d), EB(d), f"solve{half}{t}{n}.Y{d}")

            def solve_x(half, t, n):
                for d in range(2):
                    pe.wait_ge(act_done, me.at(f"solve{half}{t}{n}.Yc{d}"))
                    pe.wait_ge(dve_done, me.at(f"turn{half}{t}.XT{d}" if n == 1 else f"solve{half}{t}{n - 1}.XT{d}"))
                    b = take_bank(f"solveT{half}{t}{n}", d, f"solve{half}{t}{n}.XT{d}")
                    four_products(b, MM(d), EM(d), f"solve{half}{t}{n}.ZT{d}")
                    if n < len(LEVELS) - 1:
                        b = take_bank(f"solveZ{half}{t}{n}", d, f"solve{half}{t}{n}.X{d}")
                        four_products(b, EM(d), MM(d), f"solve{half}{t}{n}.Z{d}")

            def rows_products(b, rs, lhs, rhs, name):
                for hd in range(4):
                    ins = pe.matmul(b[rs, hd * P:(hd + 1) * P], lhs(hd), rhs(hd), start=True, stop=True)
                ins.then_inc(pe_done, me.done(*([name] if isinstance(name, str) else name)))

            def scan_in(half, st):
                if st == 0:
                    return
                for d in range(2):
                    c, t, rs = chunk_of(st, d)
                    tk = slice(64 * c, 64 * c + 64)
                    pe.wait_ge(dve_done, me.at(f"scan{half}.{st - 1}.S{d}"))
                    b = take_bank(f"scanP{half}{st}", d, f"scan{half}.{st}.r{d}")
                    rows_products(b, rs, lambda hd: kT[:, hd, tk], lambda hd: state[:, d, hd, :], f"scan{half}.{st}.P{d}")
                    b = take_bank(f"scanO{half}{st}", d, f"scan{half}.{st}.r{d}")
                    rows_products(b, rs, lambda hd: qT[:, hd, tk], lambda hd: state[:, d, hd, :],
                                  [f"scan{half}.{st}.O{d}", f"scan{half}.{st}.in.PE"])

            def scan_new(half, st):
                for d in range(2):
                    c, t, rs = chunk_of(st, d)
                    pe.wait_ge(pool_done, me.at(f"solT{half}{t}.{d}"))
                    pe.wait_ge(act_done, me.at(f"v{half}.rows{t}"))
                    if st:
                        pe.wait_ge(dve_done, me.at(f"scan{half}.{st}.r{d}"))
                    r0 = 64 * (c % 2)
                    b = take_bank(f"scanN{half}{st}", d, f"scan{half}.{st}.vnew{d}")
                    rhs = (lambda hd: RG(d)[rs, hd * P:(hd + 1) * P]) if st else (lambda hd: v_rows[rs, t, hd, :])
                    rows_products(b, rs, lambda hd: solT[rs, t, d, hd, r0:r0 + 64], rhs, f"scan{half}.{st}.new{d}")

            def scan_out(half, st):
                for d in range(2):
                    c, t, rs = chunk_of(st, d)
                    r0 = 64 * (c % 2)
                    pe.wait_ge(act_done, me.at(f"scan{half}.{st}.vnew{d}", f"turn{half}{t}.QT{d}"))
                    pe.wait_ge(dve_done, me.at(f"key{half}.{t}.{d}"))
                    b = take_bank(f"scanQ{half}{st}", d, f"scan{half}.{st}.out.DVE")
                    v = lambda hd: EB(d)[rs, hd * P:(hd + 1) * P]
                    rows_products(b, rs, lambda hd: qkT[rs, t, d, hd, r0:r0 + 64], v, f"scan{half}.{st}.o2{d}")
                    if st < 3:
                        b = take_bank(f"scanS{half}{st}", d, f"scan{half}.{st}.S{d}")
                        rows_products(b, slice(0, P), lambda hd: k_dec[rs, d, t, hd, :], v, f"scan{half}.{st}.dS{d}")
                new[f"scan{half}.{st}.out.PE"] = ("pe", me.count)
                new[f"scan{half}.{st}.new.PE"] = ("pe", me.count)

            def turned(tag, src, readers="t"):
                for j in range(4):
                    t, q = j // 2, j % 2
                    b = take_bank(tag, j, f"{tag}.{j}.{readers}")
                    for r in range(4):
                        ins = pe.transpose(b[:, r * P:(r + 1) * P], src(t, 4 * q + r), ident)
                    ins.then_inc(pe_done, me.done(f"{tag}.{j}.T", f"{tag}.T"))

            def ssm_u():
                pe.wait_ge(loaded["u"], 32)
                for j in range(4):
                    t, q = j // 2, j % 2
                    b = take_bank("uT", j, f"uT.{j}")
                    for r in range(4):
                        k = 4 * q + r
                        ins = pe.transpose(b[:, r * P:(r + 1) * P], u_rows[:, t, k * P:(k + 1) * P], ident)
                    ins.then_inc(pe_done, me.done(f"uT.{j}.T"))

            def ssm(i, part):
                if i <= 15 and part == 0:
                    ct = i // 2
                    pe.wait_ge(loaded[f"b_pad{ct % 2}"], 16 * (ct // 2 + 1))
                    pe.wait_ge(act_done, me.at("uT.3"))
                    if ct >= 2:
                        pe.wait_ge(act_done, me.at(f"gelu{ct - 2}"))
                    for g in range(2):
                        b = take_bank(f"bu{i}", g, f"ssm{i}.turned")
                        for z in range(2):
                            ins = pe.matmul(b[:, z * T:(z + 1) * T], b_pad[:, ct % 2, 2 * (i % 2) + g, z, :], uT[:, ct, :],
                                            start=True, stop=True)
                        ins.then_inc(pe_done, me.done(f"ssm{i}.bu{g}", f"ssm{i}.bu"))
                if i >= 1 and part == 1:
                    j = i - 1
                    ct = j // 2
                    pe.wait_ge(dve_done, me.at(f"ssm{j}.s"))
                    pe.wait_ge(pool_done, me.at(f"cpad{ct}"))
                    b = bank_of(f"ssy{ct}", 0)
                    if j % 2 == 0:
                        b = take_bank(f"ssy{ct}", 0, f"ssm{2 * ct + 2}.ysum")
                    for g in range(2):
                        a_ = 2 * (j % 2) + g
                        for z in range(2):
                            ins = pe.matmul(b[:, 0:T], c_pad[:, ct % 2, z, a_ * P:(a_ + 1) * P], s_out[:, j % 2, z, g, :],
                                            start=j % 2 == 0 and g == 0 and z == 0, stop=j % 2 == 1 and g == 1 and z == 1)
                    ins.then_inc(pe_done, me.done(f"ssm{i}.y"))

            def sg_mix(part):
                if part:
                    return
                pe.wait_ge(dve_done, me.at("sg.vn"))
                pe.wait_ge(pool_done, me.at("w_sg.masked"))
                for j in range(4):
                    t, q = j // 2, j % 2
                    b = take_bank("sgm", j, "sg.biased")
                    for r in range(4):
                        g = 4 * q + r
                        ins = pe.matmul(b[:, r * P:(r + 1) * P], w_sg[:, g, :], av[:, t, g * P:(g + 1) * P], start=True, stop=True)
                    ins.then_inc(pe_done, me.done(f"sg_mix.{j}", "sg_mix.PE"))

            def xa_score(h):
                pe.wait_ge(act_done, me.at("km.3.t", "xq.3.t"))
                b = take_bank("xs", h, f"xa{h}.exp")
                for t in range(NT):
                    for k in range(2):
                        ins = pe.matmul(b[:, t * T:(t + 1) * T], xqT[:, 2 * h + k, t * P:(t + 1) * P], kmT[:, 2 * h + k, :],
                                        start=k == 0, stop=k == 1)
                ins.then_inc(pe_done, me.done(f"xa{h}.S", f"xa{h}.score"))

            def xa_prob(h):
                pe.wait_ge(dve_done, me.at(f"xa{h}.prob"))
                b = take_bank("xp", h, f"xa{h}.pT")
                for m in range(NT):
                    for t in range(NT):
                        ins = pe.transpose(b[:, m * T + t * P:m * T + (t + 1) * P], prob[:, t, m * P:(m + 1) * P], ident)
                ins.then_inc(pe_done, me.done(f"xa{h}.PT"))

            def xa_out(h):
                pe.wait_ge(act_done, me.at(f"xa{h}.pT"))
                pe.wait_ge(loaded["vm"], 32)
                b = take_bank("xo_", h, f"xa{h}.out")
                for t in range(NT):
                    for m in range(NT):
                        ins = pe.matmul(b[:, t * T:(t + 1) * T], probT[:, m, t * P:(t + 1) * P], vm[:, m, h * T:(h + 1) * T],
                                        start=m == 0, stop=m == 1)
                ins.then_inc(pe_done, me.done(f"xa{h}.O"))

            def glu_rest():
                for j in range(4):
                    t, q = j // 2, j % 2
                    b = take_bank("gr", j, "glu.rows")
                    for r in range(4):
                        ins = pe.transpose(b[:, r * P:(r + 1) * P], uT[:, 4 * q + r, t * P:(t + 1) * P], ident)
                    ins.then_inc(pe_done, me.done(f"gr.{j}.T", "gelu_rows.T"))

            def xa_k():
                pe.wait_ge(loaded["km"], 32)
                turned("km", lambda t, k: km_rows[:, t, k * P:(k + 1) * P])

            def xa_q():
                pe.wait_ge(loaded["xq"], 32)
                turned("xq", lambda t, k: xq_rows[:, t, k * P:(k + 1) * P])

            def hidden_jobs(p, j):
                pe.wait_ge(act_emptied, value(me, emptied(INDEX[("w_mlp_up", 2 * p + j)], "act"), 4 * NT))
                jobs(f"hidden{p}.{j}")

            steps = {"scalars": scalars, "decays": decays, "fourier": fourier, "conv_in": conv_in, "conv_norm": conv_norm,
                     "conv_back": conv_back, "key_rows": key_rows, "gram": gram, "decay": decay, "turn": turn,
                     "solve_y": solve_y, "solve_x": solve_x, "scan_in": scan_in, "scan_new": scan_new,
                     "scan_out": scan_out,
                     "heads_in": heads_in, "x_in": x_in, "y_in": y_in, "mlp_in": mlp_in, "pre_in": pre_in,
                     "mem_in": mem_in, "hidden": hidden_jobs, "ssm_u": ssm_u, "ssm": ssm, "sg_mix": sg_mix,
                     "sg_in": sg_in, "xa_k": xa_k, "xa_q": xa_q, "xa_score": xa_score, "xa_prob": xa_prob,
                     "xa_out": xa_out, "xo_in": xo_in, "glu_rest": glu_rest, "glu_in": glu_in,
                     "merge_in": merge_in}
            pe.wait_ge(loaded["small"], 16)
            x_in(0)

            def slot_work(n):
                unit(n, 0)
                run_steps(me, steps, 2 * n)
                unit(n, 1)
                run_steps(me, steps, 2 * n + 1)

            def after_loop():
                last_use[:] = [f"hidden{NPIECE - 2}.1.0.hi"] * 4

            drive(me, slot_work, after_loop)


def prev(half, t):
    k = 2 * half + t - 1
    return f"{k // 2}{k % 2}"


def chunk_of(st, d):
    c = st if d == 0 else 3 - st
    return c, c // 2, slice(64 * (c % 2), 64 * (c % 2) + 64)


def stream(a):
    k, n = a.shape
    return a.reshape(k // (KU * P), KU, P, n // NW, NW).transpose(3, 0, 2, 1, 4).reshape(-1, P, UE)


def laid_out(i):
    m = {}
    w_in, w2 = i["w_in"][0], i["w_in_2"][0]
    for k, name in enumerate(("w_q", "w_k", "w_v", "w_z", "w_f")):
        m[name] = w_in[:, k * W:(k + 1) * W]
    m["w_gate_a"], m["w_gate_f"] = w_in[:, 5152:5152 + D], w_in[:, 5152 + D:5152 + 2 * D]
    m["w_dn_up"], m["w_fourier"], m["w_o"] = i["w_dn_up"][0], i["w_fourier"][0], i["w_o"][0]
    m["w_mlp_up"] = i["w_mlp_up"][0]
    for p in range(NPIECE):
        m[f"w_mlp_down{p}"] = i["w_mlp_down"][0][p * W:(p + 1) * W]
    for k, name in enumerate(("w2_au", "w2_av", "w2_ag", "w2_bx", "w2_bg", "w2_xq", "w2_xg")):
        m[name] = w2[:, k * W:(k + 1) * W]
    for k in range(3):
        m[f"w2_gate{k}"] = w2[:, 7 * W + k * D:7 * W + (k + 1) * D]
        m[f"w_branch{k}"] = i["w_branch_2"][0][k]
    m["xa_wk"], m["xa_wv"], m["glu_w"], m["w_out"] = \
        i["xa_wk_2"][0], i["xa_wv_2"][0], i["glu_w_2"][0], i["w_out_2"][0]
    units = {k: stream(v) for k, v in m.items()}
    w = np.concatenate([units[name][n * u:(n + 1) * u] for name, n, u, _ in CHUNKS])
    per_k = lambda a: a.reshape(-1, P).T
    every = lambda a: np.broadcast_to(a.reshape(1, -1), (P, a.size))
    masks, dft = mask_constants()
    state = lambda a: a[0].reshape(32, P).T
    small = {
        "g_mix": per_k(i["g_mix"][0]), "g_mlp": per_k(i["g_mlp"][0]),
        "pre_g": per_k(i["pre_norm_g_2"][0]),
        "mem_g": per_k(i["mem_norm_g_2"][0]), "g_final": per_k(i["g_final"]), "g_head": i["g_dn_head"][0].reshape(P, 1),
        "conv_w": i["conv_w"][0].reshape(5, 24, P).transpose(2, 1, 0).reshape(P, 120),
        "a_log": every(np.concatenate([i["a_log_fwd"][0], i["a_log_bwd"][0]])),
        "dt_bias": every(np.concatenate([i["dt_bias_fwd"][0], i["dt_bias_bwd"][0]])),
        "a_re": state(i["ssm_a_re_2"]), "a_im": state(i["ssm_a_im_2"]),
        "log_dt": np.repeat(i["ssm_log_dt_2"][0].reshape(32, 2, 1), 64, axis=2).reshape(32, P).T,
        "d": per_k(i["ssm_d_2"][0].reshape(-1)), "sg_b": i["sg_b_2"][0].T}
    small.update(masks)
    b_pad = np.zeros((KW, P, 4, 2, P), np.float32)
    for z, name in enumerate(("ssm_b_re_2", "ssm_b_im_2")):
        b = i[name][0]
        for g in range(64):
            r, u = 16 * (g % 8), 64 * (g % 2)
            b_pad[g // 8, r:r + 16, g % 8 // 2, z, u:u + 64] = b[g].T
    c_rows = lambda a: a[0].transpose(0, 2, 1).reshape(32, P, 16).transpose(1, 0, 2)
    arrays = {
        "x": i["x"][0].reshape(NT, P, D), "mem": i["mem_2"][0].reshape(NT, P, D), "w": w,
        "w_sc": w_in[:, 5120:5152].reshape(KD, P, 32).transpose(1, 0, 2).reshape(P, KD * 32),
        "small": np.concatenate([small[n] for n, _ in SMALL if n[:5] != "level"], 1),
        "level": np.concatenate([small["level_f"], small["level_b"]], 1), "dft": dft,
        "b_pad": b_pad, "c_re": c_rows(i["ssm_c_re_2"]), "c_im": c_rows(i["ssm_c_im_2"]),
        "w_sg": i["sg_w_2"][0].transpose(2, 0, 1),
        "ln_gb": np.stack([every(i["sg_ln_g_2"][0]), every(i["sg_ln_b_2"][0])], 1),
        "glu_b": every(i["glu_b_2"][0]), "g_final": every(i["g_final"]), "post_g": every(i["post_norm_g_2"][0])}
    return {k: np.ascontiguousarray(v) for k, v in arrays.items()}


def program(nc, shapes, marks):
    t_in = {k: nc.dram_tensor(f"in_{k}", shape, F32, kind="ExternalInput").ap() for k, shape in shapes.items()}
    out = nc.dram_tensor("out_0", (1, T, D), F32, kind="ExternalOutput").ap()
    new = {"bank": {}}
    build(nc, t_in, out, marks, new)
    return new


def kernel(**inputs):
    import concourse.bacc as bacc
    from concourse.bass_utils import run_bass_kernel_spmd

    arrays = laid_out({k: np.asarray(v) for k, v in inputs.items()})
    marks = None
    for _ in range(2):
        nc = bacc.Bacc("TRN2", target_bir_lowering=False, num_devices=1)
        marks = program(nc, {k: a.shape for k, a in arrays.items()}, marks)
    r = run_bass_kernel_spmd(nc, [{f"in_{k}": a for k, a in arrays.items()}], core_ids=[0])
    return r.results[0]["out_0"]
```
